# Optimizing a Trainium2 kernel written in Bass

```python
import jax, jax.numpy as jnp
from jax import lax
import numpy as np
import math

D_MODEL = 2048
BATCH = 1
SEQ = 256
DEPTH = 2

N_MIXERS = 2
N_ATTN_LAYERS = (DEPTH + N_MIXERS - 1) // N_MIXERS
N_RNN_LAYERS = DEPTH // N_MIXERS

GRID_W = 64
ROPE_THETA = 10000.0

HEAD_DIM = 128
N_Q_HEADS = D_MODEL // HEAD_DIM
N_KV_HEADS = 4
GQA_GROUP = N_Q_HEADS // N_KV_HEADS
Q_BLOCK = 128
ROPE_AXIS_DIM = HEAD_DIM // 2
ROPE_FREQS = ROPE_AXIS_DIM // 2
QKV_DIM = (N_Q_HEADS + 2 * N_KV_HEADS) * HEAD_DIM

D_RNN = D_MODEL
RNN_BLOCK_W = 256
RNN_BLOCKS = D_RNN // RNN_BLOCK_W
CONV_W = 4
CONV_LEFT = 2
CONV_RIGHT = CONV_W - 1 - CONV_LEFT
LRU_C = 8.0

D_FF = -(-8 * D_MODEL // (3 * 256)) * 256

EPS = 1e-6


def rms_norm(x, g):
    xf = x.astype(jnp.float32)
    y = xf * lax.rsqrt(jnp.mean(xf * xf, axis=-1, keepdims=True) + EPS)
    return (y * g.astype(jnp.float32)).astype(x.dtype)

def axial_rope_tables(seq_len):
    rows_n = seq_len // GRID_W
    freqs = ROPE_THETA ** (-jnp.arange(ROPE_FREQS, dtype=jnp.float32) / ROPE_FREQS)
    row_ang = jnp.arange(rows_n, dtype=jnp.float32)[:, None, None] * freqs
    col_ang = jnp.arange(GRID_W, dtype=jnp.float32)[None, :, None] * freqs
    shape = (rows_n, GRID_W, ROPE_FREQS)
    ang = jnp.stack([jnp.broadcast_to(row_ang, shape), jnp.broadcast_to(col_ang, shape)], axis=-2)
    ang = ang.reshape(seq_len, 2, ROPE_FREQS)
    return jnp.cos(ang), jnp.sin(ang)

def apply_axial_rope(x, cos, sin):
    xr = x.astype(jnp.float32).reshape(*x.shape[:-1], 2, 2, ROPE_FREQS)
    x1, x2 = xr[..., 0, :], xr[..., 1, :]
    c = cos[None, :, None]
    s = sin[None, :, None]
    out = jnp.stack([x1 * c - x2 * s, x2 * c + x1 * s], axis=-2)
    return out.reshape(x.shape).astype(x.dtype)

def attention_mixer(h, w_qkv, q_gain, k_gain, w_o, cos, sin):
    b, s, _ = h.shape
    qkv = h @ w_qkv
    q, k, v = jnp.split(qkv, [N_Q_HEADS * HEAD_DIM, (N_Q_HEADS + N_KV_HEADS) * HEAD_DIM], axis=-1)
    q = q.reshape(b, s, N_Q_HEADS, HEAD_DIM)
    k = k.reshape(b, s, N_KV_HEADS, HEAD_DIM)
    v = v.reshape(b, s, N_KV_HEADS, HEAD_DIM)
    q = apply_axial_rope(rms_norm(q, q_gain), cos, sin) * (HEAD_DIM ** -0.5)
    k = apply_axial_rope(rms_norm(k, k_gain), cos, sin)
    n_blocks = s // Q_BLOCK
    qb = q.reshape(b, n_blocks, Q_BLOCK, N_KV_HEADS, GQA_GROUP, HEAD_DIM).transpose(1, 0, 2, 3, 4, 5)

    def one_block(q_blk):
        sc = jnp.einsum('bqkgd,bskd->bkgqs', q_blk, k).astype(jnp.float32)
        p = jax.nn.softmax(sc, axis=-1).astype(v.dtype)
        return jnp.einsum('bkgqs,bskd->bqkgd', p, v)

    o = lax.map(one_block, qb)
    o = o.transpose(1, 0, 2, 3, 4, 5).reshape(b, s, N_Q_HEADS * HEAD_DIM)
    return o @ w_o

def depthwise_conv_centred(x, w, bias):
    y = lax.conv_general_dilated(
        x, w[:, None, :], window_strides=(1,), padding=[(CONV_LEFT, CONV_RIGHT)],
        dimension_numbers=('NWC', 'WIO', 'NWC'), feature_group_count=x.shape[-1])
    return y + bias

def block_diag_linear(x, w, bias):
    b, s, _ = x.shape
    xb = x.reshape(b, s, RNN_BLOCKS, RNN_BLOCK_W)
    return jnp.einsum('bsni,nij->bsnj', xb, w).reshape(b, s, D_RNN) + bias

def rg_lru(x, w_a, b_a, w_i, b_i, lam, reverse):
    xf = x.astype(jnp.float32)
    r = jax.nn.sigmoid(block_diag_linear(xf, w_a, b_a).astype(jnp.float32))
    i = jax.nn.sigmoid(block_diag_linear(xf, w_i, b_i).astype(jnp.float32))
    log_a = -LRU_C * r * jax.nn.softplus(-lam.astype(jnp.float32))
    a = jnp.exp(log_a)
    u = jnp.sqrt(-jnp.expm1(2.0 * log_a)) * (i * xf)

    def combine(e1, e2):
        a1, b1 = e1
        a2, b2 = e2
        return a1 * a2, a2 * b1 + b2

    _, hs = lax.associative_scan(combine, (a, u), axis=1, reverse=reverse)
    return hs

def recurrent_mixer(h, w_in, conv_w, conv_b, w_a, b_a, w_i, b_i, lam, w_out):
    xy = h @ w_in
    xb, yb = jnp.split(xy, 2, axis=-1)
    yb = jax.nn.gelu(yb, approximate=True)
    xb = depthwise_conv_centred(xb, conv_w, conv_b)
    h_fwd = rg_lru(xb, w_a[0], b_a[0], w_i[0], b_i[0], lam[0], reverse=False)
    h_bwd = rg_lru(xb, w_a[1], b_a[1], w_i[1], b_i[1], lam[1], reverse=True)
    out = (h_fwd + h_bwd).astype(h.dtype) * yb
    return out @ w_out

def swiglu(h, w_gate, w_up, w_down):
    return (jax.nn.silu(h @ w_gate) * (h @ w_up)) @ w_down

def first_inputs(seed: int = 0) -> dict:
    key = jax.random.key(seed)
    ks = jax.random.split(key, 24)
    f32 = jnp.float32

    def nrm(k, shape, fan_in):
        return jax.random.normal(k, shape, f32) * (fan_in ** -0.5)

    def small(k, shape, scale=0.01):
        return jax.random.normal(k, shape, f32) * scale

    u = jax.random.uniform(ks[15], (N_RNN_LAYERS, 2, D_RNN), f32, minval=0.9, maxval=0.999)
    s_lam = u ** (1.0 / LRU_C)
    rnn_lambda = jnp.log(s_lam) - jnp.log1p(-s_lam)

    return {
        "x": jax.random.normal(ks[0], (BATCH, SEQ, D_MODEL), f32),
        "norm_mix": 1.0 + small(ks[1], (DEPTH, D_MODEL), 0.02),
        "norm_ffn": 1.0 + small(ks[2], (DEPTH, D_MODEL), 0.02),
        "attn_w_qkv": nrm(ks[3], (N_ATTN_LAYERS, D_MODEL, QKV_DIM), D_MODEL),
        "attn_q_gain": 1.0 + small(ks[4], (N_ATTN_LAYERS, HEAD_DIM), 0.02),
        "attn_k_gain": 1.0 + small(ks[5], (N_ATTN_LAYERS, HEAD_DIM), 0.02),
        "attn_w_o": nrm(ks[6], (N_ATTN_LAYERS, N_Q_HEADS * HEAD_DIM, D_MODEL), N_Q_HEADS * HEAD_DIM),
        "rnn_w_in": nrm(ks[7], (N_RNN_LAYERS, D_MODEL, 2 * D_RNN), D_MODEL),
        "rnn_conv_w": nrm(ks[8], (N_RNN_LAYERS, CONV_W, D_RNN), CONV_W),
        "rnn_conv_b": small(ks[9], (N_RNN_LAYERS, D_RNN)),
        "rnn_w_a": nrm(ks[10], (N_RNN_LAYERS, 2, RNN_BLOCKS, RNN_BLOCK_W, RNN_BLOCK_W), RNN_BLOCK_W),
        "rnn_b_a": small(ks[11], (N_RNN_LAYERS, 2, D_RNN)),
        "rnn_w_i": nrm(ks[12], (N_RNN_LAYERS, 2, RNN_BLOCKS, RNN_BLOCK_W, RNN_BLOCK_W), RNN_BLOCK_W),
        "rnn_b_i": small(ks[13], (N_RNN_LAYERS, 2, D_RNN)),
        "rnn_lambda": rnn_lambda,
        "rnn_w_out": nrm(ks[14], (N_RNN_LAYERS, D_RNN, D_MODEL), D_RNN),
        "ffn_w_gate": nrm(ks[16], (DEPTH, D_MODEL, D_FF), D_MODEL),
        "ffn_w_up": nrm(ks[17], (DEPTH, D_MODEL, D_FF), D_MODEL),
        "ffn_w_down": nrm(ks[18], (DEPTH, D_FF, D_MODEL), D_FF),
    }

def first_block(x, norm_mix, norm_ffn, attn_w_qkv, attn_q_gain, attn_k_gain, attn_w_o,
              rnn_w_in, rnn_conv_w, rnn_conv_b, rnn_w_a, rnn_b_a, rnn_w_i, rnn_b_i,
              rnn_lambda, rnn_w_out, ffn_w_gate, ffn_w_up, ffn_w_down):
    seq_len = x.shape[1]
    cos, sin = axial_rope_tables(seq_len)
    for i in range(DEPTH):
        j = i // N_MIXERS
        h = rms_norm(x, norm_mix[i])
        if i % N_MIXERS == 0:
            mix = attention_mixer(h, attn_w_qkv[j], attn_q_gain[j], attn_k_gain[j], attn_w_o[j], cos, sin)
        else:
            mix = recurrent_mixer(h, rnn_w_in[j], rnn_conv_w[j], rnn_conv_b[j], rnn_w_a[j], rnn_b_a[j],
                                  rnn_w_i[j], rnn_b_i[j], rnn_lambda[j], rnn_w_out[j])
        x = x + mix
        x = x + swiglu(rms_norm(x, norm_ffn[i]), ffn_w_gate[i], ffn_w_up[i], ffn_w_down[i])
    return x


DEPTH_2 = 1

MIX_WIDTH = D_MODEL
ATTN_WIDTH = MIX_WIDTH // 2
SSM_WIDTH = MIX_WIDTH - ATTN_WIDTH
HEAD_DIM_2 = 64
N_Q_HEADS_2 = ATTN_WIDTH // HEAD_DIM_2
KV_RATIO = 8
N_KV_HEADS_2 = N_Q_HEADS_2 // KV_RATIO
KV_DIM = N_KV_HEADS_2 * HEAD_DIM_2
WINDOW = 128
SSM_GROUP = 16
N_SSM_GROUPS = SSM_WIDTH // SSM_GROUP
STATE = 64
IN_COLS = ATTN_WIDTH + 2 * KV_DIM + SSM_WIDTH
D_FF_2 = ((8 * D_MODEL // 3 + 255) // 256) * 256
CONV_WIDTH = 3
NEG = -1e30


def rmsnorm(x, g):
    x32 = x.astype(jnp.float32)
    y = x32 * lax.rsqrt(jnp.mean(x32 * x32, axis=-1, keepdims=True) + EPS)
    return y.astype(x.dtype) * g

def sliding_window_attention(q, k, v, sinks):
    bsz, seq = q.shape[0], q.shape[1]
    nb = seq // WINDOW
    grp = N_Q_HEADS_2 // N_KV_HEADS_2
    qb = q.reshape(bsz, nb, WINDOW, N_KV_HEADS_2, grp, HEAD_DIM_2).astype(jnp.float32)

    def band(t):
        tb = t.reshape(bsz, nb, WINDOW, N_KV_HEADS_2, HEAD_DIM_2)
        prev = jnp.pad(tb, ((0, 0), (1, 0), (0, 0), (0, 0), (0, 0)))[:, :-1]
        return jnp.concatenate([prev, tb], axis=2)

    kb = band(k).astype(jnp.float32)
    vb = band(v)
    s = jnp.einsum('bnqhgd,bnkhd->bnhgqk', qb, kb) * (HEAD_DIM_2 ** -0.5)
    qi = jnp.arange(WINDOW)[:, None]
    kj = jnp.arange(2 * WINDOW)[None, :]
    in_band = (kj > qi) & (kj <= qi + WINDOW)
    blk = jnp.arange(nb)[:, None, None]
    valid = in_band[None] & ((blk * WINDOW + kj[None] - WINDOW) >= 0)
    s = jnp.where(valid[None, :, None, None], s, NEG)
    sink = sinks.astype(jnp.float32).reshape(1, 1, N_KV_HEADS_2, grp, 1, 1)
    m = jnp.maximum(jnp.max(s, axis=-1, keepdims=True), sink)
    e = jnp.exp(s - m)
    p = e / (jnp.sum(e, axis=-1, keepdims=True) + jnp.exp(sink - m))
    out = jnp.einsum('bnhgqk,bnkhd->bnqhgd', p.astype(v.dtype), vb)
    return out.reshape(bsz, seq, N_Q_HEADS_2 * HEAD_DIM_2)

def s5_ssm(u, lam_re, lam_im, log_step, b_re, b_im, c_re, c_im, d_skip):
    bsz, seq = u.shape[0], u.shape[1]
    dtype = u.dtype
    u4 = u.reshape(bsz, seq, N_SSM_GROUPS, SSM_GROUP).astype(jnp.float32)
    lr = lam_re.astype(jnp.float32)
    li = lam_im.astype(jnp.float32)
    dt = jnp.exp(log_step.astype(jnp.float32))[:, None]
    mag = jnp.exp(lr * dt)
    ang = li * dt
    ab_re = mag * jnp.cos(ang)
    ab_im = mag * jnp.sin(ang)
    den = lr * lr + li * li
    f_re = ((ab_re - 1.0) * lr + ab_im * li) / den
    f_im = (ab_im * lr - (ab_re - 1.0) * li) / den
    br = b_re.astype(jnp.float32)
    bi = b_im.astype(jnp.float32)
    bb_re = f_re[..., None] * br - f_im[..., None] * bi
    bb_im = f_re[..., None] * bi + f_im[..., None] * br
    bu_re = jnp.einsum('bsgh,gph->bsgp', u4, bb_re)
    bu_im = jnp.einsum('bsgh,gph->bsgp', u4, bb_im)
    a_re = jnp.broadcast_to(ab_re[None, None], (1, seq, N_SSM_GROUPS, STATE))
    a_im = jnp.broadcast_to(ab_im[None, None], (1, seq, N_SSM_GROUPS, STATE))

    def combine(e1, e2):
        a1r, a1i, b1r, b1i = e1
        a2r, a2i, b2r, b2i = e2
        return (a2r * a1r - a2i * a1i,
                a2r * a1i + a2i * a1r,
                a2r * b1r - a2i * b1i + b2r,
                a2r * b1i + a2i * b1r + b2i)

    _, _, xr, xi = lax.associative_scan(combine, (a_re, a_im, bu_re, bu_im), axis=1)
    y = (jnp.einsum('bsgp,ghp->bsgh', xr, c_re.astype(jnp.float32))
         - jnp.einsum('bsgp,ghp->bsgh', xi, c_im.astype(jnp.float32))
         + d_skip.astype(jnp.float32)[None, None] * u4)
    return y.reshape(bsz, seq, SSM_WIDTH).astype(dtype)

def causal_depthwise_conv(h, w, b):
    seq = h.shape[1]
    hp = jnp.pad(h, ((0, 0), (CONV_WIDTH - 1, 0), (0, 0)))
    out = b
    for k in range(CONV_WIDTH):
        out = out + hp[:, k:k + seq] * w[k]
    return out

def second_inputs(seed: int = 0) -> dict:
    key = jax.random.key(seed)
    ks = jax.random.split(key, 32)
    nrm = jax.random.normal
    G, P, H = N_SSM_GROUPS, STATE, SSM_GROUP
    return {
        "x": nrm(ks[0], (BATCH, SEQ, D_MODEL), jnp.float32),
        "c": nrm(ks[1], (BATCH, D_MODEL), jnp.float32),
        "w_ada": nrm(ks[2], (DEPTH_2, D_MODEL, 6 * D_MODEL), jnp.float32) * (0.5 * D_MODEL ** -0.5),
        "b_ada": nrm(ks[3], (DEPTH_2, 6 * D_MODEL), jnp.float32) * 0.02,
        "g_pre_mix": 1.0 + 0.1 * nrm(ks[4], (DEPTH_2, D_MODEL), jnp.float32),
        "g_post_mix": 1.0 + 0.1 * nrm(ks[5], (DEPTH_2, D_MODEL), jnp.float32),
        "w_in": nrm(ks[6], (DEPTH_2, D_MODEL, IN_COLS), jnp.float32) * D_MODEL ** -0.5,
        "attn_sinks": nrm(ks[7], (DEPTH_2, N_Q_HEADS_2), jnp.float32),
        "lam_re": -0.5 + 0.01 * nrm(ks[8], (DEPTH_2, G, P), jnp.float32),
        "lam_im": jnp.pi * jnp.arange(P, dtype=jnp.float32)[None, None, :]
                  + 0.01 * nrm(ks[9], (DEPTH_2, G, P), jnp.float32),
        "log_step": jax.random.uniform(ks[10], (DEPTH_2, G), jnp.float32,
                                       minval=math.log(1e-3), maxval=math.log(1e-1)),
        "ssm_b_re": nrm(ks[11], (DEPTH_2, G, P, H), jnp.float32) * (2 * H) ** -0.5,
        "ssm_b_im": nrm(ks[12], (DEPTH_2, G, P, H), jnp.float32) * (2 * H) ** -0.5,
        "ssm_c_re": nrm(ks[13], (DEPTH_2, G, H, P), jnp.float32) * 0.5,
        "ssm_c_im": nrm(ks[14], (DEPTH_2, G, H, P), jnp.float32) * 0.5,
        "ssm_d": nrm(ks[15], (DEPTH_2, G, H), jnp.float32),
        "w_glu": nrm(ks[16], (DEPTH_2, SSM_WIDTH, SSM_WIDTH), jnp.float32) * SSM_WIDTH ** -0.5,
        "g_attn_out": 1.0 + 0.1 * nrm(ks[17], (DEPTH_2, ATTN_WIDTH), jnp.float32),
        "g_ssm_out": 1.0 + 0.1 * nrm(ks[18], (DEPTH_2, SSM_WIDTH), jnp.float32),
        "w_out": nrm(ks[19], (DEPTH_2, MIX_WIDTH, D_MODEL), jnp.float32) * MIX_WIDTH ** -0.5,
        "g_pre_ffn": 1.0 + 0.1 * nrm(ks[20], (DEPTH_2, D_MODEL), jnp.float32),
        "g_post_ffn": 1.0 + 0.1 * nrm(ks[21], (DEPTH_2, D_MODEL), jnp.float32),
        "w_up": nrm(ks[22], (DEPTH_2, D_MODEL, 2 * D_FF_2), jnp.float32) * D_MODEL ** -0.5,
        "conv_w": nrm(ks[23], (DEPTH_2, CONV_WIDTH, 2 * D_FF_2), jnp.float32) * CONV_WIDTH ** -0.5,
        "conv_b": nrm(ks[24], (DEPTH_2, 2 * D_FF_2), jnp.float32) * 0.01,
        "w_down": nrm(ks[25], (DEPTH_2, D_FF_2, D_MODEL), jnp.float32) * D_FF_2 ** -0.5,
    }

def second_block(x, c, w_ada, b_ada, g_pre_mix, g_post_mix, w_in, attn_sinks, lam_re, lam_im,
              log_step, ssm_b_re, ssm_b_im, ssm_c_re, ssm_c_im, ssm_d, w_glu, g_attn_out,
              g_ssm_out, w_out, g_pre_ffn, g_post_ffn, w_up, conv_w, conv_b, w_down):
    bsz, seq = x.shape[0], x.shape[1]
    c_act = jax.nn.silu(c)
    for l in range(DEPTH_2):
        ada = c_act @ w_ada[l] + b_ada[l]
        sh_m, sc_m, gt_m, sh_f, sc_f, gt_f = [t[:, None, :] for t in jnp.split(ada, 6, axis=-1)]

        h = rmsnorm(x, g_pre_mix[l]) * (1.0 + sc_m) + sh_m
        proj = h @ w_in[l]
        q = proj[..., :ATTN_WIDTH].reshape(bsz, seq, N_Q_HEADS_2, HEAD_DIM_2)
        k = proj[..., ATTN_WIDTH:ATTN_WIDTH + KV_DIM].reshape(bsz, seq, N_KV_HEADS_2, HEAD_DIM_2)
        v = proj[..., ATTN_WIDTH + KV_DIM:ATTN_WIDTH + 2 * KV_DIM].reshape(bsz, seq, N_KV_HEADS_2, HEAD_DIM_2)
        u = proj[..., ATTN_WIDTH + 2 * KV_DIM:]

        attn = sliding_window_attention(q, k, v, attn_sinks[l])
        y = s5_ssm(u, lam_re[l], lam_im[l], log_step[l], ssm_b_re[l], ssm_b_im[l],
                   ssm_c_re[l], ssm_c_im[l], ssm_d[l])
        z = jax.nn.gelu(y, approximate=True)
        ssm = z * jax.nn.sigmoid(z @ w_glu[l])

        merged = jnp.concatenate([rmsnorm(attn, g_attn_out[l]), rmsnorm(ssm, g_ssm_out[l])], axis=-1)
        mix = merged @ w_out[l]
        x = x + (1.0 + gt_m) * rmsnorm(mix, g_post_mix[l])

        h = rmsnorm(x, g_pre_ffn[l]) * (1.0 + sc_f) + sh_f
        up = causal_depthwise_conv(h @ w_up[l], conv_w[l], conv_b[l])
        val, gate = up[..., :D_FF_2], up[..., D_FF_2:]
        ff = (jax.nn.gelu(gate, approximate=True) * val) @ w_down[l]
        x = x + (1.0 + gt_f) * rmsnorm(ff, g_post_ffn[l])
    return x


def setup_inputs(seed=0):
    out = dict(first_inputs(seed))
    for name, value in second_inputs(seed + 1).items():
        if name != "x":
            out[name + "_2"] = value
    return out


def reference(
    x, norm_mix, norm_ffn, attn_w_qkv, attn_q_gain, attn_k_gain, attn_w_o, rnn_w_in, rnn_conv_w,
    rnn_conv_b, rnn_w_a, rnn_b_a, rnn_w_i, rnn_b_i, rnn_lambda, rnn_w_out, ffn_w_gate, ffn_w_up,
    ffn_w_down, c_2, w_ada_2, b_ada_2, g_pre_mix_2, g_post_mix_2, w_in_2, attn_sinks_2,
    lam_re_2, lam_im_2, log_step_2, ssm_b_re_2, ssm_b_im_2, ssm_c_re_2, ssm_c_im_2, ssm_d_2,
    w_glu_2, g_attn_out_2, g_ssm_out_2, w_out_2, g_pre_ffn_2, g_post_ffn_2, w_up_2, conv_w_2,
    conv_b_2, w_down_2,
):
    x = first_block(
        x, norm_mix, norm_ffn, attn_w_qkv, attn_q_gain, attn_k_gain, attn_w_o, rnn_w_in,
        rnn_conv_w, rnn_conv_b, rnn_w_a, rnn_b_a, rnn_w_i, rnn_b_i, rnn_lambda, rnn_w_out,
        ffn_w_gate, ffn_w_up, ffn_w_down,
    )
    return second_block(
        x, c_2, w_ada_2, b_ada_2, g_pre_mix_2, g_post_mix_2, w_in_2, attn_sinks_2, lam_re_2,
        lam_im_2, log_step_2, ssm_b_re_2, ssm_b_im_2, ssm_c_re_2, ssm_c_im_2, ssm_d_2, w_glu_2,
        g_attn_out_2, g_ssm_out_2, w_out_2, g_pre_ffn_2, g_post_ffn_2, w_up_2, conv_w_2,
        conv_b_2, w_down_2,
    )


_drawn_inputs = setup_inputs


def setup_inputs(seed=0):
    import zlib

    import numpy as np

    out = dict(_drawn_inputs(seed))
    spreads = {}
    factors = {'norm_mix': 3.337,
     'attn_q_gain': 8.0,
     'attn_k_gain': 8.0,
     'rnn_b_a': 160.813,
     'rnn_b_i': 117.092,
     'lam_re_2': 200.0,
     'conv_b_2': 161.331,
     'norm_ffn': 7.336,
     'rnn_conv_b': 10.399,
     'b_ada_2': 7.663,
     'g_pre_mix_2': 4.463,
     'g_post_mix_2': 29.134,
     'attn_sinks_2': 64.0,
     'lam_im_2': 38.72,
     'log_step_2': 49.912,
     'ssm_b_re_2': 52.72,
     'ssm_b_im_2': 51.872,
     'ssm_c_re_2': 50.544,
     'ssm_c_im_2': 52.2,
     'g_attn_out_2': 51.784,
     'g_ssm_out_2': 51.68,
     'g_pre_ffn_2': 14.835,
     'g_post_ffn_2': 28.601}
    for name, (base, spread) in spreads.items():
        noise = np.random.default_rng([zlib.crc32(name.encode()), seed]).standard_normal(out[name].shape)
        drawn = base * np.exp(spread * noise) if base else spread * noise
        out[name] = __import__('jax').numpy.asarray(drawn.astype(out[name].dtype))
    for name, factor in factors.items():
        out[name] = (out[name] * factor).astype(out[name].dtype)
    return out
```

```python
from contextlib import ExitStack

import numpy as np
import concourse.bass as bass
from concourse import mybir

F32 = mybir.dt.float32
F32R = mybir.dt.float32r
ACT = mybir.ActivationFunctionType
ALU = mybir.AluOpType
AX = mybir.AxisListType.X

P = 128
D = 2048
S = 256
T = S // P
FC = D // P
NW = 512
KT = 2
TW = KT * NW
RING = 4
D_FF = 5632
FFC = D_FF // P
EPS = 1e-6
HEAD = 128
QH, KVH = 16, 4
FREQS = 32
RNN_BLOCKS, RNN_W = 8, 256
HALF = 2
LRU_C = 8.0
HEAD2 = 64
QH2, KVH2 = 16, 2
W2 = 1024
WINDOW = 128
GROUP, STATE = 16, 64
ST = 32
ADA_CHUNKS = 6 * D // NW
NEG = -1e30

LAYERS = [("qkv", 3, 8), ("w_o", 2, 8), ("ffn0", 11, 8), ("down0", 2, 22), ("rnn_in", 4, 8),
          ("rnn_out", 2, 8), ("ffn1", 11, 8), ("down1", 2, 22), ("w_in", 2, 8), ("w_in_kv", 0, 4),
          ("glu", 1, 4), ("w_out", 2, 8), ("ffn2", 11, 8), ("down2", 2, 22)]
TILE0, CHUNK0, CHUNK1 = {}, {}, {}
_n = _e = _o = 0
for _name, _pairs, _kt in LAYERS:
    TILE0[_name], CHUNK0[_name], CHUNK1[_name] = _n, _e, _o
    _n += max(1, 2 * _pairs) * _kt
    _e += max(1, _pairs)
    _o += _pairs
TILES = _n
PAIRS = {a: b for a, b, _ in LAYERS}
KTILES = {a: c for a, _, c in LAYERS}
GROUPS = [("first", 2, 2), ("w_o", 2, 2), ("ffn0", 11, 0), ("down0", 2, 2), ("rnn_in", 8, 0),
          ("rnn_out", 2, 2), ("ffn1", 11, 0), ("norm_mix", 2, 2), ("ssm_b", 1, 1), ("w_in", 2, 2),
          ("w_in_k", 1, 0), ("glu", 1, 1), ("merge", 2, 2), ("norm_ffn", 2, 2), ("ffn2", 11, 11)]
GROUP_AT = {}
_a = _b = 0
for _name, _x, _y in GROUPS:
    GROUP_AT[_name] = (_a, _b)
    _a, _b = _a + _x, _b + _y

NORM_AT = {name: n + 1 for n, name in enumerate(
    ("first", "w_o", "down0", "rnn_out", "down1", "merge", "w_out", "norm_ffn", "down2"))}
RES_AT = {name: n for n, name in enumerate(("w_o", "down0", "rnn_out", "down1"))}

SMALL = [("g_mix0", 16), ("g_mix1", 16), ("g_ffn0", 16), ("g_ffn1", 16), ("conv_w", 64),
         ("conv_b", 16), ("b_a", 32), ("b_i", 32), ("lam", 32), ("c", 16), ("b_ada", 96),
         ("g_pre_mix", 16), ("g_post_mix", 16), ("g_pre_ffn", 16), ("g_post_ffn", 16),
         ("g_merged", 16), ("d_skip", 8), ("conv2_w", 264), ("conv2_b", 88), ("lam_re", 32),
         ("lam_im", 32), ("log_step", 32), ("sinks", 16), ("ident", 128)]
SMALL_AT = {}
_n = 0
for _name, _w in SMALL:
    SMALL_AT[_name] = (_n, _w)
    _n += _w
NSMALL = _n
HOOK = 3


def build(nc, x_in, weights, ada_w, gate_w, small_in, rope_in, ssm_in, mask_in, out, upto="down2"):
    names = [a for a, _, _ in LAYERS]
    order = names.index(upto)
    has = lambda name: names.index(name) <= order
    n_tiles = TILES if upto == "down2" else TILE0[upto] + max(1, 2 * PAIRS[upto]) * KTILES[upto] + RING
    ctx = ExitStack()
    with ctx:
        sems = {}

        def sem(name):
            if name not in sems:
                sems[name] = ctx.enter_context(nc.semaphore(name))
            return sems[name]

        cursor = [16512]

        def place(name, cols, dt=F32, at=None):
            if at is None:
                at = cursor[0]
                cursor[0] += 4 * cols
            return nc.alloc_sbuf_tensor_at(name, [P, cols], dt, offset=at)[:, :], at

        def shaped(ap, pattern, **kw):
            return ap.rearrange(pattern, **kw)

        raw_, _ = place("raw", RING * TW)
        whi_, _ = place("w_hi", RING * TW, F32R)
        wlo_, _ = place("w_lo", RING * TW, F32R)
        x_, _ = place("x_tok", T * D)
        _, xt_at = place("xt_region", 2 * FC * S)
        xhi_, _ = place("xt_hi", FC * S, F32R, at=xt_at)
        xlo_, _ = place("xt_lo", FC * S, F32R, at=xt_at + 4 * FC * S)
        sc_, _ = place("scratch", 2 * FC * S, at=xt_at)
        _, mid_at = place("mid_region", 2 * FFC * S)
        mhi_, _ = place("mid_hi", FFC * S, F32R, at=mid_at)
        mlo_, _ = place("mid_lo", FFC * S, F32R, at=mid_at + 4 * FFC * S)
        mid_, _ = place("mid", 2 * FFC * S, at=mid_at)
        tmp_, _ = place("tmp", 2 * T * NW)
        small_, _ = place("small", NSMALL)
        ones_, _ = place("ones", P)
        adacc_, ada_at = place("ada_acc", NW)
        araw_, araw_at = place("ada_raw", 2 * TW)
        conv_, _ = place("conv_buf", 4 * 2 * S, at=ada_at)
        adat_, _ = place("ada_t", 96)
        stat_, _ = place("stat", 48)
        assert cursor[0] <= 229344, cursor

        raw = shaped(raw_, "p (r e) -> p r e", r=RING)
        whi = shaped(whi_, "p (r e) -> p r e", r=RING)
        wlo = shaped(wlo_, "p (r e) -> p r e", r=RING)
        x = shaped(x_, "p (t n e) -> p t n e", t=T, e=NW)
        xhi = shaped(xhi_, "p (c s) -> p c s", s=S)
        xlo = shaped(xlo_, "p (c s) -> p c s", s=S)
        mhi = shaped(mhi_, "p (c s) -> p c s", s=S)
        mlo = shaped(mlo_, "p (c s) -> p c s", s=S)
        tmp = shaped(tmp_, "p (b t e) -> p b t e", b=2, t=T)
        araw = shaped(araw_, "p (r k e) -> p r k e", r=2, k=KT)
        conv = shaped(conv_, "p (c s) -> p c s", s=S)
        sm = {k: small_[:, a:a + w] for k, (a, w) in SMALL_AT.items()}
        ident = sm["ident"]
        ones = ones_
        ss = stat_[:, 0:8].rearrange("p (t n) -> p t n", t=T)
        mean = stat_[:, 8:12]
        root = stat_[:, 12:16]
        rstd = stat_[:, 16:20]
        c_act = stat_[:, 20:36]
        mid = lambda a, n: mid_[:, a:a + n]
        scr = lambda a, n: sc_[:, a:a + n]

        psum = nc.alloc_psum_tensor("psum", [P, 8, NW], F32)
        acc = [psum[:, 2 * b:2 * b + 2, :] for b in range(2)]
        tr = [psum[:, 4 + 2 * b:6 + 2 * b, :].rearrange("p b (c s) -> p (b c) s", s=S) for b in range(2)]

        raw_arrived = [sem(f"raw_arrived{s}") for s in range(RING)]
        hi_ready, lo_ready, tiles_used = sem("hi_ready"), sem("lo_ready"), sem("tiles_used")
        tr_ready = [sem("tr_ready0"), sem("tr_ready1")]
        tr_free = [sem("tr_free0"), sem("tr_free1")]
        small_arrived, x_arrived, stored = sem("small_arrived"), sem("x_arrived"), sem("stored")
        ones_ready = sem("ones_ready")
        ada_arrived = [sem("ada_arrived0"), sem("ada_arrived1")]
        ada_used, ada_step = sem("ada_used"), sem("ada_step")
        ada_summed, ada_reduced = sem("ada_summed"), sem("ada_reduced")
        ada_done = sem("ada_done")
        rstd_ready = sem("rstd_ready")


        def after(eng, what, value):
            if not isinstance(value, int) or value > 0:
                eng.wait_ge(what, value)

        steps_taken = {"vector": 0, "gpsimd": 0}

        def ordered(eng, name):
            what = sem(f"{name}_steps")

            def link(instruction):
                steps_taken[name] += 1
                instruction.then_inc(what, 1)
                eng.wait_ge(what, steps_taken[name])
            return link

        def each_pair(eng, layer, body):
            n = PAIRS[layer]
            if layer == "rnn_in":
                for i in range(n):
                    body(i, i == 0)
                return
            body(0, True)
            if n == 2:
                body(1, False)
            elif n > 2:
                with eng.Fori(1, n) as i:
                    body(i, False)

        ADA_AT = {"ffn0": 0, "ffn1": 11, "down1": 22}
        ADA_POS = range(4, 12)

        qkv = mid(0, 6144).rearrange("p (t n e) -> p t n e", t=T, e=NW)
        qkv_h = mid(0, 6144).rearrange("p (t h d) -> p t h d", t=T, d=HEAD)
        rope = mid(6144, 512)
        tabs = mid(6656, 1024).rearrange("p (k t d) -> p k t d", k=4, t=T)
        rot = mid(7680, 5120).rearrange("p (t h d) -> p t h d", t=T, d=HEAD)
        swapped = mid(12800, 5120).rearrange("p (t h d) -> p t h d", t=T, d=HEAD)
        qk_t = mid(12800, 5120).rearrange("p (h s) -> p h s", s=S)
        ohi_, _ = place("o_hi", FC * S, F32R, at=mid_at + 4 * 7680)
        olo_, _ = place("o_lo", FC * S, F32R, at=mid_at + 4 * 17920)
        ohi = shaped(ohi_, "p (c s) -> p c s", s=S)
        olo = shaped(olo_, "p (c s) -> p c s", s=S)
        squares = scr(0, 5120).rearrange("p (t h d) -> p t h d", t=T, d=HEAD)
        probs = scr(6144, 2048).rearrange("p (b i k) -> p b i k", b=2, k=S)
        probs_t = scr(0, 2048).rearrange("p (b h k q) -> p b h k q", b=2, h=2, k=T)
        ssq = mid(22016, 40)
        rq = mid(22016 + 40, 40)
        rqs = mid(22016 + 80, 40)
        mx = mid(22016 + 120, 32)
        nmx = mid(22016 + 152, 32)
        sums = mid(22016 + 184, 32)
        rinv = mid(22016 + 216, 32)
        s_rot, s_sq, s_rq = sem("rotated"), sem("squares_ready"), sem("head_root")
        s_qt, s_qe_a, s_qe_v = sem("qk_transposed"), sem("qk_out_act"), sem("qk_out_dve")
        s_sc, s_nm, s_exp, s_pn = sem("scores_ready"), sem("max_ready"), sem("exp_ready"), sem("probs_ready")
        s_pt, s_pte, s_pv, s_oh, s_ol = (sem("probs_turned"), sem("probs_t_ready"), sem("heads_ready"),
                                         sem("o_hi_ready"), sem("o_lo_ready"))
        s_rope = sem("rope_arrived")

        xb = mid(0, 4096).rearrange("p (c s) -> p c s", s=S)
        y_gelu = mid(4096, 4096).rearrange("p (c s) -> p c s", s=S)
        xc = mid(8192, 4096).rearrange("p (c s) -> p c s", s=S)
        hhi_, _ = place("h_hi", FC * S, F32R, at=mid_at + 4 * 8192)
        hlo_, _ = place("h_lo", FC * S, F32R, at=mid_at + 4 * 4096)
        hhi = shaped(hhi_, "p (c s) -> p c s", s=S)
        hlo = shaped(hlo_, "p (c s) -> p c s", s=S)
        of_batch = lambda at: mid(at, 2048).rearrange("p (c d s) -> p c d s", d=2, s=S)
        half_tanh = [of_batch(12288), of_batch(0)]
        decay = [of_batch(14336), of_batch(18432)]
        drive = [of_batch(16384), of_batch(2048)]
        gw_shape = lambda ap: ap.rearrange("p (k d g j) -> p k d g j", k=2, d=2, g=2)
        gate_ws = [gw_shape(mid(20480, 2048)), gw_shape(araw_)]
        gates = psum[:, 6:8, :].rearrange("p d (g s) -> p d g s", g=2)
        lam_tmp = [mid(22016 + 32 * i, 32) for i in range(4)]
        neg4sp = sm["lam"]
        gate_arrived = [sem("gate_w_arrived0"), sem("gate_w_arrived1")]
        s_xb, s_base, s_conv, s_y = sem("xb_ready"), sem("conv_base"), sem("conv_ready"), sem("y_ready")
        s_gate, s_sig, s_tanh, s_ig, s_drive = (sem("gates_summed"), sem("r_ready"), sem("tanh_ready"),
                                                sem("i_ready"), sem("drive_started"))
        s_unit, s_sqrt, s_mixed, s_hhi, s_hlo = (sem("unit_ready"), sem("sqrt_ready"), sem("mixed_ready"),
                                                 sem("h_hi_ready"), sem("h_lo_ready"))
        s_lam = sem("lambda_ready")
        UNITS = 16

        normed = mid(0, 4096).rearrange("p (t e) -> p t e", t=T)
        shifted = [mid(4608 + 1024 * i, 1024).rearrange("p (c s) -> p c s", s=S) for i in range(2)]
        proj = mid(4608, 4608).rearrange("p (t e) -> p t e", t=T)
        q2_t = mid(0, 2048).rearrange("p (c s) -> p c s", s=S)
        k2_t = mid(2048, S)
        u_t = mid(2304, 2048).rearrange("p (c s) -> p c s", s=S)
        merged = mid(9216, 4096).rearrange("p (t e) -> p t e", t=T)
        by_tile = lambda ap, e: ap.rearrange("p (c e) -> p c e", e=e)
        e1 = [by_tile(mid(13312 + 512 * i, 512), 16) for i in range(2)]
        e16 = [by_tile(mid(14336 + 512 * i, 512), 16) for i in range(2)]
        bb_t = [by_tile(mid(15360 + 1024 * i, 1024), P) for i in range(2)]
        c_re, nc_re, nc_im = (by_tile(mid(17408 + 1024 * i, 1024), 2 * GROUP) for i in range(3))
        ssm_raw = mid(20480, 2048)
        b_raw = [by_tile(ssm_raw[:, 512 * i:512 * i + 512], GROUP) for i in range(2)]
        c_raw = [by_tile(ssm_raw[:, 1024 + 512 * i:1536 + 512 * i], GROUP) for i in range(2)]
        z_t = by_tile(mid(20480, 2048), S)
        bd = [by_tile(mid(1024 * i, 1024), 2 * GROUP) for i in range(2)]
        cm_tmp = [mid(2048 + 256 * i, 256) for i in range(4)]
        st_tmp = [mid(3072 + 32 * i, 32) for i in range(32)]
        mag_keep = sm["lam_re"]
        mask = conv_[:, 0:384]
        masked = conv_[:, 384:1920].rearrange("p (h k) -> p h k", k=384)
        turned = tmp_[:, 0:1536].rearrange("p (h n q) -> p h n q", h=4, n=3)
        m2, nm2, sum2, rinv2 = (scr(8 * 4 * i, 32) for i in range(4))
        big = lambda ap: ap.rearrange("p (c s) -> p c s", s=S)
        cos_t = [scr(1024 * i, 1024) for i in range(2)]
        sin_t = [scr(2048 + 1024 * i, 1024) for i in range(2)]
        tab_tmp = [scr(4096 + 1024 * i, 1024) for i in range(2)]
        z_re, z_im = scr(6144, 1024), scr(7168, 1024)
        parts = [mid(4608 + 1024 * i, 1024) for i in range(4)]
        rot_tmp = [tmp_[:, 1024 * i:1024 * i + 1024] for i in range(2)]
        mixed = mid(0, 4096).rearrange("p (t n e) -> p t n e", t=T, e=NW)
        mixed_ff = scr(0, 4096).rearrange("p (t n e) -> p t n e", t=T, e=NW)
        gain_mix, gain_ff = mid(4096, D), scr(4096, D)
        diag_mix, diag_ff = mid(13312, D), conv_
        sh_m, gs_m, gp_m, sh_f, gs_f, gp_f = (adat_[:, 16 * i:16 * i + 16] for i in range(6))
        ssm_arrived, mask_arrived, ada_ready = sem("ssm_arrived"), sem("mask_arrived"), sem("ada_gains")

        LHS = {"qkv": (xhi, xlo), "w_o": (ohi, olo), "ffn0": (xhi, xlo), "down0": (mhi, mlo),
               "rnn_in": (xhi, xlo), "rnn_out": (hhi, hlo), "ffn1": (xhi, xlo), "down1": (mhi, mlo), "w_in": (xhi, xlo),
               "w_in_kv": (xhi, xlo), "glu": (xhi, xlo), "w_out": (xhi, xlo), "ffn2": (xhi, xlo),
               "down2": (mhi, mlo)}
        RESIDUAL = {"w_o": "g_ffn0", "down0": "g_mix1", "rnn_out": "g_ffn1", "down1": None}
        GATHERED = {"w_out": mixed, "down2": mixed_ff}
        GATED = ("ffn0", "ffn1")

        def released(layer, b):
            if layer in RESIDUAL:
                return f"sum_ready{b}"
            if layer == "ffn2":
                return f"ffn2_copied{b}"
            return f"{layer}_{('gate', 'prod')[b]}" if layer in GATED else f"{layer}_out{b}"

        block = ctx.enter_context(nc.Block())

        @block.sync
        def _(sp):
            sp.dma_start(small_, small_in).then_inc(small_arrived, 16)
            sp.dma_start(x_.rearrange("p (t e) -> p t e", t=T),
                         x_in.rearrange("(t p) e -> p t e", p=P)).then_inc(x_arrived, 16)
            for s in range(RING):
                sp.dma_start(raw[:, s, :], weights[s]).then_inc(raw_arrived[s], 16)
            sp.dma_start(rope, rope_in).then_inc(s_rope, 16)
            with sp.Fori(1, n_tiles // RING) as i:
                for s in range(RING):
                    sp.wait_ge(lo_ready, i * RING + (s - 3))
                    sp.dma_start(raw[:, s, :], weights[i * RING + s]).then_inc(raw_arrived[s], 16)

        def finish(pool):
            pool.wait_ge(sem("x_final"), 2 if upto == "down2" else 1)
            pool.dma_start(out.rearrange("(t p) e -> p t e", p=P),
                           x_.rearrange("p (t e) -> p t e", t=T)).then_inc(stored, 16)
            pool.wait_ge(stored, 16)

        @block.gpsimd
        def _(pool):
            nc.gpsimd.memset(ones, 1.0).then_inc(ones_ready, 1)
            if has("down1"):
                for s in range(2):
                    pool.dma_start(araw_[:, s * TW:(s + 1) * TW], ada_w[s]).then_inc(ada_arrived[s], 16)

                def ada_tiles(i):
                    for s in range(2):
                        pool.wait_ge(ada_step, i * 4 + (2 * s - 2))
                        pool.dma_start(araw_[:, s * TW:(s + 1) * TW], ada_w[i * 2 + s]).then_inc(ada_arrived[s], 16)
                with pool.Fori(1, 11 * 4) as i:
                    ada_tiles(i)
            if has("rnn_in"):
                for b in range(RNN_BLOCKS):
                    if b == 0:
                        pool.wait_ge(tiles_used, TILE0["rnn_in"])
                    elif b == 1:
                        after(pool, ada_step, 11 * 16 if has("down1") else 0)
                    else:
                        pool.wait_ge(s_gate, 2 * (b - 1))
                    dst = mid(20480, 2048) if b % 2 == 0 else araw_
                    pool.dma_start(dst, gate_w[b]).then_inc(gate_arrived[b % 2], 16)
            if has("down1"):
                pool.wait_ge(s_gate, UNITS)
                with pool.Fori(11 * 4, ADA_CHUNKS * 4) as i:
                    ada_tiles(i)
            if has("w_in"):
                pool.wait_ge(tiles_used, TILE0["w_in"])
                pool.dma_start(ssm_raw, ssm_in).then_inc(ssm_arrived, 16)
                pool.wait_ge(ada_step, ADA_CHUNKS * 16)
                pool.wait_ge(ada_summed, ADA_CHUNKS)
                pool.dma_start(mask, mask_in).then_inc(mask_arrived, 16)
                pool.wait_ge(sem("e_ready"), 1)
                pool.wait_ge(sem("attn2_done"), 1)
                link = ordered(pool, "gpsimd")
                G = nc.gpsimd
                for q in range(8):
                    s4 = slice(4 * q, 4 * q + 4)
                    grid = [P, 4, 16, 16]
                    coarse = [e16[i][:, s4, :].unsqueeze(3).to_broadcast(grid) for i in range(2)]
                    fine = [e1[i][:, s4, :].unsqueeze(2).to_broadcast(grid) for i in range(2)]
                    four = lambda ap: ap.rearrange("p (c a b) -> p c a b", a=16, b=16)
                    after(pool, sem("tables_used"), q - 1)
                    G.tensor_tensor(four(tab_tmp[0]), coarse[0], fine[0], ALU.mult)
                    link(G.tensor_tensor(four(tab_tmp[1]), coarse[1], fine[1], ALU.mult))
                    link(G.tensor_tensor(cos_t[q % 2], tab_tmp[0], tab_tmp[1], ALU.subtract))
                    G.tensor_tensor(four(tab_tmp[0]), coarse[0], fine[1], ALU.mult)
                    link(G.tensor_tensor(four(tab_tmp[1]), coarse[1], fine[0], ALU.mult))
                    G.tensor_tensor(sin_t[q % 2], tab_tmp[0], tab_tmp[1], ALU.add).then_inc(sem("tables_ready"), 1)
                    pool.wait_ge(sem("tables_ready"), q + 1)
            finish(pool)


        @block.scalar
        def _(act):
            A = nc.scalar.activation
            splits = [0]

            def split(tile):
                s = splits[0] % RING
                splits[0] += 1
                act.wait_ge(raw_arrived[s], (tile + (RING - s)) * (16 // RING))
                after(act, tiles_used, tile - (RING - 1) if isinstance(tile, int) else tile + (1 - RING))
                A(whi[:, s, :], raw[:, s, :], ACT.Copy).then_inc(hi_ready, 1)

            def group_hi(b, before, dst, g, signal):
                act.wait_ge(tr_ready[b], before + 1)
                for j in range(4):
                    ins = A(dst[:, j, :], tr[b][:, j, :], ACT.Copy, scale=g[:, j:j + 1])
                ins.then_inc(signal, 1)

            def root_of(name, n):
                act.wait_ge(sem("mean_ready"), NORM_AT[name])
                A(root[:, 0:n], mean[:, 0:n], ACT.Sqrt).then_inc(sem("root_ready"), 1)

            def run(layer, evac, tail=None, extra=None, late=()):
                kt = KTILES[layer]

                def body(i, first):
                    splits[0] = TILE0[layer] + RING
                    for pos in range(2 * kt):
                        if not (layer == "down2" and not first and pos >= 2 * kt - RING):
                            split(i * (2 * kt) + (TILE0[layer] + pos + RING))
                        if extra:
                            extra(i, pos)
                        for at, step in late:
                            if at == pos and not first:
                                step(i - 1)
                        if tail and pos == HOOK and not first:
                            tail(i - 1, 1)
                        if pos == kt - 1:
                            evac(i, 0)
                        if tail and pos == kt + HOOK:
                            tail(i, 0)
                        if pos == 2 * kt - 1:
                            evac(i, 1)

                each_pair(act, layer, body)
                if tail:
                    tail(PAIRS[layer] - 1, 1)
                for _, step in late:
                    step(PAIRS[layer] - 1)

            def chunk_done(layer, i, b):
                act.wait_ge(tiles_used, i * (2 * KTILES[layer]) + (TILE0[layer] + (b + 1) * KTILES[layer]))

            def scaled_to(layer, dst, ready=None):
                def evac(i, b):
                    if ready:
                        ready(i, b)
                    chunk_done(layer, i, b)
                    for t in range(T):
                        ins = A(dst(i, b, t), acc[b][:, t, :], ACT.Copy, scale=rstd[:, t:t + 1])
                    ins.then_inc(sem(f"{layer}_out{b}"), 1)
                return evac

            def residual(layer):
                g = RESIDUAL[layer]

                def evac(i, b):
                    act.wait_ge(sem(f"sum_ready{b}"), i + (2 * RES_AT[layer] + 1))
                    A(x[:, :, 2 * i + b, :], tmp[:, b, :, :], ACT.Copy).then_inc(sem(f"x_new{b}"), 1)

                def tail(i, b):
                    if g:
                        c = 4 * (2 * i + b)
                        group_hi(b, GROUP_AT[layer][b] + i, xhi[:, c:c + 4, :], sm[g][:, c:c + 4],
                                 sem("residual_hi"))
                    act.wait_ge(sem(f"x_new{b}"), i + (2 * RES_AT[layer] + 1))
                    for t in range(T):
                        ins = A(tmp[:, b, t, :], tmp[:, b, t, :], ACT.Square,
                                accum_out=ss[:, t, 2 * i + b:2 * i + b + 1])
                    ins.then_inc(sem(f"sum_used{b}"), 1)
                run(layer, evac, tail)
                root_of(layer, 2)

            def gated(layer):
                def evac(i, b):
                    if b:
                        return
                    if not isinstance(i, int):
                        act.wait_ge(sem(f"{layer}_prod"), i)
                    chunk_done(layer, i, 0)
                    for t in range(T):
                        ins = A(tmp[:, 0, t, :], acc[0][:, t, :], ACT.Silu, scale=rstd[:, t:t + 1])
                    ins.then_inc(sem(f"{layer}_gate"), 1)

                def tail(i, b):
                    if b:
                        act.wait_ge(tr_ready[0], i + (GROUP_AT[layer][0] + 1))
                        A(mhi_.rearrange("p (n e) -> p n e", e=4 * S)[:, i, :],
                          tr[0].rearrange("p c s -> p (c s)"), ACT.Copy).then_inc(sem(f"{layer}_hi"), 1)
                act.wait_ge(rstd_ready, {"ffn0": 2, "ffn1": 4}[layer])
                run(layer, evac, tail)

            def recurrent_in():
                def evac(i, b):
                    chunk_done("rnn_in", i, b)
                    c = 2 * i + b
                    if c >= 2:
                        act.wait_ge(tr_ready[0], GROUP_AT["rnn_in"][0] + c - 1)
                    for t in range(T):
                        ins = A(tmp[:, b, t, :], acc[b][:, t, :], ACT.Copy, scale=rstd[:, t:t + 1])
                    ins.then_inc(sem(f"rnn_in_out{b}"), 1)

                def tail(i, b):
                    c = 2 * i + b
                    if c < 4:
                        act.wait_ge(s_xb, c + 1)
                        for j in range(4 * c, 4 * c + 4):
                            ins = A(xc[:, j, :], xb[:, j, :], ACT.Identity, scale=sm["conv_w"][:, 32 + j:33 + j],
                                    bias=sm["conv_b"][:, j:j + 1])
                        ins.then_inc(s_base, 1)
                    else:
                        act.wait_ge(tr_ready[0], GROUP_AT["rnn_in"][0] + c + 1)
                        A(y_gelu[:, 4 * c - 16:4 * c - 12, :], tr[0], ACT.Gelu_apprx_tanh).then_inc(tr_free[0], 1)
                        batch_end(c - 4)

                def batch_end(k):
                    act.wait_ge(s_unit, 4 * k + 4)
                    th = half_tanh[k % 2]
                    A(th, th, ACT.Sqrt, scale=-1.0).then_inc(s_sqrt, 1)
                    act.wait_ge(s_mixed, k + 1)
                    A(hhi[:, 4 * k:4 * k + 4, :], th.rearrange("p c d s -> p (c d) s")[:, 0:4, :],
                      ACT.Copy).then_inc(s_hhi, 1)

                def unit(i, pos):
                    if i < 2 or pos % 2:
                        return
                    u = 8 * (i - 2) + pos // 2
                    th = half_tanh[u // 4 % 2][:, u % 4]
                    act.wait_ge(s_gate, u + 1)
                    for d in range(2):
                        A(gates[:, d, 0, :], gates[:, d, 0, :], ACT.Sigmoid,
                          bias=sm["b_a"][:, 16 * d + u:16 * d + u + 1]).then_inc(s_sig, 1)
                        A(gates[:, d, 1, :], gates[:, d, 1, :], ACT.Sigmoid,
                          bias=sm["b_i"][:, 16 * d + u:16 * d + u + 1]).then_inc(s_ig, 1)
                    act.wait_ge(s_sig, 2 * u + 2)
                    if u >= 8:
                        act.wait_ge(s_hlo, u // 4 - 1)
                    for d in range(2):
                        A(th[:, d, :], gates[:, d, 0, :], ACT.Tanh,
                          scale=neg4sp[:, 16 * d + u:16 * d + u + 1]).then_inc(s_tanh, 1)
                act.wait_ge(s_lam, 1)
                act.wait_ge(rstd_ready, 3)
                run("rnn_in", evac, tail, unit)

            act.wait_ge(small_arrived, 16)
            A(lam_tmp[0], sm["lam"], ACT.Abs).then_inc(sem("lam_abs"), 1)
            act.wait_ge(sem("lam_abs"), 1)
            A(lam_tmp[0], lam_tmp[0], ACT.Exp, scale=-1.0).then_inc(sem("lam_exp"), 1)
            A(c_act, sm["c"], ACT.Silu).then_inc(sem("c_ready"), 1)
            act.wait_ge(x_arrived, 16)
            for t in range(T):
                ins = A(mid(t * D, D), x_[:, t * D:(t + 1) * D], ACT.Square, accum_out=ss[:, t, 0:1])
            ins.then_inc(sem("first_squares"), 1)
            root_of("first", 2)
            for q in range(4):
                group_hi(q % 2, q // 2, xhi[:, 4 * q:4 * q + 4, :], sm["g_mix0"][:, 4 * q:4 * q + 4], sem("first_hi"))
            for s in range(RING):
                splits[0] = s
                split(s)
            act.wait_ge(rstd_ready, 1)
            run("qkv", scaled_to("qkv", lambda i, b, t: qkv[:, t, 2 * i + b, :]))

            act.wait_ge(sem("qkv_out0"), 3)
            act.wait_ge(sem("qkv_out1"), 3)
            A(squares, qkv_h[:, :, 0:QH + KVH, :], ACT.Square).then_inc(s_sq, 1)
            act.wait_ge(sem("head_mean"), 1)
            A(rq, ssq, ACT.Sqrt).then_inc(s_rq, 1)
            for n, gi in enumerate((0, 2, 4)):
                act.wait_ge(s_qt, gi + 1)
                A(qk_t[:, 4 * gi:4 * gi + 4, :], [acc[0].rearrange("p t (h s) -> p (t h) s", s=S), tr[0],
                                                  acc[0].rearrange("p t (h s) -> p (t h) s", s=S)][n],
                  ACT.Copy).then_inc(s_qe_a, 1)

            def exps(u):
                act.wait_ge(s_nm, u + 1)
                after(act, s_pt, u - 1)
                for i in range(4):
                    n = 4 * u + i
                    ins = A(probs[:, u % 2, i, :], psum[:, 2 * (u % 2) + i // 2, (i % 2) * S:(i % 2 + 1) * S], ACT.Exp,
                            scale=rqs[:, n:n + 1], bias=nmx[:, n:n + 1], accum_out=sums[:, n:n + 1])
                ins.then_inc(s_exp, 1)

            def heads_hi(u):
                act.wait_ge(s_pv, u + 1)
                A(ohi[:, 2 * u:2 * u + 2, :], psum[:, 6 + u % 2, :].rearrange("p (h s) -> p h s", s=S),
                  ACT.Copy).then_inc(s_oh, 1)
            exps(0)
            for u in range(8):
                if u < 7:
                    exps(u + 1)
                if u:
                    heads_hi(u - 1)
                act.wait_ge(s_pt, u + 1)
                after(act, s_pv, u - 1)
                A(probs_t[:, u % 2, :, :, :].rearrange("p h k q -> p (h k q)"),
                  tr[0].rearrange("p c s -> p (c s)"), ACT.Copy).then_inc(s_pte, 1)
            heads_hi(7)
            residual("w_o")
            if has("ffn0"):
                gated("ffn0")
            if has("down0"):
                residual("down0")
            if has("rnn_in"):
                recurrent_in()
                residual("rnn_out")
            if has("ffn1"):
                gated("ffn1")
            if has("down1"):
                residual("down1")

            def token_norm(name, n_rstd, sh, gs):
                act.wait_ge(rstd_ready, n_rstd)
                A(normed[:, 0, :], x_[:, 0:D], ACT.Copy, scale=rstd[:, 0:1]).then_inc(sem(f"{name}_normed"), 1)
                for q in range(4):
                    b = q % 2
                    act.wait_ge(tr_ready[b], GROUP_AT[name][b] + q // 2 + 1)
                    for j in range(4):
                        c = 4 * q + j
                        ins = A(xhi[:, c, :], tr[b][:, j, :], ACT.Identity, scale=gs[:, c:c + 1], bias=sh[:, c:c + 1])
                    ins.then_inc(sem(f"{name}_hi"), 1)

            def project_in():
                def evac(i, b):
                    chunk_done("w_in", i, b)
                    c = 2 * i + b
                    A(proj[:, :, NW * c:NW * (c + 1)], acc[b], ACT.Copy).then_inc(sem(f"w_in_out{b}"), 1)

                def parameters(i, pos):
                    if (i, pos) == (0, 1):
                        A(st_tmp[0], sm["log_step"], ACT.Exp).then_inc(sem("dt_ready"), 1)
                    if (i, pos) == (0, 3):
                        act.wait_ge(sem("angle_ready"), 1)
                        A(st_tmp[4], st_tmp[3], ACT.Sin)
                        A(st_tmp[5], st_tmp[3], ACT.Sin, scale=0.5)
                        A(st_tmp[6], st_tmp[2], ACT.Tanh, scale=0.5).then_inc(sem("sines_ready"), 1)
                run("w_in", evac, None, parameters)
                for n in range(4):
                    splits[0] = TILE0["w_in_kv"] + RING + n
                    split(TILE0["w_in_kv"] + RING + n)
                act.wait_ge(tiles_used, TILE0["glu"])
                A(proj[:, :, D:D + 256], acc[0][:, :, 0:256], ACT.Copy).then_inc(sem("w_in_kv_out"), 1)

            def window_attention():
                for u in range(4):
                    act.wait_ge(sem("max2_ready"), u + 1)
                    for h in range(4):
                        for n, k in enumerate((slice(0, P), slice(P, 3 * P))):
                            c = 8 * u + 2 * h + n
                            A(masked[:, h, k], masked[:, h, k], ACT.Exp, bias=nm2[:, c:c + 1],
                              accum_out=sum2[:, c:c + 1])
                    A(m2[:, 8 * u:8 * u + 8], m2[:, 8 * u:8 * u + 8], ACT.Exp).then_inc(sem("exp2_ready"), 1)
                    act.wait_ge(sem("probs2_turned"), u + 1)
                    A(turned.rearrange("p h n q -> p (h n q)"), psum[:, 4:7, :].rearrange("p b e -> p (b e)"),
                      ACT.Copy).then_inc(sem("turned2_ready"), 1)

            def state_space():
                for q in range(8):
                    act.wait_ge(sem("skip_added"), q + 1)
                    A(z_t[:, q, :], z_t[:, q, :], ACT.Gelu_apprx_tanh).then_inc(sem("z_ready"), 1)
                act.wait_ge(sem("z_ready"), 8)
                act.wait_ge(sem("state_out"), 8)
                A(xhi[:, 0:8, :], z_t, ACT.Copy).then_inc(sem("z_hi_ready"), 1)

            def glu_and_merge():
                def evac(i, b):
                    chunk_done("glu", i, b)
                    A(tmp[:, b, :, :], acc[b], ACT.Sigmoid).then_inc(sem(f"glu_out{b}"), 1)
                run("glu", evac)
                act.wait_ge(sem("merged_ready"), 2)
                for t in range(T):
                    for half in range(2):
                        ins = A(mid((2 * t + half) * W2, W2), merged[:, t, half * W2:(half + 1) * W2], ACT.Square,
                                accum_out=mean[:, 2 * t + half:2 * t + half + 1])
                ins.then_inc(sem("merge_squares"), 1)
                root_of("merge", 4)
                act.wait_ge(rstd_ready, 6)
                for half in range(2):
                    m = merged[:, 0, half * W2:(half + 1) * W2]
                    A(m, m, ACT.Copy, scale=rstd[:, half:half + 1]).then_inc(sem("merge_scaled"), 1)
                for q in range(4):
                    group_hi(q % 2, GROUP_AT["merge"][q % 2] + q // 2, xhi[:, 4 * q:4 * q + 4, :],
                             sm["g_merged"][:, 4 * q:4 * q + 4], sem("merge_hi"))

            def gathered(layer):
                dst = GATHERED[layer]

                def evac(i, b):
                    chunk_done(layer, i, b)
                    n = 2 * i + b
                    after(act, sem(f"{layer}_out{b}"), i)
                    A(dst[:, :, n, :], acc[b], ACT.Copy)
                    for t in range(T):
                        ins = A(tmp[:, b, t, :], acc[b][:, t, :], ACT.Square, accum_out=ss[:, t, n:n + 1])
                    ins.then_inc(sem(f"{layer}_out{b}"), 1)
                run(layer, evac)
                root_of(layer, 2)

            def up_convolved():
                w = sm["conv2_w"].rearrange("p (k h n j) -> p k h n j", k=3, h=2, j=4)
                bias = sm["conv2_b"].rearrange("p (h n j) -> p h n j", h=2, j=4)
                flat = conv_.rearrange("p (h e) -> p h e", h=2)

                def evac(i, b):
                    chunk_done("ffn2", i, b)
                    after(act, tr_ready[b], i + GROUP_AT["ffn2"][b])
                    A(tmp[:, b, :, :], acc[b], ACT.Copy).then_inc(sem(f"ffn2_copied{b}"), 1)

                def base(i):
                    after(act, sem("ffn2_lo"), i)
                    for b in range(2):
                        act.wait_ge(tr_ready[b], i + (GROUP_AT["ffn2"][b] + 1))
                        for j in range(4):
                            ins = A(conv[:, 4 * b + j, :], tr[b][:, j, :], ACT.Identity, scale=w[:, 2, b, i, j:j + 1],
                                    bias=bias[:, b, i, j:j + 1])
                        ins.then_inc(sem("ffn2_base"), 1)

                def gelu(i):
                    act.wait_ge(tr_free[1], i + (GROUP_AT["ffn2"][1] + 1))
                    A(flat[:, 1, :], flat[:, 1, :], ACT.Gelu_apprx_tanh).then_inc(sem("ffn2_gelu"), 1)

                def hi(i):
                    act.wait_ge(sem("ffn2_prod"), i + 1)
                    A(mhi_.rearrange("p (n e) -> p n e", e=4 * S)[:, i, :], flat[:, 0, :], ACT.Copy).then_inc(sem("ffn2_hi"), 1)
                run("ffn2", evac, None, None, ((3, base), (6, gelu), (9, hi)))

            if has("w_in"):
                act.wait_ge(ada_ready, 1)
                token_norm("norm_mix", 5, sh_m, gs_m)
                project_in()
                window_attention()
                state_space()
                glu_and_merge()
                gathered("w_out")
                for t in range(T):
                    act.wait_ge(sem("x_mixed"), t + 1)
                    ins = A(mid(8192 + t * D, D), x_[:, t * D:(t + 1) * D], ACT.Square, accum_out=ss[:, t, 0:1])
                ins.then_inc(sem("x_squares"), 1)
                root_of("norm_ffn", 2)
                token_norm("norm_ffn", 8, sh_f, gs_f)
                up_convolved()
                gathered("down2")

        @block.vector
        def _(dve):
            V = nc.vector
            splits = [0]

            def split(tile):
                s = splits[0] % RING
                splits[0] += 1
                dve.wait_ge(hi_ready, tile + 1)
                V.tensor_tensor(wlo[:, s, :], raw[:, s, :], whi[:, s, :].bitcast(F32), ALU.subtract).then_inc(lo_ready, 1)

            def group_lo(b, dst_lo, dst_hi, g, signal, count):
                dve.wait_ge(signal, count)
                for j in range(4):
                    ins = V.scalar_tensor_tensor(dst_lo[:, j, :], tr[b][:, j, :], g[:, j:j + 1],
                                                 dst_hi[:, j, :].bitcast(F32), ALU.mult, ALU.subtract)
                ins.then_inc(tr_free[b], 1)

            def rstd_of(name, total, count, n=2):
                if total is not None:
                    ordered(dve, "vector")(total)
                V.tensor_scalar(mean[:, 0:n], mean[:, 0:n], 1.0 / (D if n == 2 else W2), EPS, ALU.mult,
                                ALU.add).then_inc(sem("mean_ready"), 1)
                dve.wait_ge(sem("root_ready"), NORM_AT[name])
                V.reciprocal(rstd[:, 0:n], root[:, 0:n]).then_inc(rstd_ready, 1)

            def ada_product(a, i, at):
                s = a % 2
                dve.wait_ge(ada_arrived[s], (i * 4 + (at * 4 + a // 2 + 1)) * 16)
                for k in range(KT):
                    w, c = araw[:, s, k, :], c_act[:, 2 * a + k:2 * a + k + 1]
                    if a == 0 and k == 0:
                        after(dve, ada_summed, i + at)
                        ins = V.tensor_scalar(adacc_, w, c, None, ALU.mult)
                    else:
                        dve.wait_ge(ada_step, i * 16 + (at * 16 + 2 * a + k))
                        ins = V.scalar_tensor_tensor(adacc_, w, c, adacc_, ALU.mult, ALU.add)
                    ins.then_inc(ada_step, 1)

            def ada_out(i, at):
                dve.wait_ge(ada_summed, i + (at + 1))
                cols = adat_.rearrange("p (n j) -> p n j", j=4)
                bias = sm["b_ada"].rearrange("p (n j) -> p n j", j=4)
                V.tensor_tensor(cols[:, i + at, :], psum[:, 6, 0:4], bias[:, i + at, :], ALU.add).then_inc(ada_done, 1)

            def run(layer, evac=None, tail=None, extra=None, late=()):
                kt = KTILES[layer]
                ada = ADA_AT.get(layer) if has("down1") else None

                def body(i, first):
                    splits[0] = TILE0[layer] + RING
                    for pos in range(2 * kt):
                        if not (layer == "down2" and not first and pos >= 2 * kt - RING):
                            split(i * (2 * kt) + (TILE0[layer] + pos + RING))
                        if extra:
                            extra(i, pos)
                        for at, step in late:
                            if at == pos and not first:
                                step(i - 1)
                        if ada is not None and pos in ADA_POS:
                            ada_product(pos - ADA_POS[0], i, ada)
                        if pos == HOOK and not first:
                            if tail:
                                tail(i - 1, 1)
                            if ada is not None:
                                ada_out(i - 1, ada)
                        if evac and pos == kt - 1:
                            evac(i, 0)
                        if tail and pos == kt + HOOK:
                            tail(i, 0)
                        if evac and pos == 2 * kt - 1:
                            evac(i, 1)
                each_pair(dve, layer, body)
                if tail:
                    tail(PAIRS[layer] - 1, 1)
                for _, step in late:
                    step(PAIRS[layer] - 1)
                if ada is not None:
                    ada_out(PAIRS[layer] - 1, ada)

            def chunk_done(layer, i, b):
                dve.wait_ge(tiles_used, i * (2 * KTILES[layer]) + (TILE0[layer] + (b + 1) * KTILES[layer]))

            def residual(layer, count):
                g = RESIDUAL[layer]

                def evac(i, b):
                    chunk_done(layer, i, b)
                    after(dve, sem(f"sum_used{b}"), i + 2 * RES_AT[layer])
                    V.tensor_tensor(tmp[:, b, :, :], acc[b], x[:, :, 2 * i + b, :], ALU.add).then_inc(
                        sem(f"sum_ready{b}"), 1)

                def tail(i, b):
                    if g:
                        c = 4 * (2 * i + b)
                        group_lo(b, xlo[:, c:c + 4, :], xhi[:, c:c + 4, :], sm[g][:, c:c + 4],
                                 sem("residual_hi"), 4 * RES_AT[layer] + 2 * i + b + 1)
                run(layer, evac, tail)
                for b in range(2):
                    dve.wait_ge(sem(f"sum_used{b}"), 2 * RES_AT[layer] + 2)
                rstd_of(layer, V.reduce_sum(mean[:, 0:T], ss, AX), count)

            def gated(layer):
                dve.wait_ge(rstd_ready, {"ffn0": 2, "ffn1": 4}[layer])

                def evac(i, b):
                    if not b:
                        return
                    chunk_done(layer, i, 1)
                    after(dve, tr_ready[0], i + GROUP_AT[layer][0])
                    dve.wait_ge(sem(f"{layer}_gate"), i + 1)
                    for t in range(T):
                        ins = V.scalar_tensor_tensor(tmp[:, 1, t, :], acc[1][:, t, :], rstd[:, t:t + 1],
                                                     tmp[:, 0, t, :], ALU.mult, ALU.mult)
                    ins.then_inc(sem(f"{layer}_prod"), 1)

                def tail(i, b):
                    if b:
                        dve.wait_ge(sem(f"{layer}_hi"), i + 1)
                        hi = mhi_.rearrange("p (n e) -> p n e", e=4 * S)[:, i, :]
                        lo = mlo_.rearrange("p (n e) -> p n e", e=4 * S)[:, i, :]
                        V.tensor_tensor(lo, tr[0].rearrange("p c s -> p (c s)"), hi.bitcast(F32),
                                        ALU.subtract).then_inc(tr_free[0], 1)
                run(layer, evac, tail)

            def softplus_of_lambda():
                link = ordered(dve, "vector")
                y, z, z2, poly = lam_tmp
                dve.wait_ge(sem("lam_exp"), 1)
                link(V.tensor_scalar(z, y, 2.0, None, ALU.add))
                link(V.reciprocal(z, z))
                link(V.tensor_tensor(z, z, y, ALU.mult))
                link(V.tensor_tensor(z2, z, z, ALU.mult))
                link(V.tensor_scalar(poly, z2, 1.0 / 17, 1.0 / 15, ALU.mult, ALU.add))
                for n in (13, 11, 9, 7, 5, 3, 1):
                    link(V.tensor_tensor(poly, poly, z2, ALU.mult))
                    link(V.tensor_scalar(poly, poly, 1.0 / n, None, ALU.add))
                link(V.tensor_tensor(poly, poly, z, ALU.mult))
                link(V.tensor_scalar(z, sm["lam"], -1.0, 0.0, ALU.mult, ALU.max))
                link(V.scalar_tensor_tensor(z, poly, 2.0, z, ALU.mult, ALU.add))
                V.tensor_scalar(neg4sp, z, -LRU_C / 2, None, ALU.mult).then_inc(s_lam, 1)

            def recurrent_in():
                def tail(i, b):
                    c = 2 * i + b
                    if c >= 4:
                        batch_end(c - 4)
                        return
                    dve.wait_ge(tr_ready[0], GROUP_AT["rnn_in"][0] + c + 1)
                    V.tensor_copy(xb[:, 4 * c:4 * c + 4, :], tr[0]).then_inc(tr_free[0], 1)
                    dve.wait_ge(tr_free[0], GROUP_AT["rnn_in"][0] + c + 1)
                    V.engine_nop().then_inc(s_xb, 1)
                    dve.wait_ge(s_base, c + 1)
                    for n, (tap, dst, src) in enumerate(((0, slice(2, S), slice(0, S - 2)), (1, slice(1, S), slice(0, S - 1)),
                                                         (3, slice(0, S - 1), slice(1, S)))):
                        for j in range(4 * c, 4 * c + 4):
                            ins = V.scalar_tensor_tensor(xc[:, j, dst], xb[:, j, src], sm["conv_w"][:, 16 * tap + j:16 * tap + j + 1],
                                                         xc[:, j, dst], ALU.mult, ALU.add)
                        ins.then_inc(s_conv, 1)
                        dve.wait_ge(s_conv, 3 * c + n + 1)

                link = ordered(dve, "vector")

                def unit(i, pos):
                    if i < 2 or pos % 2:
                        return
                    u = 8 * (i - 2) + pos // 2
                    k = u // 4 % 2
                    th, a, w = (v[k][:, u % 4] for v in (half_tanh, decay, drive))
                    dve.wait_ge(s_ig, 2 * u + 2)
                    dve.wait_ge(s_tanh, 2 * u + 2)
                    V.tensor_tensor(w, gates[:, :, 1, :], xc[:, u, :].unsqueeze(1).to_broadcast([P, 2, S]), ALU.mult).then_inc(s_drive, 1)
                    link(V.tensor_scalar(a, th, -1.0, 1.0, ALU.mult, ALU.add))
                    link(V.reciprocal(a, a))
                    dve.wait_ge(s_drive, u + 1)
                    link(V.scalar_tensor_tensor(w, w, 2.0, a, ALU.mult, ALU.mult))
                    V.scalar_tensor_tensor(a, th, 1.0, a, ALU.add, ALU.mult).then_inc(s_unit, 1)

                def batch_end(k):
                    th, a, w = (v[k % 2] for v in (half_tanh, decay, drive))
                    flat = lambda v: v.rearrange("p c d s -> p (c d s)")
                    dve.wait_ge(s_unit, 4 * k + 4)
                    dve.wait_ge(s_sqrt, k + 1)
                    link(V.tensor_tensor(flat(w), flat(w), flat(th), ALU.mult))
                    for c in range(4):
                        V.tensor_tensor_scan(w[:, c, 0, :], a[:, c, 0, :], w[:, c, 0, :], 0.0, ALU.mult, ALU.add)
                        ins = V.tensor_tensor_scan(w[:, c, 1, ::-1], a[:, c, 1, ::-1], w[:, c, 1, ::-1], 0.0, ALU.mult, ALU.add)
                    link(ins)
                    out_ = th.rearrange("p c d s -> p (c d) s")[:, 0:4, :]
                    link(V.tensor_tensor(out_, w[:, :, 0, :], w[:, :, 1, :], ALU.add))
                    dve.wait_ge(tr_free[0], GROUP_AT["rnn_in"][0] + 5 + k)
                    V.tensor_tensor(out_, out_, y_gelu[:, 4 * k:4 * k + 4, :], ALU.mult).then_inc(s_mixed, 1)
                    dve.wait_ge(s_hhi, k + 1)
                    V.tensor_tensor(hlo[:, 4 * k:4 * k + 4, :], out_, hhi[:, 4 * k:4 * k + 4, :].bitcast(F32),
                                    ALU.subtract).then_inc(s_hlo, 1)
                run("rnn_in", None, tail, unit)

            dve.wait_ge(sem("first_squares"), 1)
            rstd_of("first", V.tensor_copy(mean[:, 0:T], ss[:, :, 0]), 1)
            for q in range(4):
                group_lo(q % 2, xlo[:, 4 * q:4 * q + 4, :], xhi[:, 4 * q:4 * q + 4, :],
                         sm["g_mix0"][:, 4 * q:4 * q + 4], sem("first_hi"), q + 1)
            for s in range(RING):
                splits[0] = s
                split(s)
            if has("ffn0"):
                dve.wait_ge(sem("c_ready"), 1)
            dve.wait_ge(s_rope, 16)
            cos = rope[:, 0:128].rearrange("p (t a f) -> p t a f", t=T, a=2)
            sin = rope[:, 128:256].rearrange("p (t a f) -> p t a f", t=T, a=2)
            for k in range(2):
                gain = rope[:, 256 + 128 * k:384 + 128 * k].rearrange("p (a h f) -> p a h f", a=2, h=2)
                for t in range(T):
                    keep = tabs[:, 2 * k, t, :].rearrange("p (a h f) -> p a h f", a=2, h=2)
                    cross = tabs[:, 2 * k + 1, t, :].rearrange("p (a h f) -> p a h f", a=2, h=2)
                    for h in range(2):
                        V.tensor_tensor(keep[:, :, h, :], gain[:, :, h, :], cos[:, t], ALU.mult)
                        ins = V.scalar_tensor_tensor(cross[:, :, h, :], gain[:, :, 1 - h, :], 1.0 if h else -1.0,
                                                     sin[:, t], ALU.mult, ALU.mult)
                    ins.then_inc(sem("tabs_ready"), 1)
            softplus_of_lambda()
            run("qkv")
            dve.wait_ge(sem("tabs_ready"), 4)
            dve.wait_ge(sem("qkv_out0"), 3)
            dve.wait_ge(sem("qkv_out1"), 3)
            for t in range(T):
                for k, (a, n) in enumerate(((0, QH), (QH, KVH))):
                    src, out_, sw = qkv_h[:, t, a:a + n, :], rot[:, t, a:a + n, :], swapped[:, t, a:a + n, :]
                    V.tensor_tensor(out_, src, tabs[:, 2 * k, t, :].unsqueeze(1).to_broadcast([P, n, HEAD]), ALU.mult)
                    s5 = src.rearrange("p h (a z f) -> p h a z f", a=2, z=2)
                    w5 = sw.rearrange("p h (a z f) -> p h a z f", a=2, z=2)
                    c4 = tabs[:, 2 * k + 1, t, :].rearrange("p (a z f) -> p a z f", a=2, z=2)
                    for z in range(2):
                        ins = V.tensor_tensor(w5[:, :, :, z, :], s5[:, :, :, 1 - z, :],
                                              c4[:, :, z, :].unsqueeze(1).to_broadcast([P, n, 2, FREQS]), ALU.mult)
            link = ordered(dve, "vector")
            link(ins)
            link(V.tensor_tensor(rot, rot, swapped, ALU.add))
            dve.wait_ge(s_sq, 1)
            by_head = lambda ap: ap.rearrange("p (h t) -> p t h", t=T)
            link(V.reduce_sum(by_head(ssq), squares, AX))
            V.tensor_scalar(ssq, ssq, 1.0 / HEAD, EPS, ALU.mult, ALU.add).then_inc(sem("head_mean"), 1)
            dve.wait_ge(s_rq, 1)
            link(V.reciprocal(rq, rq))
            V.tensor_scalar(rqs, rq, HEAD ** -0.5, None, ALU.mult)
            for t in range(T):
                ins = V.tensor_tensor(rot[:, t, QH:, :], rot[:, t, QH:, :],
                                      by_head(rq)[:, t, QH:].unsqueeze(2).to_broadcast([P, KVH, HEAD]), ALU.mult)
            ins.then_inc(s_rot, 1)
            for n, gi in enumerate((1, 3)):
                dve.wait_ge(s_qt, gi + 1)
                V.tensor_copy(qk_t[:, 4 * gi:4 * gi + 4, :], [acc[1].rearrange("p t (h s) -> p (t h) s", s=S), tr[1]][n]).then_inc(s_qe_v, 1)

            def head_max(u):
                dve.wait_ge(s_sc, u + 1)
                b = 2 * (u % 2)
                link(V.tensor_reduce(mx[:, 4 * u:4 * u + 4], psum[:, b:b + 2, :].rearrange("p h (t k) -> p (h t) k", k=S), AX, ALU.max))
                V.scalar_tensor_tensor(nmx[:, 4 * u:4 * u + 4], mx[:, 4 * u:4 * u + 4], -1.0, rqs[:, 4 * u:4 * u + 4],
                                       ALU.mult, ALU.mult).then_inc(s_nm, 1)

            def heads_lo(u):
                dve.wait_ge(s_oh, u + 1)
                V.tensor_tensor(olo[:, 2 * u:2 * u + 2, :], psum[:, 6 + u % 2, :].rearrange("p (h s) -> p h s", s=S),
                                ohi[:, 2 * u:2 * u + 2, :].bitcast(F32), ALU.subtract).then_inc(s_ol, 1)
            head_max(0)
            for u in range(8):
                if u < 7:
                    head_max(u + 1)
                dve.wait_ge(s_exp, u + 1)
                link(V.reciprocal(rinv[:, 4 * u:4 * u + 4], sums[:, 4 * u:4 * u + 4]))
                V.tensor_tensor(probs[:, u % 2, :, :], probs[:, u % 2, :, :],
                                rinv[:, 4 * u:4 * u + 4].unsqueeze(2).to_broadcast([P, 4, S]), ALU.mult).then_inc(s_pn, 1)
                if u:
                    heads_lo(u - 1)
            heads_lo(7)
            residual("w_o", 2)
            if has("ffn0"):
                gated("ffn0")
            if has("down0"):
                residual("down0", 3)
            if has("rnn_in"):
                recurrent_in()
                residual("rnn_out", 4)
            if has("ffn1"):
                gated("ffn1")
            if has("down1"):
                residual("down1", 5)

            def ada_gains():
                dve.wait_ge(ada_done, ADA_CHUNKS)
                for at, g in ((1, "g_pre_mix"), (2, "g_post_mix"), (4, "g_pre_ffn"), (5, "g_post_ffn")):
                    v = adat_[:, 16 * at:16 * at + 16]
                    ins = V.scalar_tensor_tensor(v, v, 1.0, sm[g], ALU.add, ALU.mult)
                ins.then_inc(ada_ready, 1)
                dve.wait_ge(ada_ready, 1)

            def token_norm(name, n_rstd, sh, gs):
                dve.wait_ge(rstd_ready, n_rstd)
                V.tensor_scalar(normed[:, 1, :], x_[:, D:2 * D], rstd[:, 1:2], None, ALU.mult).then_inc(sem(f"{name}_normed"), 1)
                for q in range(4):
                    b = q % 2
                    dve.wait_ge(sem(f"{name}_hi"), q + 1)
                    for j in range(4):
                        c = 4 * q + j
                        ins = V.tensor_scalar(shifted[b][:, j, :], tr[b][:, j, :], gs[:, c:c + 1], sh[:, c:c + 1], ALU.mult, ALU.add)
                    ins.then_inc(sem(f"{name}_shifted"), 1)
                    dve.wait_ge(sem(f"{name}_shifted"), q + 1)
                    V.tensor_tensor(xlo[:, 4 * q:4 * q + 4, :], shifted[b], xhi[:, 4 * q:4 * q + 4, :].bitcast(F32),
                                    ALU.subtract).then_inc(tr_free[b], 1)

            def project_in():
                link = ordered(dve, "vector")
                lr, li = sm["lam_re"], sm["lam_im"]
                dt, ang, lrdt, red, sin_, half_, th, cos_, e, m, f_re, f_im, a1, a2, a3, den = st_tmp[:16]
                w_re, w_im, v_re, v_im = st_tmp[16:20]
                TWO_PI = [6.28125, 0.0019350051879882812, 3.019916050561733e-07]
                MAGIC = 1.5 * 2.0 ** 23

                def angles():
                    dve.wait_ge(sem("dt_ready"), 1)
                    link(V.tensor_tensor(lrdt, lr, dt, ALU.mult))
                    link(V.tensor_tensor(ang, li, dt, ALU.mult))
                    link(V.tensor_scalar(a1, ang, 1.0 / (2.0 * np.pi), MAGIC, ALU.mult, ALU.add))
                    link(V.tensor_scalar(a1, a1, MAGIC, None, ALU.subtract))
                    link(V.scalar_tensor_tensor(red, a1, -TWO_PI[0], ang, ALU.mult, ALU.add))
                    link(V.scalar_tensor_tensor(red, a1, -TWO_PI[1], red, ALU.mult, ALU.add))
                    link(V.scalar_tensor_tensor(red, a1, -TWO_PI[2], red, ALU.mult, ALU.add))
                    V.tensor_scalar(red, red, 3.1415925, -3.1415925, ALU.min, ALU.max).then_inc(sem("angle_ready"), 1)

                def factors():
                    dve.wait_ge(sem("sines_ready"), 1)
                    link(V.tensor_scalar(a1, th, -1.0, 1.0, ALU.mult, ALU.add))
                    link(V.reciprocal(a1, a1))
                    link(V.scalar_tensor_tensor(e, th, 2.0, a1, ALU.mult, ALU.mult))
                    link(V.tensor_scalar(m, e, 1.0, None, ALU.add))
                    link(V.tensor_tensor(a2, half_, half_, ALU.mult))
                    link(V.tensor_scalar(cos_, a2, -2.0, 1.0, ALU.mult, ALU.add))
                    link(V.scalar_tensor_tensor(a3, a2, -2.0, m, ALU.mult, ALU.mult))
                    link(V.tensor_tensor(e, e, a3, ALU.add))
                    link(V.tensor_tensor(a1, m, sin_, ALU.mult))
                    link(V.tensor_tensor(a2, lr, lr, ALU.mult))
                    link(V.tensor_tensor(a3, li, li, ALU.mult))
                    link(V.tensor_tensor(den, a2, a3, ALU.add))
                    link(V.reciprocal(den, den))

                def factors2():
                    link(V.tensor_tensor(a2, e, lr, ALU.mult))
                    link(V.tensor_tensor(a3, a1, li, ALU.mult))
                    link(V.tensor_tensor(f_re, a2, a3, ALU.add))
                    link(V.tensor_tensor(f_re, f_re, den, ALU.mult))
                    link(V.tensor_tensor(a2, a1, lr, ALU.mult))
                    link(V.tensor_tensor(a3, e, li, ALU.mult))
                    link(V.tensor_tensor(f_im, a2, a3, ALU.subtract))
                    link(V.tensor_tensor(f_im, f_im, den, ALU.mult))
                    link(V.tensor_copy(mag_keep, m))

                def input_matrix(part):
                    if part == 0:
                        dve.wait_ge(ssm_arrived, 16)
                        link(V.memset(mid(0, 2048), 0.0))
                        link(V.memset(mid(17408, 3072), 0.0))
                    f = [v.unsqueeze(2).to_broadcast([P, ST, GROUP]) for v in (f_re, f_im)]
                    t0, t1 = (by_tile(mid(2048 + 512 * i, 512), GROUP) for i in range(2))
                    link(V.tensor_tensor(t0, b_raw[part], f[0], ALU.mult))
                    link(V.tensor_tensor(t1, b_raw[1 - part], f[1], ALU.mult))
                    for g in range(2):
                        r = slice(64 * g, 64 * g + 64)
                        ins = V.tensor_tensor(bd[part][r, :, GROUP * g:GROUP * g + GROUP], t0[r], t1[r],
                                              ALU.add if part else ALU.subtract)
                    link(ins)
                    if part:
                        V.engine_nop().then_inc(sem("input_matrix"), 1)

                def output_matrix():
                    for g in range(2):
                        r, c = slice(64 * g, 64 * g + 64), slice(GROUP * g, GROUP * g + GROUP)
                        V.tensor_copy(c_re[r, :, c], c_raw[0][r])
                        V.tensor_scalar(nc_re[r, :, c], c_raw[0][r], -1.0, None, ALU.mult)
                        ins = V.tensor_scalar(nc_im[r, :, c], c_raw[1][r], -1.0, None, ALU.mult)
                    ins.then_inc(sem("output_matrix"), 1)

                def cmul(out_, a_, w_, n):
                    t_ = [by_tile(v[:, 0:ST * n], n) for v in cm_tmp]
                    wb = [v.unsqueeze(2).to_broadcast([P, ST, n]) for v in w_]
                    V.tensor_tensor(t_[0], a_[0], wb[0], ALU.mult)
                    V.tensor_tensor(t_[1], a_[1], wb[1], ALU.mult)
                    V.tensor_tensor(t_[2], a_[0], wb[1], ALU.mult)
                    link(V.tensor_tensor(t_[3], a_[1], wb[0], ALU.mult))
                    V.tensor_tensor(out_[0], t_[0], t_[1], ALU.subtract)
                    link(V.tensor_tensor(out_[1], t_[2], t_[3], ALU.add))

                def powers(step):
                    dst = e1 if step < 4 else e16
                    k = 1 << (step % 4)
                    one = lambda v: v.unsqueeze(2)
                    if step == 0:
                        V.tensor_copy(w_re, cos_)
                        link(V.tensor_copy(w_im, sin_))
                    if k == 1:
                        V.memset(dst[0][:, :, 0:1], 1.0)
                        link(V.memset(dst[1][:, :, 0:1], 0.0))
                    cmul([v[:, :, k:2 * k] for v in dst], [v[:, :, 0:k] for v in dst], (w_re, w_im), k)
                    if step < 7:
                        cmul([one(v_re), one(v_im)], [one(w_re), one(w_im)], (w_re, w_im), 1)
                        V.tensor_copy(w_re, v_re)
                        link(V.tensor_copy(w_im, v_im))
                    else:
                        V.engine_nop().then_inc(sem("e_ready"), 1)
                steps = {(0, 1): angles, (0, 3): factors, (0, 4): factors2, (0, 5): lambda: input_matrix(0),
                         (0, 6): lambda: input_matrix(1), (0, 8): output_matrix}
                for n in range(8):
                    steps[(0 if n < 4 else 1, (12 + n) if n < 4 else n - 2)] = lambda n=n: powers(n)
                w_in_steps = lambda i, pos: steps[(i, pos)]() if (i, pos) in steps else None

                def tail(i, b):
                    c = 2 * i + b
                    dve.wait_ge(tr_ready[b], GROUP_AT["w_in"][b] + i + 1)
                    dst = q2_t[:, 4 * c:4 * c + 4, :] if c < 2 else u_t[:, 4 * c - 8:4 * c - 4, :]
                    V.tensor_copy(dst, tr[b]).then_inc(tr_free[b], 1)
                return w_in_steps, tail

            if has("w_in"):
                ada_gains()
                token_norm("norm_mix", 5, sh_m, gs_m)
                extra, tail = project_in()
                run("w_in", None, None, extra)
                for n in range(4):
                    splits[0] = TILE0["w_in_kv"] + RING + n
                    split(TILE0["w_in_kv"] + RING + n)
                for b in range(2):
                    dve.wait_ge(tr_ready[b], GROUP_AT["ssm_b"][b] + 1)
                    V.tensor_copy(bb_t[b].rearrange("p c e -> p (c e)"), tr[b].rearrange("p c s -> p (c s)")).then_inc(tr_free[b], 1)
                for i in range(2):
                    for b in range(2):
                        tail(i, b)
                dve.wait_ge(tr_ready[0], GROUP_AT["w_in_k"][0] + 1)
                V.tensor_copy(k2_t, tr[0][:, 0, :]).then_inc(tr_free[0], 1)

                dve.wait_ge(mask_arrived, 16)
                dve.wait_ge(sem("w_in_kv_out"), 1)
                link = ordered(dve, "vector")
                for u in range(4):
                    dve.wait_ge(sem("scores2_ready"), u + 1)
                    if u:
                        dve.wait_ge(sem("probs2_turned"), u)
                    link(V.scalar_tensor_tensor(masked, psum[:, 0:4, 0:384], HEAD2 ** -0.5,
                                                mask.unsqueeze(1).to_broadcast([P, 4, 384]), ALU.mult, ALU.add))
                    c8 = slice(8 * u, 8 * u + 8)
                    pair = lambda v: v[:, c8].rearrange("p (h n) -> p h n", n=2)
                    V.tensor_reduce(pair(m2)[:, :, 0], masked[:, :, 0:P], AX, ALU.max)
                    link(V.tensor_reduce(pair(m2)[:, :, 1], masked[:, :, P:3 * P], AX, ALU.max))
                    sink = sm["sinks"][:, 4 * u:4 * u + 4].unsqueeze(2).to_broadcast([P, 4, 2])
                    link(V.tensor_tensor(pair(m2), pair(m2), sink, ALU.max))
                    link(V.tensor_scalar(nm2[:, c8], m2[:, c8], -1.0, None, ALU.mult))
                    V.tensor_tensor(pair(m2), pair(nm2), sink, ALU.add).then_inc(sem("max2_ready"), 1)
                    dve.wait_ge(sem("exp2_ready"), u + 1)
                    link(V.tensor_tensor(sum2[:, c8], sum2[:, c8], m2[:, c8], ALU.add))
                    link(V.reciprocal(rinv2[:, c8], sum2[:, c8]))
                    dve.wait_ge(sem("heads2_ready"), u + 1)
                    V.tensor_tensor(merged[:, :, 256 * u:256 * u + 256].rearrange("p t (h d) -> p h t d", d=HEAD2),
                                    psum[:, 7, :].rearrange("p (h t d) -> p h t d", h=4, t=T),
                                    pair(rinv2).unsqueeze(3).to_broadcast([P, 4, 2, HEAD2]), ALU.mult).then_inc(sem("attn2_out"), 1)
                dve.wait_ge(sem("attn2_out"), 4)
                V.engine_nop().then_inc(sem("attn2_done"), 1)

                link = ordered(dve, "vector")
                re_, im_ = (psum[:, 0:4, b * S:(b + 1) * S] for b in range(2))
                t0, t1 = (big(v) for v in rot_tmp)
                for q in range(8):
                    c_, s_ = big(cos_t[q % 2]), big(sin_t[q % 2])
                    dve.wait_ge(sem("tables_ready"), q + 1)
                    dve.wait_ge(sem("inputs_ready"), q + 1)
                    V.tensor_tensor(t0, re_, c_, ALU.mult)
                    link(V.tensor_tensor(t1, im_, s_, ALU.mult))
                    link(V.tensor_tensor(big(z_re), t0, t1, ALU.add))
                    V.tensor_tensor(t0, im_, c_, ALU.mult)
                    V.tensor_tensor(t1, re_, s_, ALU.mult).then_inc(sem("inputs_taken"), 1)
                    dve.wait_ge(sem("inputs_taken"), q + 1)
                    link(V.tensor_tensor(big(z_im), t0, t1, ALU.subtract))
                    for j in range(4):
                        decay_ = mag_keep[:, 4 * q + j:4 * q + j + 1].to_broadcast([P, S])
                        for z in (z_re, z_im):
                            v = z[:, j * S:(j + 1) * S]
                            ins = V.tensor_tensor_scan(v, decay_, v, 0.0, ALU.mult, ALU.add)
                    link(ins)
                    if q:
                        dve.wait_ge(sem("state_out"), q)
                    for n, (z, r_) in enumerate(((z_re, c_), (z_im, s_), (z_re, s_), (z_im, c_))):
                        ins = V.tensor_tensor(big(parts[n]), big(z), r_, ALU.mult)
                    ins.then_inc(sem("tables_used"), 1)
                    dve.wait_ge(sem("state_out"), q + 1)
                    V.scalar_tensor_tensor(z_t[:, q, :], u_t[:, q, :], sm["d_skip"][:, q:q + 1], psum[:, 4 + q % 2, 0:S],
                                           ALU.mult, ALU.add).then_inc(sem("skip_added"), 1)
                dve.wait_ge(sem("z_hi_ready"), 1)
                V.tensor_tensor(xlo[:, 0:8, :], z_t, xhi[:, 0:8, :].bitcast(F32), ALU.subtract).then_inc(sem("z_lo_ready"), 1)

                def glu_out(i, b):
                    dve.wait_ge(sem(f"glu_out{b}"), 1)
                    dve.wait_ge(tr_ready[b], GROUP_AT["glu"][b] + 1)
                    V.tensor_tensor(merged[:, :, W2 + NW * b:W2 + NW * (b + 1)], tmp[:, b, :, :],
                                    psum[:, 4 + 2 * b:6 + 2 * b, :], ALU.mult).then_inc(tr_free[b], 1)
                    dve.wait_ge(tr_free[b], GROUP_AT["glu"][b] + 1)
                    V.engine_nop().then_inc(sem("merged_ready"), 1)
                run("glu", glu_out)
                dve.wait_ge(sem("merge_squares"), 1)
                rstd_of("merge", None, 6, 4)
                dve.wait_ge(rstd_ready, 6)
                for half in range(2):
                    m_ = merged[:, 1, half * W2:(half + 1) * W2]
                    V.tensor_scalar(m_, m_, rstd[:, 2 + half:3 + half], None, ALU.mult).then_inc(sem("merge_scaled"), 1)
                for q in range(4):
                    group_lo(q % 2, xlo[:, 4 * q:4 * q + 4, :], xhi[:, 4 * q:4 * q + 4, :],
                             sm["g_merged"][:, 4 * q:4 * q + 4], sem("merge_hi"), q + 1)

                def gain_row(name, gain, diag, dst):
                    for c in range(FC):
                        ins = V.tensor_scalar(diag[:, c * P:(c + 1) * P], ident, gain[:, c:c + 1], None, ALU.mult)
                    ins.then_inc(sem(f"{name}_diagonal"), 1)
                    dve.wait_ge(sem(f"{name}_rows"), 1)
                    V.tensor_copy(dst, psum[:, 4:8, :].rearrange("p b e -> p (b e)")).then_inc(sem(f"{name}_gain"), 1)
                gain_row("w_out", gp_m, diag_mix, gain_mix)
                run("w_out")

                def post_norm(layer, count, gain, signal):
                    for b in range(2):
                        dve.wait_ge(sem(f"{layer}_out{b}"), 2)
                    rstd_of(layer, V.reduce_sum(mean[:, 0:T], ss, AX), count)
                    dve.wait_ge(rstd_ready, count)
                    dve.wait_ge(sem(f"{layer}_gain"), 1)
                    link = ordered(dve, "vector")
                    rows = GATHERED[layer].rearrange("p t n e -> p t (n e)")
                    for t in range(T):
                        link(V.scalar_tensor_tensor(rows[:, t, :], rows[:, t, :], rstd[:, t:t + 1], gain, ALU.mult, ALU.mult))
                        V.tensor_tensor(x_[:, t * D:(t + 1) * D], x_[:, t * D:(t + 1) * D], rows[:, t, :], ALU.add).then_inc(signal, 1)
                post_norm("w_out", 7, gain_mix, sem("x_mixed"))
                dve.wait_ge(sem("x_squares"), 1)
                rstd_of("norm_ffn", V.tensor_copy(mean[:, 0:T], ss[:, :, 0]), 8)
                token_norm("norm_ffn", 8, sh_f, gs_f)

                w = sm["conv2_w"].rearrange("p (k h n j) -> p k h n j", k=3, h=2, j=4)
                flat = conv_.rearrange("p (h e) -> p h e", h=2)

                def taps(i):
                    for b in range(2):
                        dve.wait_ge(sem("ffn2_base"), i * 2 + (b + 1))
                        for n, (k, by) in enumerate(((1, 1), (0, 2))):
                            for j in range(4):
                                dst = conv[:, 4 * b + j, by:S]
                                ins = V.scalar_tensor_tensor(dst, tr[b][:, j, 0:S - by], w[:, k, b, i, j:j + 1], dst, ALU.mult, ALU.add)
                            if n == 0:
                                ins.then_inc(sem("ffn2_tap"), 1)
                                dve.wait_ge(sem("ffn2_tap"), i * 2 + (b + 1))
                        ins.then_inc(tr_free[b], 1)

                def prod(i):
                    dve.wait_ge(sem("ffn2_gelu"), i + 1)
                    V.tensor_tensor(flat[:, 0, :], flat[:, 0, :], flat[:, 1, :], ALU.mult).then_inc(sem("ffn2_prod"), 1)

                def lo(i):
                    dve.wait_ge(sem("ffn2_hi"), i + 1)
                    V.tensor_tensor(mlo_.rearrange("p (n e) -> p n e", e=4 * S)[:, i, :], flat[:, 0, :],
                                    mhi_.rearrange("p (n e) -> p n e", e=4 * S)[:, i, :].bitcast(F32),
                                    ALU.subtract).then_inc(sem("ffn2_lo"), 1)
                run("ffn2", None, None, None, ((4, taps), (8, prod), (10, lo)))
                dve.wait_ge(sem("ffn2_lo"), 11)
                gain_row("down2", gp_f, diag_ff, gain_ff)
                run("down2")
                post_norm("down2", 9, gain_ff, sem("x_final"))
            if upto != "down2":
                for b in range(2):
                    dve.wait_ge(sem(f"sum_used{b}"), 2 * RES_AT[upto] + 2)
                V.engine_nop().then_inc(sem("x_final"), 1)

        @block.tensor
        def _(pe):
            M = nc.tensor.matmul
            slots = [0]

            def tile_products(layer, tile, b, k0, first, last, nk=KT, width=NW):
                hi, lo = LHS[layer]
                s = slots[0] % RING
                slots[0] += 1
                pe.wait_ge(lo_ready, tile + 1)
                for k in range(nk):
                    wh = whi[:, s, k * width:(k + 1) * width]
                    wl = wlo[:, s, k * width:(k + 1) * width]
                    for t in range(T):
                        xh, xl = (v[:, k0 + k, t * P:(t + 1) * P] for v in (hi, lo))
                        for n, (a, w) in enumerate(((xh, wh), (xh, wl), (xl, wh))):
                            ins = M(acc[b][:, t, 0:width], a, w, start=first and k == 0 and n == 0,
                                    stop=last and k == nk - 1 and n == 2)
                ins.then_inc(tiles_used, 1)

            def turn(b, before, src, signal=None):
                after(pe, tr_free[b], before)
                for j in range(4):
                    for t in range(T):
                        ins = nc.tensor.transpose(tr[b][:, j, t * P:(t + 1) * P], src(t, j), ident)
                ins.then_inc(tr_ready[b], 1)

            def ada_sum(i, at):
                pe.wait_ge(ada_step, i * 16 + (16 * at + 16))
                after(pe, ada_done, i + at)
                for j in range(4):
                    ins = M(psum[:, 6, j:j + 1], adacc_[:, j * P:(j + 1) * P], ones[:, 0:1], start=True, stop=True)
                ins.then_inc(ada_summed, 1)

            def run(layer, tail=None, extra=None):
                kt = KTILES[layer]
                ada = ADA_AT.get(layer) if has("down1") else None

                def body(i, first):
                    slots[0] = TILE0[layer]
                    for pos in range(2 * kt):
                        b, k = pos // kt, pos % kt
                        if extra:
                            extra(i, pos)
                        if pos == HOOK and not first:
                            if tail:
                                tail(i - 1, 1)
                            if ada is not None:
                                ada_sum(i - 1, ada)
                        if tail and pos == kt + HOOK:
                            tail(i, 0)
                        if k == 0:
                            after(pe, sem(released(layer, b)), i + 2 * RES_AT.get(layer, 0))
                        tile_products(layer, i * (2 * kt) + (TILE0[layer] + pos), b, KT * k, k == 0, k == kt - 1)
                each_pair(pe, layer, body)
                if tail:
                    tail(PAIRS[layer] - 1, 1)
                if ada is not None:
                    ada_sum(PAIRS[layer] - 1, ada)
                    pe.wait_ge(ada_done, ada + PAIRS[layer])

            def residual(layer):
                def tail(i, b):
                    pe.wait_ge(sem(f"sum_ready{b}"), i + (2 * RES_AT[layer] + 1))
                    turn(b, GROUP_AT[layer][b] + i, lambda t, j: tmp[:, b, t, j * P:(j + 1) * P])
                run(layer, tail if RESIDUAL[layer] else None)

            def gated(layer):
                def tail(i, b):
                    if b:
                        pe.wait_ge(sem(f"{layer}_prod"), i + 1)
                        turn(0, i + GROUP_AT[layer][0], lambda t, j: tmp[:, 1, t, j * P:(j + 1) * P])
                run(layer, tail)

            def input_ready(name, signal=None):
                for b in range(2):
                    n = GROUP_AT[name][b] + dict((g[0], g[1 + b]) for g in GROUPS)[name]
                    after(pe, tr_free[b], n)

            pe.wait_ge(small_arrived, 16)
            pe.wait_ge(ones_ready, 1)
            pe.wait_ge(x_arrived, 16)
            for q in range(4):
                turn(q % 2, q // 2, lambda t, j: x[:, t, q, j * P:(j + 1) * P])
            input_ready("first")
            run("qkv")
            pe.wait_ge(s_rot, 1)
            banks = [acc[0].rearrange("p t (h s) -> p (t h) s", s=S), acc[1].rearrange("p t (h s) -> p (t h) s", s=S),
                     tr[0], tr[1], acc[0].rearrange("p t (h s) -> p (t h) s", s=S)]
            for gi in range(5):
                if gi == 4:
                    pe.wait_ge(s_qe_a, 1)
                for j in range(4):
                    for t in range(T):
                        ins = nc.tensor.transpose(banks[gi][:, j, t * P:(t + 1) * P], rot[:, t, 4 * gi + j, :], ident)
                ins.then_inc(s_qt, 1)
            pe.wait_ge(s_qe_a, 3)
            pe.wait_ge(s_qe_v, 2)

            def scores(u):
                after(pe, s_exp, u - 1)
                for h in range(2):
                    for t in range(T):
                        ins = M(psum[:, 2 * (u % 2) + h, t * S:(t + 1) * S], qk_t[:, 2 * u + h, t * P:(t + 1) * P],
                                qk_t[:, QH + u // 2, :], start=True, stop=True)
                ins.then_inc(s_sc, 1)
            scores(0)
            for u in range(8):
                if u < 7:
                    scores(u + 1)
                pe.wait_ge(s_pn, u + 1)
                after(pe, s_pte, u)
                for h in range(2):
                    for k in range(T):
                        for t in range(T):
                            ins = nc.tensor.transpose(tr[0][:, 2 * h + k, t * P:(t + 1) * P],
                                                      probs[:, u % 2, 2 * h + t, k * P:(k + 1) * P], ident)
                ins.then_inc(s_pt, 1)
                pe.wait_ge(s_pte, u + 1)
                after(pe, s_ol, u - 1)
                for h in range(2):
                    for k in range(T):
                        ins = M(psum[:, 6 + u % 2, h * S:(h + 1) * S], qkv_h[:, k, QH + KVH + u // 2, :],
                                probs_t[:, u % 2, h, k, :], start=k == 0, stop=k == T - 1)
                ins.then_inc(s_pv, 1)
            pe.wait_ge(s_ol, 8)
            residual("w_o")
            if has("ffn0"):
                input_ready("w_o")
                gated("ffn0")
            if has("down0"):
                input_ready("ffn0")
                residual("down0")

            def recurrent_in():
                def tail(i, b):
                    c = 2 * i + b
                    pe.wait_ge(sem(f"rnn_in_out{b}"), i + 1)
                    turn(0, GROUP_AT["rnn_in"][0] + c, lambda t, j: tmp[:, b, t, j * P:(j + 1) * P])

                def unit(i, pos):
                    if i < 2 or pos % 2:
                        return
                    u = 8 * (i - 2) + pos // 2
                    blk, half = u // 2, u % 2
                    pe.wait_ge(gate_arrived[blk % 2], 16 * (blk // 2 + 1))
                    pe.wait_ge(s_conv, 3 * ((2 * blk + 1) // 4 + 1))
                    if u:
                        pe.wait_ge(s_drive, u)
                        pe.wait_ge(s_tanh, 2 * u)
                    for d in range(2):
                        for g in range(2):
                            for k in range(2):
                                ins = M(gates[:, d, g, :], gate_ws[blk % 2][:, k, d, g, half * P:(half + 1) * P],
                                        xc[:, 2 * blk + k, :], start=k == 0, stop=k == 1)
                    ins.then_inc(s_gate, 1)
                run("rnn_in", tail, unit)
            if has("rnn_in"):
                input_ready("down0")
                recurrent_in()
                pe.wait_ge(s_hlo, 4)
                residual("rnn_out")
            if has("ffn1"):
                input_ready("rnn_out")
                gated("ffn1")
            if has("down1"):
                input_ready("ffn1")
                residual("down1")

            def token_norm(name):
                pe.wait_ge(sem(f"{name}_normed"), 2)
                for q in range(4):
                    turn(q % 2, GROUP_AT[name][q % 2] + q // 2, lambda t, j: normed[:, t, (4 * q + j) * P:(4 * q + j + 1) * P])
                input_ready(name)

            def window_attention():
                for u in range(4):
                    if u:
                        pe.wait_ge(sem("max2_ready"), u)
                    for h in range(4):
                        pos = 4 * u + h
                        rows = slice(HEAD2 * (pos % 2), HEAD2 * (pos % 2) + HEAD2)
                        for t in range(T):
                            k = S if t else P
                            ins = M(psum[:, h, t * P:t * P + k], q2_t[rows, pos // 2, t * P:(t + 1) * P], k2_t[rows, 0:k],
                                    start=True, stop=True)
                    ins.then_inc(sem("scores2_ready"), 1)
                    pe.wait_ge(sem("exp2_ready"), u + 1)
                    flat = psum[:, 4:7, :].rearrange("p b (n q) -> p (b n) q", q=P)
                    for h in range(4):
                        for n in range(3):
                            ins = nc.tensor.transpose(flat[:, 3 * h + n, :], masked[:, h, n * P:(n + 1) * P], ident)
                    ins.then_inc(sem("probs2_turned"), 1)
                    pe.wait_ge(sem("turned2_ready"), u + 1)
                    after(pe, sem("attn2_out"), u)
                    for h in range(4):
                        kv = (4 * u + h) % 2
                        o = lambda t: psum[:, 7, (2 * h + t) * HEAD2:(2 * h + t + 1) * HEAD2]
                        v = lambda t: proj[:, t, D + P + HEAD2 * kv:D + P + HEAD2 * (kv + 1)]
                        M(o(0), turned[:, h, 0, :], v(0), start=True, stop=True)
                        M(o(1), turned[:, h, 1, :], v(0), start=True, stop=False)
                        ins = M(o(1), turned[:, h, 2, :], v(1), start=False, stop=True)
                    ins.then_inc(sem("heads2_ready"), 1)
                pe.wait_ge(sem("attn2_out"), 4)

            def state_space():
                def inputs(q):
                    after(pe, sem("inputs_taken"), q)
                    for b in range(2):
                        for j in range(4):
                            r = slice(32 * j, 32 * j + 32)
                            ins = M(psum[:, j, b * S:(b + 1) * S], bb_t[b][r, q, :], u_t[r, q, :], start=True, stop=True)
                    ins.then_inc(sem("inputs_ready"), 1)
                inputs(0)
                for q in range(8):
                    if q < 7:
                        inputs(q + 1)
                    pe.wait_ge(sem("tables_used"), q + 1)
                    after(pe, sem("skip_added"), q - 1)
                    for j in range(4):
                        for n, c_ in enumerate((c_re, nc_re, nc_im, nc_im)):
                            ins = M(psum[32 * j:32 * j + 32, 4 + q % 2, 0:S], c_[:, 4 * q + j, :], parts[n][:, j * S:(j + 1) * S],
                                    start=n == 0, stop=n == 3)
                    ins.then_inc(sem("state_out"), 1)
                pe.wait_ge(sem("skip_added"), 8)
                pe.wait_ge(sem("z_lo_ready"), 1)

            def gain_rows(name, diag):
                pe.wait_ge(sem(f"{name}_diagonal"), 1)
                for c in range(FC):
                    ins = M(psum[:, 4 + c // 4, (c % 4) * P:(c % 4 + 1) * P], ones, diag[:, c * P:(c + 1) * P], start=True, stop=True)
                ins.then_inc(sem(f"{name}_rows"), 1)

            if has("w_in"):
                token_norm("norm_mix")
                run("w_in")
                pe.wait_ge(sem("w_in_out0"), 2)
                for n in range(4):
                    slots[0] = n
                    tile_products("w_in_kv", TILE0["w_in_kv"] + n, 0, 4 * n, n == 0, n == 3, nk=4, width=256)
                pe.wait_ge(sem("input_matrix"), 1)
                for b in range(2):
                    after(pe, tr_free[b], GROUP_AT["ssm_b"][b])
                    for j in range(8):
                        ins = nc.tensor.transpose(tr[b].rearrange("p c s -> p (c s)")[:, j * P:(j + 1) * P],
                                                  bd[b].rearrange("p c e -> p (c e)")[:, j * P:(j + 1) * P], ident)
                    ins.then_inc(tr_ready[b], 1)
                pe.wait_ge(sem("e_ready"), 1)
                for i in range(2):
                    for b in range(2):
                        c = 2 * i + b
                        pe.wait_ge(sem(f"w_in_out{b}"), i + 1)
                        turn(b, GROUP_AT["w_in"][b] + i, lambda t, j: proj[:, t, NW * c + j * P:NW * c + (j + 1) * P])
                pe.wait_ge(sem("w_in_kv_out"), 1)
                pe.wait_ge(tr_free[0], GROUP_AT["w_in_k"][0])
                for t in range(T):
                    ins = nc.tensor.transpose(tr[0][:, 0, t * P:(t + 1) * P], proj[:, t, D:D + P], ident)
                ins.then_inc(tr_ready[0], 1)
                pe.wait_ge(tr_free[0], GROUP_AT["w_in_k"][0] + 1)
                pe.wait_ge(tr_free[1], GROUP_AT["w_in_k"][1])
                window_attention()
                state_space()
                run("glu")
                for b in range(2):
                    after(pe, tr_free[b], GROUP_AT["glu"][b])
                    for j in range(4):
                        for t in range(T):
                            ins = nc.tensor.transpose(psum[:, 4 + 2 * b + t, j * P:(j + 1) * P], z_t[:, 4 * b + j, t * P:(t + 1) * P], ident)
                    ins.then_inc(tr_ready[b], 1)
                pe.wait_ge(sem("merge_scaled"), 4)
                for q in range(4):
                    turn(q % 2, GROUP_AT["merge"][q % 2] + q // 2, lambda t, j: merged[:, t, (4 * q + j) * P:(4 * q + j + 1) * P])
                input_ready("merge")
                gain_rows("w_out", diag_mix)
                run("w_out")
                pe.wait_ge(sem("w_out_gain"), 1)
                token_norm("norm_ffn")

                def up_tail(i, b):
                    if b:
                        for v in range(2):
                            pe.wait_ge(sem(f"ffn2_copied{v}"), i + 1)
                            turn(v, i + GROUP_AT["ffn2"][v], lambda t, j: tmp[:, v, t, j * P:(j + 1) * P])
                run("ffn2", up_tail)
                input_ready("ffn2")
                gain_rows("down2", diag_ff)
                run("down2")
def _tiles(w):
    k, n = w.shape
    return w.reshape(k // (KT * P), KT, P, n // NW, NW).transpose(3, 0, 2, 1, 4).reshape(n // NW, k // (KT * P), P, TW)

def _cols(v):
    return v.reshape(-1, P).T

def _head_order(n, per):
    return np.arange(n * per).reshape(2, n // 2, per).transpose(1, 0, 2).reshape(-1)

def pack(**a):
    a = {k: np.asarray(v) for k, v in a.items()}
    flat = lambda w: w.reshape(-1, P, TW)
    both = lambda g, u: np.stack([_tiles(g), _tiles(u)], axis=1)
    order2 = _head_order(QH2, HEAD2)
    w_in = a["w_in_2"][0]
    w_in_qu = np.concatenate([w_in[:, :W2][:, order2], w_in[:, W2 + 256:]], axis=1)
    w_in_kv = w_in[:, W2:W2 + 256].reshape(4, 4, P, 256).transpose(0, 2, 1, 3)
    w_up = a["w_up_2"][0]
    stream = [_tiles(a["attn_w_qkv"][0]), _tiles(a["attn_w_o"][0]),
              both(a["ffn_w_gate"][0], a["ffn_w_up"][0]), _tiles(a["ffn_w_down"][0]),
              _tiles(a["rnn_w_in"][0]), _tiles(a["rnn_w_out"][0]),
              both(a["ffn_w_gate"][1], a["ffn_w_up"][1]), _tiles(a["ffn_w_down"][1]),
              _tiles(w_in_qu), w_in_kv, _tiles(a["w_glu_2"][0]),
              _tiles(np.concatenate([a["w_out_2"][0][:W2][order2], a["w_out_2"][0][W2:]])),
              both(w_up[:, :D_FF], w_up[:, D_FF:]), _tiles(a["w_down_2"][0])]
    weights = np.concatenate([flat(w) for w in stream])
    gates = np.stack([a["rnn_w_a"][0], a["rnn_w_i"][0]], axis=1)
    gates = gates.reshape(2, 2, RNN_BLOCKS, 2, P, RNN_W).transpose(2, 4, 3, 0, 1, 5).reshape(RNN_BLOCKS, P, 2048)
    by_state = lambda v: v.reshape(ST, P).T
    small = {"g_mix0": _cols(a["norm_mix"][0]), "g_mix1": _cols(a["norm_mix"][1]),
             "g_ffn0": _cols(a["norm_ffn"][0]), "g_ffn1": _cols(a["norm_ffn"][1]),
             "conv_w": _cols(a["rnn_conv_w"][0]), "conv_b": _cols(a["rnn_conv_b"][0]),
             "b_a": _cols(a["rnn_b_a"][0]), "b_i": _cols(a["rnn_b_i"][0]), "lam": _cols(a["rnn_lambda"][0]),
             "c": _cols(a["c_2"]), "b_ada": _cols(a["b_ada_2"][0]), "g_pre_mix": _cols(a["g_pre_mix_2"][0]),
             "g_post_mix": _cols(a["g_post_mix_2"][0]), "g_pre_ffn": _cols(a["g_pre_ffn_2"][0]),
             "g_post_ffn": _cols(a["g_post_ffn_2"][0]),
             "g_merged": _cols(np.concatenate([a["g_attn_out_2"][0][order2], a["g_ssm_out_2"][0]])),
             "d_skip": _cols(a["ssm_d_2"][0].reshape(-1)), "conv2_w": _cols(a["conv_w_2"][0]),
             "conv2_b": _cols(a["conv_b_2"][0]), "lam_re": by_state(a["lam_re_2"][0]),
             "lam_im": by_state(a["lam_im_2"][0]), "log_step": by_state(np.repeat(a["log_step_2"][0], STATE)),
             "sinks": np.broadcast_to(a["attn_sinks_2"][0][_head_order(QH2, 1)], (P, QH2)),
             "ident": np.eye(P, dtype=np.float32)}
    small = np.concatenate([small[k] for k, _ in SMALL], axis=1)
    pos = np.arange(S)
    freqs = np.float32(10000.0) ** (-np.arange(FREQS, dtype=np.float32) / np.float32(FREQS))
    ang = np.stack([(pos // 64).astype(np.float32)[:, None] * freqs, (pos % 64).astype(np.float32)[:, None] * freqs], axis=1)
    table = lambda f: f(ang).astype(np.float32).reshape(T, P, 64).transpose(1, 0, 2).reshape(P, 128)
    rope = np.concatenate([table(np.cos), table(np.sin), np.broadcast_to(a["attn_q_gain"][0], (P, HEAD)),
                           np.broadcast_to(a["attn_k_gain"][0], (P, HEAD))], axis=1)
    b = lambda v: v[0].reshape(ST, P, GROUP).transpose(1, 0, 2).reshape(P, -1)
    c = lambda v: v[0].transpose(0, 2, 1).reshape(ST, P, GROUP).transpose(1, 0, 2).reshape(P, -1)
    ssm = np.concatenate([b(a["ssm_b_re_2"]), b(a["ssm_b_im_2"]), c(a["ssm_c_re_2"]), c(a["ssm_c_im_2"])], axis=1)
    q, k = np.arange(P)[:, None], np.arange(S)[None, :]
    own = np.where(q >= k[:, :P], 0.0, NEG)
    band = np.where((k > q) & (k <= q + WINDOW), 0.0, NEG)
    mask = np.concatenate([own, band], axis=1).astype(np.float32)
    return {"x": a["x"][0], "weights": weights, "ada_w": flat(_tiles(a["w_ada_2"][0])), "gate_w": gates,
            "small": small, "rope": rope, "ssm": ssm, "mask": mask}


_INS = ("x", "weights", "ada_w", "gate_w", "small", "rope", "ssm", "mask")


def kernel(**inputs):
    import concourse.bacc as bacc
    from concourse.bass_utils import run_bass_kernel_spmd

    arrays = {k: np.ascontiguousarray(v) for k, v in pack(**inputs).items()}
    nc = bacc.Bacc("TRN2", target_bir_lowering=False, num_devices=1)
    args = [nc.dram_tensor(k, arrays[k].shape, mybir.dt.from_np(arrays[k].dtype), kind="ExternalInput").ap() for k in _INS]
    out = nc.dram_tensor("out_0", (S, D), F32, kind="ExternalOutput").ap()
    build(nc, *args, out)
    r = run_bass_kernel_spmd(nc, [arrays], core_ids=[0])
    return r.results[0]["out_0"].reshape(1, S, D)
```

```python
from contextlib import ExitStack

import numpy as np
import concourse.bass as bass
from concourse import mybir

F32 = mybir.dt.float32
F32R = mybir.dt.float32r
ACT = mybir.ActivationFunctionType
ALU = mybir.AluOpType
AX = mybir.AxisListType.X

P = 128
D = 2048
S = 256
T = S // P
FC = D // P
NW = 512
KT = 2
TW = KT * NW
RING = 4
D_FF = 5632
FFC = D_FF // P
EPS = 1e-6
HEAD = 128
QH, KVH = 16, 4
FREQS = 32
RNN_BLOCKS, RNN_W = 8, 256
HALF = 2
LRU_C = 8.0
HEAD2 = 64
QH2, KVH2 = 16, 2
W2 = 1024
WINDOW = 128
GROUP, STATE = 16, 64
ST = 32
ADA_CHUNKS = 6 * D // NW
NEG = -1e30

LAYERS = [("qkv", 3, 8), ("w_o", 2, 8), ("ffn0", 11, 8), ("down0", 2, 22), ("rnn_in", 4, 8),
          ("rnn_out", 2, 8), ("ffn1", 11, 8), ("down1", 2, 22), ("w_in", 2, 8), ("w_in_kv", 0, 4),
          ("glu", 1, 4), ("w_out", 2, 8), ("ffn2", 11, 8), ("down2", 2, 22)]
TILE0, CHUNK0, CHUNK1 = {}, {}, {}
_n = _e = _o = 0
for _name, _pairs, _kt in LAYERS:
    TILE0[_name], CHUNK0[_name], CHUNK1[_name] = _n, _e, _o
    _n += max(1, 2 * _pairs) * _kt
    _e += max(1, _pairs)
    _o += _pairs
TILES = _n
PAIRS = {a: b for a, b, _ in LAYERS}
KTILES = {a: c for a, _, c in LAYERS}
GROUPS = [("first", 2, 2), ("w_o", 4, 0), ("ffn0", 11, 0), ("down0", 4, 0), ("rnn_in", 8, 0),
          ("rnn_out", 4, 0), ("ffn1", 11, 0), ("ssm_b", 2, 0), ("norm_mix", 2, 2), ("w_in", 8, 0),
          ("w_in_k", 1, 0), ("glu", 1, 1), ("merge", 2, 2), ("norm_ffn", 2, 2), ("ffn2", 11, 11)]
GROUP_AT = {}
_a = _b = 0
for _name, _x, _y in GROUPS:
    GROUP_AT[_name] = (_a, _b)
    _a, _b = _a + _x, _b + _y

NORM_AT = {name: n + 1 for n, name in enumerate(
    ("first", "w_o", "down0", "rnn_out", "down1", "merge", "w_out", "norm_ffn", "down2"))}
PARAMETER_STEPS = {"angle_ready": 1, "input_matrix": 2, "output_matrix": 3, "e_ready": 4}
SETUP_STEPS = {"lam_abs": 1, "lam_exp": 2, "c_ready": 3, "dt_ready": 4, "sines_ready": 5}
RES_AT = {name: n for n, name in enumerate(("w_o", "down0", "rnn_out", "down1"))}

SMALL = [("g_mix0", 16), ("g_mix1", 16), ("g_ffn0", 16), ("g_ffn1", 16), ("conv_w", 64),
         ("conv_b", 16), ("b_a", 32), ("b_i", 32), ("lam", 32), ("c", 16), ("b_ada", 96),
         ("g_pre_mix", 16), ("g_post_mix", 16), ("g_pre_ffn", 16), ("g_post_ffn", 16),
         ("g_merged", 16), ("d_skip", 8), ("conv2_w", 264), ("conv2_b", 88), ("lam_re", 32),
         ("lam_im", 32), ("log_step", 32), ("sinks", 16), ("ident", 128)]
SMALL_AT = {}
_n = 0
for _name, _w in SMALL:
    SMALL_AT[_name] = (_n, _w)
    _n += _w
NSMALL = _n
HOOK = 3
CARRIED_AT = {"w_o": HOOK, "ffn0": HOOK, "down0": HOOK, "rnn_in": 1, "rnn_out": HOOK, "ffn1": HOOK}


def build(nc, x_in, weights, ada_w, gate_w, small_in, rope_in, ssm_in, mask_in, out, upto="down2"):
    names = [a for a, _, _ in LAYERS]
    order = names.index(upto)
    has = lambda name: names.index(name) <= order
    n_tiles = TILES if upto == "down2" else TILE0[upto] + max(1, 2 * PAIRS[upto]) * KTILES[upto] + RING
    ctx = ExitStack()
    with ctx:
        sems = {}

        def sem(name):
            if name not in sems:
                sems[name] = ctx.enter_context(nc.semaphore(name))
            return sems[name]

        cursor = [16512]

        def place(name, cols, dt=F32, at=None):
            if at is None:
                at = cursor[0]
                cursor[0] += 4 * cols
            return nc.alloc_sbuf_tensor_at(name, [P, cols], dt, offset=at)[:, :], at

        def shaped(ap, pattern, **kw):
            return ap.rearrange(pattern, **kw)

        raw_, _ = place("raw", RING * TW)
        whi_, _ = place("w_hi", RING * TW, F32R)
        wlo_, _ = place("w_lo", RING * TW, F32R)
        x_, _ = place("x_tok", T * D)
        _, xt_at = place("xt_region", 2 * FC * S)
        xhi_, _ = place("xt_hi", FC * S, F32R, at=xt_at)
        xlo_, _ = place("xt_lo", FC * S, F32R, at=xt_at + 4 * FC * S)
        sc_, _ = place("scratch", 2 * FC * S, at=xt_at)
        _, mid_at = place("mid_region", 2 * FFC * S)
        mhi_, _ = place("mid_hi", FFC * S, F32R, at=mid_at)
        mlo_, _ = place("mid_lo", FFC * S, F32R, at=mid_at + 4 * FFC * S)
        mid_, _ = place("mid", 2 * FFC * S, at=mid_at)
        tmp_, _ = place("tmp", 2 * T * NW)
        small_, _ = place("small", NSMALL)
        ones_, _ = place("ones", P)
        adacc_, ada_at = place("ada_acc", NW)
        araw_, araw_at = place("ada_raw", 2 * TW)
        conv_, _ = place("conv_buf", 4 * 2 * S, at=ada_at)
        adat_, _ = place("ada_t", 96)
        stat_, _ = place("stat", 48)
        assert cursor[0] <= 229344, cursor

        raw = shaped(raw_, "p (r e) -> p r e", r=RING)
        whi = shaped(whi_, "p (r e) -> p r e", r=RING)
        wlo = shaped(wlo_, "p (r e) -> p r e", r=RING)
        x = shaped(x_, "p (t n e) -> p t n e", t=T, e=NW)
        xhi = shaped(xhi_, "p (c s) -> p c s", s=S)
        xlo = shaped(xlo_, "p (c s) -> p c s", s=S)
        mhi = shaped(mhi_, "p (c s) -> p c s", s=S)
        mlo = shaped(mlo_, "p (c s) -> p c s", s=S)
        tmp = shaped(tmp_, "p (b t e) -> p b t e", b=2, t=T)
        araw = shaped(araw_, "p (r k e) -> p r k e", r=2, k=KT)
        conv = shaped(conv_, "p (c s) -> p c s", s=S)
        sm = {k: small_[:, a:a + w] for k, (a, w) in SMALL_AT.items()}
        ident = sm["ident"]
        ones = ones_
        ss = stat_[:, 0:8].rearrange("p (t n) -> p t n", t=T)
        mean = stat_[:, 8:12]
        root = stat_[:, 12:16]
        rstd = stat_[:, 16:20]
        c_act = stat_[:, 20:36]
        mid = lambda a, n: mid_[:, a:a + n]
        scr = lambda a, n: sc_[:, a:a + n]

        psum = nc.alloc_psum_tensor("psum", [P, 8, NW], F32)
        acc = [psum[:, 2 * b:2 * b + 2, :] for b in range(2)]
        tr = [psum[:, 4 + 2 * b:6 + 2 * b, :].rearrange("p b (c s) -> p (b c) s", s=S) for b in range(2)]

        raw_arrived = [sem(f"raw_arrived{s}") for s in range(RING)]
        hi_ready, lo_ready, tiles_used = sem("hi_ready"), sem("lo_ready"), sem("tiles_used")
        tr_ready = [sem("tr_ready0"), sem("tr_ready1")]
        tr_free = [sem("tr_free0"), sem("tr_free1")]
        small_arrived, x_arrived, stored = sem("small_arrived"), sem("x_arrived"), sem("stored")
        ones_ready = sem("ones_ready")
        ada_arrived = [sem("ada_arrived0"), sem("ada_arrived1")]
        ada_used, ada_step = sem("ada_used"), sem("ada_step")
        ada_summed, ada_reduced = sem("ada_summed"), sem("ada_reduced")
        ada_done = sem("ada_done")
        rstd_ready = sem("rstd_ready")


        def after(eng, what, value):
            if not isinstance(value, int) or value > 0:
                eng.wait_ge(what, value)

        steps_taken = {"vector": 0, "gpsimd": 0}

        def ordered(eng, name):
            what = sem(f"{name}_steps")

            def link(instruction):
                steps_taken[name] += 1
                instruction.then_inc(what, 1)
                eng.wait_ge(what, steps_taken[name])
            return link

        def each_pair(eng, layer, body):
            n = PAIRS[layer]
            if layer == "rnn_in":
                for i in range(n):
                    body(i, i == 0)
                return
            body(0, True)
            if n == 2:
                body(1, False)
            elif n > 2:
                with eng.Fori(1, n) as i:
                    body(i, False)

        ADA_AT = {"ffn0": 0, "rnn_out": 11, "ffn1": 13}
        ADA_POS = range(4, 12)

        qkv = mid(0, 6144).rearrange("p (t n e) -> p t n e", t=T, e=NW)
        qkv_h = mid(0, 6144).rearrange("p (t h d) -> p t h d", t=T, d=HEAD)
        rope = mid(6144, 512)
        tabs = mid(6656, 1024).rearrange("p (k t d) -> p k t d", k=4, t=T)
        rot = mid(7680, 5120).rearrange("p (t h d) -> p t h d", t=T, d=HEAD)
        swapped = mid(12800, 5120).rearrange("p (t h d) -> p t h d", t=T, d=HEAD)
        qk_t = mid(12800, 5120).rearrange("p (h s) -> p h s", s=S)
        ohi_, _ = place("o_hi", FC * S, F32R, at=mid_at + 4 * 7680)
        olo_, _ = place("o_lo", FC * S, F32R, at=mid_at + 4 * 17920)
        ohi = shaped(ohi_, "p (c s) -> p c s", s=S)
        olo = shaped(olo_, "p (c s) -> p c s", s=S)
        squares = scr(0, 5120).rearrange("p (t h d) -> p t h d", t=T, d=HEAD)
        probs = scr(6144, 2048).rearrange("p (b i k) -> p b i k", b=2, k=S)
        probs_t = scr(0, 2048).rearrange("p (b h k q) -> p b h k q", b=2, h=2, k=T)
        ssq = mid(22016, 40)
        rq = mid(22016 + 40, 40)
        rqs = mid(22016 + 80, 40)
        mx = mid(22016 + 120, 32)
        nmx = mid(22016 + 152, 32)
        sums = mid(22016 + 184, 32)
        rinv = mid(22016 + 216, 32)
        s_rot, s_sq, s_rq = sem("rotated"), sem("squares_ready"), sem("head_root")
        s_qt, s_qe_a, s_qe_v = sem("qk_transposed"), sem("qk_out_act"), sem("qk_out_dve")
        s_sc, s_nm, s_exp, s_pn = sem("scores_ready"), sem("max_ready"), sem("exp_ready"), sem("probs_ready")
        s_pt, s_pte, s_pv, s_oh, s_ol = (sem("probs_turned"), sem("probs_t_ready"), sem("heads_ready"),
                                         sem("o_hi_ready"), sem("o_lo_ready"))
        s_rope = sem("rope_arrived")

        xb = mid(0, 4096).rearrange("p (c s) -> p c s", s=S)
        y_gelu = mid(4096, 4096).rearrange("p (c s) -> p c s", s=S)
        xc = mid(8192, 4096).rearrange("p (c s) -> p c s", s=S)
        hhi_, _ = place("h_hi", FC * S, F32R, at=mid_at + 4 * 8192)
        hlo_, _ = place("h_lo", FC * S, F32R, at=mid_at + 4 * 4096)
        hhi = shaped(hhi_, "p (c s) -> p c s", s=S)
        hlo = shaped(hlo_, "p (c s) -> p c s", s=S)
        of_batch = lambda at: mid(at, 2048).rearrange("p (c d s) -> p c d s", d=2, s=S)
        half_tanh = [of_batch(12288), of_batch(0)]
        decay = [of_batch(14336), of_batch(18432)]
        drive = [of_batch(16384), of_batch(2048)]
        gw_shape = lambda ap: ap.rearrange("p (k d g j) -> p k d g j", k=2, d=2, g=2)
        gate_ws = [gw_shape(mid(20480, 2048)), gw_shape(araw_)]
        gates = psum[:, 6:8, :].rearrange("p d (g s) -> p d g s", g=2)
        lam_tmp = [mid(22016 + 32 * i, 32) for i in range(4)]
        neg4sp = sm["lam"]
        gate_arrived = [sem("gate_w_arrived0"), sem("gate_w_arrived1")]
        s_xb, s_base, s_conv, s_y = sem("xb_ready"), sem("conv_base"), sem("conv_ready"), sem("y_ready")
        s_gate, s_sig, s_tanh, s_ig, s_drive = (sem("gates_summed"), sem("r_ready"), sem("tanh_ready"),
                                                sem("i_ready"), sem("drive_started"))
        s_unit, s_sqrt, s_mixed, s_hhi, s_hlo = (sem("unit_ready"), sem("sqrt_ready"), sem("mixed_ready"),
                                                 sem("h_hi_ready"), sem("h_lo_ready"))
        s_decay, s_below, s_scaled, s_scan = (sem("decay_ready"), sem("below_one"), sem("drive_scaled"),
                                              sem("batch_scanned"))
        s_lam = sem("lambda_ready")
        BATCH_AT = {"root": 8, "scan": 11, "hi": 14, "lo": 15}
        LAST_BATCH_AT = {"scan": 2, "hi": 4, "lo": 5}
        UNITS = 16

        UNITS2 = ST // 2
        by_tile = lambda ap, e: ap.rearrange("p (c e) -> p c e", e=e)
        q2_t, k2_t, u_t = by_tile(mid(0, 2048), S), mid(2048, S), by_tile(mid(2816, 2048), S)
        kv = mid(2304, 512).rearrange("p (t e) -> p t e", t=T)
        z_t = u_t
        merged = mid(4864, 4096).rearrange("p (t e) -> p t e", t=T)
        bb_t = [by_tile(mid(8960 + 1024 * i, 1024), P) for i in range(2)]
        c_re, nc_im = (by_tile(mid(11008 + 1024 * i, 1024), 2 * GROUP) for i in range(2))
        tables = [mid(13056 + 1024 * i, 1024).rearrange("p (f c s) -> p f c s", f=2, s=S) for i in range(4)]
        unit_bufs = [[by_tile(mid(17152 + 2048 * i + 512 * n, 512), S) for n in range(4)]
                     + [by_tile(merged[:, i, W2 + 512 * n:W2 + 512 * n + 512], S) for n in range(2)] for i in range(2)]
        normed = mid(17152, 4096).rearrange("p (t e) -> p t e", t=T)
        shifted = [by_tile(mid(4864 + 1024 * i, 1024), S) for i in range(2)]
        m2, nm2, sum2, rinv2 = (mid(21248 + 32 * i, 32) for i in range(4))
        squares_out = mid(8960, 4096)
        ssm_raw = scr(0, 2048)
        b_raw = [by_tile(scr(512 * i, 512), GROUP) for i in range(2)]
        c_raw = [by_tile(scr(1024 + 512 * i, 512), GROUP) for i in range(2)]
        bd = [by_tile(scr(2048 + 1024 * i, 1024), 2 * GROUP) for i in range(2)]
        c_made = bd
        bb_made = scr(5120, 2048)
        e1 = [by_tile(scr(512 * i, 512), 16) for i in range(2)]
        e16 = [by_tile(scr(1024 + 512 * i, 512), 16) for i in range(2)]
        cm_tmp = [scr(4096 + 256 * i, 256) for i in range(4)]
        table_out = [scr(2048 + 1024 * i, 1024) for i in range(2)]
        table_tmp = scr(4096, 512)
        st_tmp = [scr(7168 + 32 * i, 32) for i in range(32)]
        mag_keep = sm["lam_re"]
        mask = conv_[:, 0:384]
        masked = [conv_[:, 384 + 768 * i:1152 + 768 * i].rearrange("p (h k) -> p h k", k=384) for i in range(2)]
        turned = [tmp_[:, 768 * i:768 * i + 768].rearrange("p (h n q) -> p h n q", h=2, n=3) for i in range(2)]
        mixed = mid(0, 4096).rearrange("p (t n e) -> p t n e", t=T, e=NW)
        mixed_ff = scr(0, 4096).rearrange("p (t n e) -> p t n e", t=T, e=NW)
        gain_mix, gain_ff = mid(13056, D), scr(4096, D)
        diag_mix, diag_ff = mid(15104, D), conv_
        sh_m, gs_m, gp_m, sh_f, gs_f, gp_f = (adat_[:, 16 * i:16 * i + 16] for i in range(6))
        ssm_arrived, mask_arrived, ada_ready = sem("ssm_arrived"), sem("mask_arrived"), sem("ada_gains")
        table_store = nc.dram_tensor("table_store", [UNITS2, P, 1024], F32, kind="Internal").ap()
        matrix_store = nc.dram_tensor("matrix_store", [2, P, 2048], F32, kind="Internal").ap()
        table_arrived = [sem(f"table_arrived{i}") for i in range(4)]
        STREAM_UNITS = {(0, 14): 0, (1, 2): 1, (1, 6): 2, (1, 10): 3, (1, 14): 4}
        TURN_AT = (HOOK, HOOK + 3)
        Y_BANK = [4, 4] + [4 + (q + 1) % 2 for q in range(2, 8)]

        LHS = {"qkv": (xhi, xlo), "w_o": (ohi, olo), "ffn0": (xhi, xlo), "down0": (mhi, mlo),
               "rnn_in": (xhi, xlo), "rnn_out": (hhi, hlo), "ffn1": (xhi, xlo), "down1": (mhi, mlo), "w_in": (xhi, xlo),
               "w_in_kv": (xhi, xlo), "glu": (xhi, xlo), "w_out": (xhi, xlo), "ffn2": (xhi, xlo),
               "down2": (mhi, mlo)}
        RESIDUAL = {"w_o": "g_ffn0", "down0": "g_mix1", "rnn_out": "g_ffn1", "down1": None}
        GATHERED = {"w_out": mixed, "down2": mixed_ff}
        GATED = ("ffn0", "ffn1")

        def released(layer, b):
            if layer in RESIDUAL:
                return f"sum_ready{b}"
            if layer == "ffn2":
                return f"ffn2_copied{b}"
            return f"{layer}_{('gate', 'prod')[b]}" if layer in GATED else f"{layer}_out{b}"

        block = ctx.enter_context(nc.Block())

        @block.sync
        def _(sp):
            sp.dma_start(small_, small_in).then_inc(small_arrived, 16)
            sp.dma_start(x_.rearrange("p (t e) -> p t e", t=T),
                         x_in.rearrange("(t p) e -> p t e", p=P)).then_inc(x_arrived, 16)
            for s in range(RING):
                sp.dma_start(raw[:, s, :], weights[s]).then_inc(raw_arrived[s], 16)
            sp.dma_start(rope, rope_in).then_inc(s_rope, 16)
            with sp.Fori(1, n_tiles // RING) as i:
                for s in range(RING):
                    sp.wait_ge(lo_ready, i * RING + (s - 3))
                    sp.dma_start(raw[:, s, :], weights[i * RING + s]).then_inc(raw_arrived[s], 16)

        def finish(pool):
            pool.wait_ge(sem("x_final"), 2 if upto == "down2" else 1)
            pool.dma_start(out.rearrange("(t p) e -> p t e", p=P),
                           x_.rearrange("p (t e) -> p t e", t=T)).then_inc(stored, 16)
            pool.wait_ge(stored, 16)

        @block.gpsimd
        def _(pool):
            nc.gpsimd.memset(ones, 1.0).then_inc(ones_ready, 1)
            if has("down1"):
                for s in range(2):
                    pool.dma_start(araw_[:, s * TW:(s + 1) * TW], ada_w[s]).then_inc(ada_arrived[s], 16)

                def ada_tiles(i):
                    for s in range(2):
                        pool.wait_ge(ada_step, i * 4 + (2 * s - 2))
                        pool.dma_start(araw_[:, s * TW:(s + 1) * TW], ada_w[i * 2 + s]).then_inc(ada_arrived[s], 16)
                with pool.Fori(1, 11 * 4) as i:
                    ada_tiles(i)
            def batch_before_scan(k):
                pool.wait_ge(s_sqrt, k + 1)
                nc.gpsimd.tensor_tensor(drive[k % 2], drive[k % 2], half_tanh[k % 2], ALU.mult).then_inc(s_scaled, 1)

            def batch_after_scan(k):
                w, th = drive[k % 2], half_tanh[k % 2]
                out_ = th.rearrange("p c d s -> p (c d) s")[:, 0:4, :]
                pool.wait_ge(s_scan, k + 1)
                ordered(pool, "gpsimd")(nc.gpsimd.tensor_tensor(out_, w[:, :, 0, :], w[:, :, 1, :], ALU.add))
                pool.wait_ge(tr_free[0], GROUP_AT["rnn_in"][0] + 5 + k)
                nc.gpsimd.tensor_tensor(out_, out_, y_gelu[:, 4 * k:4 * k + 4, :], ALU.mult).then_inc(s_mixed, 1)

            if has("rnn_in"):
                for b in range(RNN_BLOCKS):
                    if b in (4, 6):
                        batch_before_scan(b // 2 - 2)
                    if b == 0:
                        pool.wait_ge(tiles_used, TILE0["rnn_in"])
                    elif b == 1:
                        after(pool, ada_step, 11 * 16 if has("down1") else 0)
                    else:
                        pool.wait_ge(s_gate, 2 * (b - 1))
                    dst = mid(20480, 2048) if b % 2 == 0 else araw_
                    pool.dma_start(dst, gate_w[b]).then_inc(gate_arrived[b % 2], 16)
                    if b in (4, 6):
                        batch_after_scan(b // 2 - 2)
                batch_before_scan(2)
                batch_after_scan(2)
            if has("down1"):
                pool.wait_ge(s_gate, UNITS)
                batch_before_scan(3)
                batch_after_scan(3)
                with pool.Fori(11 * 4, ADA_CHUNKS * 4) as i:
                    ada_tiles(i)
            if has("w_in"):
                pool.wait_ge(ada_step, ADA_CHUNKS * 16)
                pool.wait_ge(ada_summed, ADA_CHUNKS)
                pool.dma_start(mask, mask_in).then_inc(mask_arrived, 16)
                pool.wait_ge(sem("parameter_steps"), PARAMETER_STEPS["output_matrix"])
                pool.dma_start(matrix_store[0], bb_made).then_inc(sem("matrices_stored"), 16)
                pool.dma_start(matrix_store[1], scr(2048, 2048)).then_inc(sem("matrices_stored"), 16)
                pool.wait_ge(sem("matrices_stored"), 32)
                pool.wait_ge(sem("parameter_steps"), PARAMETER_STEPS["e_ready"])
                link = ordered(pool, "gpsimd")
                G = nc.gpsimd
                stored_tables = [sem("tables_stored0"), sem("tables_stored1")]
                grid = [P, 2, 16, 16]
                four = lambda ap: ap.rearrange("p (c a b) -> p c a b", a=16, b=16)
                for k in range(UNITS2):
                    two = slice(2 * k, 2 * k + 2)
                    coarse = [e16[i][:, two, :].unsqueeze(3).to_broadcast(grid) for i in range(2)]
                    fine = [e1[i][:, two, :].unsqueeze(2).to_broadcast(grid) for i in range(2)]
                    out_ = table_out[k % 2]
                    if k >= 2:
                        pool.wait_ge(stored_tables[k % 2], 16 * (k // 2))
                    G.tensor_tensor(four(out_[:, 0:512]), coarse[0], fine[0], ALU.mult)
                    link(G.tensor_tensor(four(table_tmp), coarse[1], fine[1], ALU.mult))
                    link(G.tensor_tensor(out_[:, 0:512], out_[:, 0:512], table_tmp, ALU.subtract))
                    G.tensor_tensor(four(out_[:, 512:]), coarse[0], fine[1], ALU.mult)
                    link(G.tensor_tensor(four(table_tmp), coarse[1], fine[0], ALU.mult))
                    link(G.tensor_tensor(out_[:, 512:], out_[:, 512:], table_tmp, ALU.add))
                    pool.dma_start(table_store[k], out_).then_inc(stored_tables[k % 2], 16)
                for b in range(2):
                    pool.wait_ge(stored_tables[b], 16 * UNITS2 // 2)
                pool.wait_ge(tiles_used, TILE0["w_in"])
                pool.dma_start(mid(8960, 2048), matrix_store[0]).then_inc(sem("matrices_back"), 16)
                pool.dma_start(mid(11008, 2048), matrix_store[1]).then_inc(sem("matrices_back"), 16)
                def load_tables(k):
                    pool.dma_start(mid(13056 + 1024 * (k % 4), 1024), table_store[k]).then_inc(table_arrived[k % 4], 16)
                for k in range(4):
                    load_tables(k)
                for k in range(UNITS2):
                    zr, zi, a0, a1, b0, b1 = unit_bufs[k % 2]
                    c_, s_ = tables[k % 4][:, 0], tables[k % 4][:, 1]
                    pool.wait_ge(sem("scanned"), k + 1)
                    G.tensor_tensor(a0, zr, c_, ALU.mult)
                    G.tensor_tensor(a1, zi, s_, ALU.mult)
                    G.tensor_tensor(b0, zr, s_, ALU.mult)
                    link(G.tensor_tensor(b1, zi, c_, ALU.mult))
                    G.tensor_tensor(a0, a0, a1, ALU.subtract)
                    G.tensor_tensor(b0, b0, b1, ALU.add).then_inc(sem("parts_ready"), 1)
                    if k + 4 < UNITS2:
                        load_tables(k + 4)
            finish(pool)


        @block.scalar
        def _(act):
            A = nc.scalar.activation
            splits = [0]

            def split(tile):
                s = splits[0] % RING
                splits[0] += 1
                act.wait_ge(raw_arrived[s], (tile + (RING - s)) * (16 // RING))
                after(act, tiles_used, tile - (RING - 1) if isinstance(tile, int) else tile + (1 - RING))
                A(whi[:, s, :], raw[:, s, :], ACT.Copy).then_inc(hi_ready, 1)

            def group_hi(b, before, dst, g, signal):
                act.wait_ge(tr_ready[b], before + 1)
                for j in range(4):
                    ins = A(dst[:, j, :], tr[b][:, j, :], ACT.Copy, scale=g[:, j:j + 1])
                ins.then_inc(signal, 1)

            def root_of(name, n):
                act.wait_ge(sem("mean_ready"), NORM_AT[name])
                A(root[:, 0:n], mean[:, 0:n], ACT.Sqrt).then_inc(sem("root_ready"), 1)

            carried = []

            def carried_steps(pos):
                for at, step in [c for c in carried if c[0] == pos]:
                    step()
                    carried.remove((at, step))

            def carry(layer, tail, late):
                n = PAIRS[layer] - 1
                if tail and layer in CARRIED_AT:
                    carried.append((CARRIED_AT[layer], lambda: tail(n, 1)))
                elif tail:
                    tail(n, 1)
                for at, step in late:
                    carried.append((at, lambda step=step: step(n)))

            def run(layer, evac, tail=None, extra=None, late=()):
                kt = KTILES[layer]

                def body(i, first):
                    splits[0] = TILE0[layer] + RING
                    for pos in range(2 * kt):
                        if not (layer == "down2" and not first and pos >= 2 * kt - RING):
                            split(i * (2 * kt) + (TILE0[layer] + pos + RING))
                        if extra:
                            extra(i, pos)
                        for at, step in late:
                            if at == pos and not first:
                                step(i - 1)
                        if first:
                            carried_steps(pos)
                        if tail and pos == HOOK and not first:
                            tail(i - 1, 1)
                        if pos == kt - 1:
                            evac(i, 0)
                        if tail and pos == kt + HOOK:
                            tail(i, 0)
                        if pos == 2 * kt - 1:
                            evac(i, 1)

                each_pair(act, layer, body)
                carry(layer, tail, late)

            def chunk_done(layer, i, b):
                act.wait_ge(tiles_used, i * (2 * KTILES[layer]) + (TILE0[layer] + (b + 1) * KTILES[layer]))

            def scaled_to(layer, dst, ready=None):
                def evac(i, b):
                    if ready:
                        ready(i, b)
                    chunk_done(layer, i, b)
                    for t in range(T):
                        ins = A(dst(i, b, t), acc[b][:, t, :], ACT.Copy, scale=rstd[:, t:t + 1])
                    ins.then_inc(sem(f"{layer}_out{b}"), 1)
                return evac

            def residual(layer, extra=None):
                g = RESIDUAL[layer]

                def evac(i, b):
                    act.wait_ge(sem(f"sum_ready{b}"), i + (2 * RES_AT[layer] + 1))
                    A(x[:, :, 2 * i + b, :], tmp[:, b, :, :], ACT.Copy).then_inc(sem(f"x_new{b}"), 1)

                def turned(i, b):
                    if g:
                        c = 4 * (2 * i + b)
                        group_hi(0, GROUP_AT[layer][0] + 2 * i + b, xhi[:, c:c + 4, :], sm[g][:, c:c + 4],
                                 sem("residual_hi"))

                def tail(i, b):
                    last = (i, b) == (PAIRS[layer] - 1, 1)
                    if last and g:
                        carried.append((CARRIED_AT[layer], lambda: turned(i, b)))
                    else:
                        turned(i, b)
                    act.wait_ge(sem(f"x_new{b}"), i + (2 * RES_AT[layer] + 1))
                    for t in range(T):
                        ins = A(mid(t * NW, NW) if last and g else tmp[:, b, t, :], tmp[:, b, t, :], ACT.Square,
                                accum_out=ss[:, t, 2 * i + b:2 * i + b + 1])
                    ins.then_inc(sem(f"sum_used{b}"), 1)
                run(layer, evac, tail, extra)
                if g:
                    carried.pop(-1)[1]()
                root_of(layer, 2)

            def gated(layer):
                def evac(i, b):
                    if b:
                        return
                    if not isinstance(i, int):
                        act.wait_ge(sem(f"{layer}_prod"), i)
                    chunk_done(layer, i, 0)
                    for t in range(T):
                        ins = A(tmp[:, 0, t, :], acc[0][:, t, :], ACT.Silu, scale=rstd[:, t:t + 1])
                    ins.then_inc(sem(f"{layer}_gate"), 1)

                def tail(i, b):
                    if b:
                        act.wait_ge(tr_ready[0], i + (GROUP_AT[layer][0] + 1))
                        A(mhi_.rearrange("p (n e) -> p n e", e=4 * S)[:, i, :],
                          tr[0].rearrange("p c s -> p (c s)"), ACT.Copy).then_inc(sem(f"{layer}_hi"), 1)
                act.wait_ge(rstd_ready, {"ffn0": 2, "ffn1": 4}[layer])
                run(layer, evac, tail)

            def recurrent_in():
                def evac(i, b):
                    chunk_done("rnn_in", i, b)
                    c = 2 * i + b
                    if c >= 2:
                        act.wait_ge(tr_ready[0], GROUP_AT["rnn_in"][0] + c - 1)
                    for t in range(T):
                        ins = A(tmp[:, b, t, :], acc[b][:, t, :], ACT.Copy, scale=rstd[:, t:t + 1])
                    ins.then_inc(sem(f"rnn_in_out{b}"), 1)

                def tail(i, b):
                    c = 2 * i + b
                    if c < 4:
                        act.wait_ge(s_xb, c + 1)
                        for j in range(4 * c, 4 * c + 4):
                            ins = A(xc[:, j, :], xb[:, j, :], ACT.Identity, scale=sm["conv_w"][:, 32 + j:33 + j],
                                    bias=sm["conv_b"][:, j:j + 1])
                        ins.then_inc(s_base, 1)
                    else:
                        act.wait_ge(tr_ready[0], GROUP_AT["rnn_in"][0] + c + 1)
                        A(y_gelu[:, 4 * c - 16:4 * c - 12, :], tr[0], ACT.Gelu_apprx_tanh).then_inc(tr_free[0], 1)

                def decay_of(u):
                    act.wait_ge(s_unit, u + 1)
                    a = decay[u // 4 % 2][:, u % 4]
                    A(a, a, ACT.Copy, scale=2.0, bias=-1.0).then_inc(s_decay, 1)

                def root_of_drive(k):
                    act.wait_ge(s_unit, 4 * k + 4)
                    th = half_tanh[k % 2]
                    A(th, th, ACT.Sqrt, scale=-1.0).then_inc(s_sqrt, 1)

                def state_hi(k):
                    act.wait_ge(s_mixed, k + 1)
                    A(hhi[:, 4 * k:4 * k + 4, :], half_tanh[k % 2].rearrange("p c d s -> p (c d) s")[:, 0:4, :],
                      ACT.Copy).then_inc(s_hhi, 1)

                def unit(i, pos):
                    if i < 2:
                        return
                    f = 16 * (i - 2) + pos
                    if pos % 2 == 0:
                        gate_functions(f // 2)
                        if f:
                            decay_of(f // 2 - 1)
                    for k in range(3):
                        if f == 8 * k + BATCH_AT["root"]:
                            root_of_drive(k)
                        if f == 8 * k + BATCH_AT["hi"]:
                            state_hi(k)

                def gate_functions(u):
                    th = half_tanh[u // 4 % 2][:, u % 4]
                    act.wait_ge(s_gate, u + 1)
                    for d in range(2):
                        A(gates[:, d, 0, :], gates[:, d, 0, :], ACT.Sigmoid,
                          bias=sm["b_a"][:, 16 * d + u:16 * d + u + 1]).then_inc(s_sig, 1)
                        A(gates[:, d, 1, :], gates[:, d, 1, :], ACT.Sigmoid,
                          bias=sm["b_i"][:, 16 * d + u:16 * d + u + 1]).then_inc(s_ig, 1)
                    act.wait_ge(s_sig, 2 * u + 2)
                    if u >= 8:
                        act.wait_ge(s_hlo, u // 4 - 1)
                    for d in range(2):
                        A(th[:, d, :], gates[:, d, 0, :], ACT.Tanh,
                          scale=neg4sp[:, 16 * d + u:16 * d + u + 1]).then_inc(s_tanh, 1)
                    act.wait_ge(s_tanh, 2 * u + 2)
                    A(decay[u // 4 % 2][:, u % 4], th, ACT.Copy, scale=-1.0, bias=1.0).then_inc(s_below, 1)
                act.wait_ge(s_lam, 1)
                act.wait_ge(rstd_ready, 3)
                run("rnn_in", evac, tail, unit)
                carried.append((0, lambda: (decay_of(15), root_of_drive(3))))
                carried.append((LAST_BATCH_AT["hi"], lambda: state_hi(3)))

            act.wait_ge(small_arrived, 16)
            A(lam_tmp[0], sm["lam"], ACT.Abs).then_inc(sem("setup_steps"), 1)
            act.wait_ge(sem("setup_steps"), SETUP_STEPS["lam_abs"])
            A(lam_tmp[0], lam_tmp[0], ACT.Exp, scale=-1.0).then_inc(sem("setup_steps"), 1)
            A(c_act, sm["c"], ACT.Silu).then_inc(sem("setup_steps"), 1)
            act.wait_ge(x_arrived, 16)
            for t in range(T):
                ins = A(mid(t * D, D), x_[:, t * D:(t + 1) * D], ACT.Square, accum_out=ss[:, t, 0:1])
            ins.then_inc(sem("first_squares"), 1)
            root_of("first", 2)
            for q in range(4):
                group_hi(q % 2, q // 2, xhi[:, 4 * q:4 * q + 4, :], sm["g_mix0"][:, 4 * q:4 * q + 4], sem("first_hi"))
            for s in range(RING):
                splits[0] = s
                split(s)
            act.wait_ge(rstd_ready, 1)
            run("qkv", scaled_to("qkv", lambda i, b, t: qkv[:, t, 2 * i + b, :]))

            act.wait_ge(sem("qkv_out0"), 3)
            act.wait_ge(sem("qkv_out1"), 3)
            A(squares, qkv_h[:, :, 0:QH + KVH, :], ACT.Square).then_inc(s_sq, 1)
            act.wait_ge(sem("head_mean"), 1)
            A(rq, ssq, ACT.Sqrt).then_inc(s_rq, 1)
            for n, gi in enumerate((0, 2, 4)):
                act.wait_ge(s_qt, gi + 1)
                A(qk_t[:, 4 * gi:4 * gi + 4, :], [acc[0].rearrange("p t (h s) -> p (t h) s", s=S), tr[0],
                                                  acc[0].rearrange("p t (h s) -> p (t h) s", s=S)][n],
                  ACT.Copy).then_inc(s_qe_a, 1)

            def exps(u):
                act.wait_ge(s_nm, u + 1)
                after(act, s_pt, u - 1)
                for i in range(4):
                    n = 4 * u + i
                    ins = A(probs[:, u % 2, i, :], psum[:, 2 * (u % 2) + i // 2, (i % 2) * S:(i % 2 + 1) * S], ACT.Exp,
                            scale=rqs[:, n:n + 1], bias=nmx[:, n:n + 1], accum_out=sums[:, n:n + 1])
                ins.then_inc(s_exp, 1)

            def heads_hi(u):
                act.wait_ge(s_pv, u + 1)
                A(ohi[:, 2 * u:2 * u + 2, :], psum[:, 6 + u % 2, :].rearrange("p (h s) -> p h s", s=S),
                  ACT.Copy).then_inc(s_oh, 1)
            exps(0)
            for u in range(8):
                if u < 7:
                    exps(u + 1)
                if u:
                    heads_hi(u - 1)
                act.wait_ge(s_pt, u + 1)
                after(act, s_pv, u - 1)
                A(probs_t[:, u % 2, :, :, :].rearrange("p h k q -> p (h k q)"),
                  tr[0].rearrange("p c s -> p (c s)"), ACT.Copy).then_inc(s_pte, 1)
            heads_hi(7)
            residual("w_o")
            if has("ffn0"):
                gated("ffn0")
            if has("down0"):
                residual("down0")
            if has("rnn_in"):
                recurrent_in()
                residual("rnn_out")
            if has("ffn1"):
                gated("ffn1")
            def token_norm(name, n_rstd, sh, gs):
                act.wait_ge(rstd_ready, n_rstd)
                A(normed[:, 0, :], x_[:, 0:D], ACT.Copy, scale=rstd[:, 0:1]).then_inc(sem(f"{name}_normed"), 1)
                for q in range(4):
                    b = q % 2
                    act.wait_ge(tr_ready[b], GROUP_AT[name][b] + q // 2 + 1)
                    for j in range(4):
                        c = 4 * q + j
                        ins = A(xhi[:, c, :], tr[b][:, j, :], ACT.Identity, scale=gs[:, c:c + 1], bias=sh[:, c:c + 1])
                    ins.then_inc(sem(f"{name}_hi"), 1)

            def parameters(i, pos):
                if (i, pos) == (0, 0):
                    act.wait_ge(tiles_used, TILE0["down1"])
                    act.dma_start(ssm_raw, ssm_in).then_inc(ssm_arrived, 16)
                    A(st_tmp[0], sm["log_step"], ACT.Exp).then_inc(sem("setup_steps"), 1)
                if (i, pos) == (0, 14):
                    act.wait_ge(sem("parameter_steps"), PARAMETER_STEPS["angle_ready"])
                    A(st_tmp[4], st_tmp[3], ACT.Sin)
                    A(st_tmp[5], st_tmp[3], ACT.Sin, scale=0.5)
                    A(st_tmp[6], st_tmp[2], ACT.Tanh, scale=0.5).then_inc(sem("setup_steps"), 1)

            def project_in():
                def evac(i, b):
                    chunk_done("w_in", i, b)
                    after(act, tr_ready[0], 0 if not i else GROUP_AT["w_in"][0] + 2 * b + 2)
                    A(tmp[:, b, :, :], acc[b], ACT.Copy).then_inc(sem(f"w_in_out{b}"), 1)

                def extra(i, pos):
                    if (i, pos) == (1, 13):
                        gelu(0)
                run("w_in", evac, None, extra)
                for n in range(4):
                    splits[0] = TILE0["w_in_kv"] + RING + n
                    split(TILE0["w_in_kv"] + RING + n)
                act.wait_ge(tiles_used, TILE0["glu"])
                A(kv, acc[0][:, :, 0:256], ACT.Copy).then_inc(sem("w_in_kv_out"), 1)

            def gelu(q):
                act.wait_ge(sem("skip_added"), q + 1)
                A(z_t[:, q, :], z_t[:, q, :], ACT.Gelu_apprx_tanh).then_inc(sem("z_ready"), 1)

            def window_exps(w):
                act.wait_ge(sem("max2_ready"), w + 1)
                for h in range(2):
                    for n, k in enumerate((slice(0, P), slice(P, 3 * P))):
                        c = 4 * w + 2 * h + n
                        A(masked[w % 2][:, h, k], masked[w % 2][:, h, k], ACT.Exp, bias=nm2[:, c:c + 1],
                          accum_out=sum2[:, c:c + 1])
                A(m2[:, 4 * w:4 * w + 4], m2[:, 4 * w:4 * w + 4], ACT.Exp).then_inc(sem("exp2_ready"), 1)

            def window_turned(w):
                act.wait_ge(sem("probs2_turned"), w + 1)
                after(act, sem("heads2_ready"), w - 1)
                A(turned[w % 2].rearrange("p h n q -> p (h n q)"), psum[:, 2:4, :].rearrange("p b e -> p (b e)")[:, 0:768],
                  ACT.Copy).then_inc(sem("turned2_ready"), 1)

            def z_hi(half):
                act.wait_ge(sem("z_ready"), 4 * half + 4)
                A(xhi[:, 4 * half:4 * half + 4, :], z_t[:, 4 * half:4 * half + 4, :], ACT.Copy).then_inc(sem("z_hi_ready"), 1)

            def mixers():
                for n in range(11):
                    k, w = 5 + n, n
                    if 1 <= w <= 8:
                        window_turned(w - 1)
                    if k % 2:
                        gelu((k - 3) // 2)
                    if w < 8:
                        window_exps(w)
                    if k == 9:
                        z_hi(0)
                gelu(7)
                z_hi(1)

            def glu_and_merge():
                def evac(i, b):
                    chunk_done("glu", i, b)
                    A(tmp[:, b, :, :], acc[b], ACT.Sigmoid).then_inc(sem(f"glu_out{b}"), 1)
                run("glu", evac)
                act.wait_ge(sem("merged_ready"), 2)
                for t in range(T):
                    for half in range(2):
                        ins = A(squares_out[:, (2 * t + half) * W2:(2 * t + half + 1) * W2], merged[:, t, half * W2:(half + 1) * W2], ACT.Square,
                                accum_out=mean[:, 2 * t + half:2 * t + half + 1])
                ins.then_inc(sem("merge_squares"), 1)
                root_of("merge", 4)
                act.wait_ge(rstd_ready, 6)
                for half in range(2):
                    m = merged[:, 0, half * W2:(half + 1) * W2]
                    A(m, m, ACT.Copy, scale=rstd[:, half:half + 1]).then_inc(sem("merge_scaled"), 1)
                for q in range(4):
                    group_hi(q % 2, GROUP_AT["merge"][q % 2] + q // 2, xhi[:, 4 * q:4 * q + 4, :],
                             sm["g_merged"][:, 4 * q:4 * q + 4], sem("merge_hi"))

            def gathered(layer):
                dst = GATHERED[layer]

                def evac(i, b):
                    chunk_done(layer, i, b)
                    n = 2 * i + b
                    after(act, sem(f"{layer}_out{b}"), i)
                    A(dst[:, :, n, :], acc[b], ACT.Copy)
                    for t in range(T):
                        ins = A(tmp[:, b, t, :], acc[b][:, t, :], ACT.Square, accum_out=ss[:, t, n:n + 1])
                    ins.then_inc(sem(f"{layer}_out{b}"), 1)
                run(layer, evac)
                root_of(layer, 2)

            def up_convolved():
                w = sm["conv2_w"].rearrange("p (k h n j) -> p k h n j", k=3, h=2, j=4)
                bias = sm["conv2_b"].rearrange("p (h n j) -> p h n j", h=2, j=4)
                flat = conv_.rearrange("p (h e) -> p h e", h=2)

                def evac(i, b):
                    chunk_done("ffn2", i, b)
                    after(act, tr_ready[b], i + GROUP_AT["ffn2"][b])
                    A(tmp[:, b, :, :], acc[b], ACT.Copy).then_inc(sem(f"ffn2_copied{b}"), 1)

                def base(i, b):
                    after(act, sem("ffn2_lo"), i)
                    act.wait_ge(tr_ready[b], i + (GROUP_AT["ffn2"][b] + 1))
                    for j in range(4):
                        ins = A(conv[:, 4 * b + j, :], tr[b][:, j, :], ACT.Identity, scale=w[:, 2, b, i, j:j + 1],
                                bias=bias[:, b, i, j:j + 1])
                    ins.then_inc(sem(f"ffn2_base{b}"), 1)

                def gelu(i):
                    act.wait_ge(tr_free[1], i + (GROUP_AT["ffn2"][1] + 1))
                    A(flat[:, 1, :], flat[:, 1, :], ACT.Gelu_apprx_tanh).then_inc(sem("ffn2_gelu"), 1)

                def hi(i):
                    act.wait_ge(sem("ffn2_prod"), i + 1)
                    A(mhi_.rearrange("p (n e) -> p n e", e=4 * S)[:, i, :], flat[:, 0, :], ACT.Copy).then_inc(sem("ffn2_hi"), 1)
                run("ffn2", evac, None, None, ((4, lambda i: base(i, 0)), (5, lambda i: base(i, 1)), (9, gelu), (11, hi)))

            if has("w_in"):
                residual("down1", parameters)
                act.wait_ge(ada_ready, 1)
                for b in range(2):
                    act.wait_ge(sem(f"tables_stored{b}"), 16 * UNITS2 // 2)
                token_norm("norm_mix", 5, sh_m, gs_m)
                project_in()
                mixers()
                glu_and_merge()
                gathered("w_out")
                for t in range(T):
                    act.wait_ge(sem("x_mixed"), t + 1)
                    ins = A(mid(6912 + t * D, D), x_[:, t * D:(t + 1) * D], ACT.Square, accum_out=ss[:, t, 0:1])
                ins.then_inc(sem("x_squares"), 1)
                root_of("norm_ffn", 2)
                token_norm("norm_ffn", 8, sh_f, gs_f)
                up_convolved()
                gathered("down2")

        @block.vector
        def _(dve):
            V = nc.vector
            splits = [0]

            def split(tile):
                s = splits[0] % RING
                splits[0] += 1
                dve.wait_ge(hi_ready, tile + 1)
                V.tensor_tensor(wlo[:, s, :], raw[:, s, :], whi[:, s, :].bitcast(F32), ALU.subtract).then_inc(lo_ready, 1)

            def group_lo(b, dst_lo, dst_hi, g, signal, count):
                dve.wait_ge(signal, count)
                for j in range(4):
                    ins = V.scalar_tensor_tensor(dst_lo[:, j, :], tr[b][:, j, :], g[:, j:j + 1],
                                                 dst_hi[:, j, :].bitcast(F32), ALU.mult, ALU.subtract)
                ins.then_inc(tr_free[b], 1)

            def rstd_of(name, total, count, n=2):
                if total is not None:
                    ordered(dve, "vector")(total)
                V.tensor_scalar(mean[:, 0:n], mean[:, 0:n], 1.0 / (D if n == 2 else W2), EPS, ALU.mult,
                                ALU.add).then_inc(sem("mean_ready"), 1)
                dve.wait_ge(sem("root_ready"), NORM_AT[name])
                V.reciprocal(rstd[:, 0:n], root[:, 0:n]).then_inc(rstd_ready, 1)

            def ada_product(a, i, at):
                s = a % 2
                dve.wait_ge(ada_arrived[s], (i * 4 + (at * 4 + a // 2 + 1)) * 16)
                for k in range(KT):
                    w, c = araw[:, s, k, :], c_act[:, 2 * a + k:2 * a + k + 1]
                    if a == 0 and k == 0:
                        after(dve, ada_summed, i + at)
                        ins = V.tensor_scalar(adacc_, w, c, None, ALU.mult)
                    else:
                        dve.wait_ge(ada_step, i * 16 + (at * 16 + 2 * a + k))
                        ins = V.scalar_tensor_tensor(adacc_, w, c, adacc_, ALU.mult, ALU.add)
                    ins.then_inc(ada_step, 1)

            def ada_out(i, at):
                dve.wait_ge(ada_summed, i + (at + 1))
                cols = adat_.rearrange("p (n j) -> p n j", j=4)
                bias = sm["b_ada"].rearrange("p (n j) -> p n j", j=4)
                V.tensor_tensor(cols[:, i + at, :], psum[:, 6, 0:4], bias[:, i + at, :], ALU.add).then_inc(ada_done, 1)

            carried = []

            def carried_steps(pos):
                for at, step in [c for c in carried if c[0] == pos]:
                    step()
                    carried.remove((at, step))

            def carry(layer, tail, late):
                n = PAIRS[layer] - 1
                if tail and layer in CARRIED_AT:
                    carried.append((CARRIED_AT[layer], lambda: tail(n, 1)))
                elif tail:
                    tail(n, 1)
                for at, step in late:
                    carried.append((at, lambda step=step: step(n)))

            def run(layer, evac=None, tail=None, extra=None, late=()):
                kt = KTILES[layer]
                ada = ADA_AT.get(layer) if has("down1") else None

                def body(i, first):
                    splits[0] = TILE0[layer] + RING
                    for pos in range(2 * kt):
                        if not (layer == "down2" and not first and pos >= 2 * kt - RING):
                            split(i * (2 * kt) + (TILE0[layer] + pos + RING))
                        if extra:
                            extra(i, pos)
                        for at, step in late:
                            if at == pos and not first:
                                step(i - 1)
                        if first:
                            carried_steps(pos)
                        if ada is not None and pos in ADA_POS:
                            ada_product(pos - ADA_POS[0], i, ada)
                        if pos == HOOK and not first:
                            if tail:
                                tail(i - 1, 1)
                            if ada is not None:
                                ada_out(i - 1, ada)
                        if evac and pos == kt - 1:
                            evac(i, 0)
                        if tail and pos == kt + HOOK:
                            tail(i, 0)
                        if evac and pos == 2 * kt - 1:
                            evac(i, 1)
                each_pair(dve, layer, body)
                carry(layer, tail, late)
                if ada is not None:
                    ada_out(PAIRS[layer] - 1, ada)

            def chunk_done(layer, i, b):
                dve.wait_ge(tiles_used, i * (2 * KTILES[layer]) + (TILE0[layer] + (b + 1) * KTILES[layer]))

            def residual(layer, count, extra=None):
                g = RESIDUAL[layer]

                def evac(i, b):
                    chunk_done(layer, i, b)
                    after(dve, sem(f"sum_used{b}"), i + 2 * RES_AT[layer])
                    V.tensor_tensor(tmp[:, b, :, :], acc[b], x[:, :, 2 * i + b, :], ALU.add).then_inc(
                        sem(f"sum_ready{b}"), 1)

                def tail(i, b):
                    if g:
                        c = 4 * (2 * i + b)
                        group_lo(0, xlo[:, c:c + 4, :], xhi[:, c:c + 4, :], sm[g][:, c:c + 4],
                                 sem("residual_hi"), 4 * RES_AT[layer] + 2 * i + b + 1)
                run(layer, evac, tail, extra)
                for b in range(2):
                    dve.wait_ge(sem(f"sum_used{b}"), 2 * RES_AT[layer] + 2)
                rstd_of(layer, V.reduce_sum(mean[:, 0:T], ss, AX), count)

            def gated(layer):
                dve.wait_ge(rstd_ready, {"ffn0": 2, "ffn1": 4}[layer])

                def evac(i, b):
                    if not b:
                        return
                    chunk_done(layer, i, 1)
                    after(dve, tr_ready[0], i + GROUP_AT[layer][0])
                    dve.wait_ge(sem(f"{layer}_gate"), i + 1)
                    for t in range(T):
                        ins = V.scalar_tensor_tensor(tmp[:, 1, t, :], acc[1][:, t, :], rstd[:, t:t + 1],
                                                     tmp[:, 0, t, :], ALU.mult, ALU.mult)
                    ins.then_inc(sem(f"{layer}_prod"), 1)

                def tail(i, b):
                    if b:
                        dve.wait_ge(sem(f"{layer}_hi"), i + 1)
                        hi = mhi_.rearrange("p (n e) -> p n e", e=4 * S)[:, i, :]
                        lo = mlo_.rearrange("p (n e) -> p n e", e=4 * S)[:, i, :]
                        V.tensor_tensor(lo, tr[0].rearrange("p c s -> p (c s)"), hi.bitcast(F32),
                                        ALU.subtract).then_inc(tr_free[0], 1)
                run(layer, evac, tail)

            def softplus_of_lambda():
                link = ordered(dve, "vector")
                y, z, z2, poly = lam_tmp
                dve.wait_ge(sem("setup_steps"), SETUP_STEPS["lam_exp"])
                link(V.tensor_scalar(z, y, 2.0, None, ALU.add))
                link(V.reciprocal(z, z))
                link(V.tensor_tensor(z, z, y, ALU.mult))
                link(V.tensor_tensor(z2, z, z, ALU.mult))
                link(V.tensor_scalar(poly, z2, 1.0 / 17, 1.0 / 15, ALU.mult, ALU.add))
                for n in (13, 11, 9, 7, 5, 3, 1):
                    link(V.tensor_tensor(poly, poly, z2, ALU.mult))
                    link(V.tensor_scalar(poly, poly, 1.0 / n, None, ALU.add))
                link(V.tensor_tensor(poly, poly, z, ALU.mult))
                link(V.tensor_scalar(z, sm["lam"], -1.0, 0.0, ALU.mult, ALU.max))
                link(V.scalar_tensor_tensor(z, poly, 2.0, z, ALU.mult, ALU.add))
                V.tensor_scalar(neg4sp, z, -LRU_C / 2, None, ALU.mult).then_inc(s_lam, 1)

            def recurrent_in():
                def tail(i, b):
                    c = 2 * i + b
                    if c >= 4:
                        return
                    dve.wait_ge(tr_ready[0], GROUP_AT["rnn_in"][0] + c + 1)
                    V.tensor_copy(xb[:, 4 * c:4 * c + 4, :], tr[0]).then_inc(tr_free[0], 1)
                    dve.wait_ge(tr_free[0], GROUP_AT["rnn_in"][0] + c + 1)
                    V.engine_nop().then_inc(s_xb, 1)
                    dve.wait_ge(s_base, c + 1)
                    for n, (tap, dst, src) in enumerate(((0, slice(2, S), slice(0, S - 2)), (1, slice(1, S), slice(0, S - 1)),
                                                         (3, slice(0, S - 1), slice(1, S)))):
                        for j in range(4 * c, 4 * c + 4):
                            ins = V.scalar_tensor_tensor(xc[:, j, dst], xb[:, j, src], sm["conv_w"][:, 16 * tap + j:16 * tap + j + 1],
                                                         xc[:, j, dst], ALU.mult, ALU.add)
                        ins.then_inc(s_conv, 1)
                        dve.wait_ge(s_conv, 3 * c + n + 1)

                link = ordered(dve, "vector")

                def gated_input(u):
                    w = drive[u // 4 % 2][:, u % 4]
                    dve.wait_ge(s_ig, 2 * u + 2)
                    dve.wait_ge(s_tanh, 2 * u + 2)
                    V.tensor_tensor(w, gates[:, :, 1, :], xc[:, u, :].unsqueeze(1).to_broadcast([P, 2, S]), ALU.mult).then_inc(s_drive, 1)

                def one_plus_decay(u):
                    a, w = (v[u // 4 % 2][:, u % 4] for v in (decay, drive))
                    dve.wait_ge(s_below, u + 1)
                    link(V.reciprocal(a, a))
                    V.scalar_tensor_tensor(w, w, 2.0, a, ALU.mult, ALU.mult).then_inc(s_unit, 1)

                def scans(k):
                    a, w = (v[k % 2] for v in (decay, drive))
                    dve.wait_ge(s_decay, 4 * k + 4)
                    dve.wait_ge(s_scaled, k + 1)
                    for c in range(4):
                        V.tensor_tensor_scan(w[:, c, 0, :], a[:, c, 0, :], w[:, c, 0, :], 0.0, ALU.mult, ALU.add)
                        ins = V.tensor_tensor_scan(w[:, c, 1, ::-1], a[:, c, 1, ::-1], w[:, c, 1, ::-1], 0.0, ALU.mult, ALU.add)
                    ins.then_inc(s_scan, 1)

                def state_lo(k):
                    dve.wait_ge(s_hhi, k + 1)
                    V.tensor_tensor(hlo[:, 4 * k:4 * k + 4, :], half_tanh[k % 2].rearrange("p c d s -> p (c d) s")[:, 0:4, :],
                                    hhi[:, 4 * k:4 * k + 4, :].bitcast(F32), ALU.subtract).then_inc(s_hlo, 1)

                def unit(i, pos):
                    if i < 2:
                        return
                    f = 16 * (i - 2) + pos
                    (one_plus_decay if f % 2 else gated_input)(f // 2)
                    for k in range(3):
                        if f == 8 * k + BATCH_AT["scan"]:
                            scans(k)
                        if f == 8 * k + BATCH_AT["lo"]:
                            state_lo(k)
                run("rnn_in", None, tail, unit)
                carried.append((LAST_BATCH_AT["scan"], lambda: scans(3)))
                carried.append((LAST_BATCH_AT["lo"], lambda: state_lo(3)))

            dve.wait_ge(sem("first_squares"), 1)
            rstd_of("first", V.tensor_copy(mean[:, 0:T], ss[:, :, 0]), 1)
            for q in range(4):
                group_lo(q % 2, xlo[:, 4 * q:4 * q + 4, :], xhi[:, 4 * q:4 * q + 4, :],
                         sm["g_mix0"][:, 4 * q:4 * q + 4], sem("first_hi"), q + 1)
            for s in range(RING):
                splits[0] = s
                split(s)
            if has("ffn0"):
                dve.wait_ge(sem("setup_steps"), SETUP_STEPS["c_ready"])
            dve.wait_ge(s_rope, 16)
            cos = rope[:, 0:128].rearrange("p (t a f) -> p t a f", t=T, a=2)
            sin = rope[:, 128:256].rearrange("p (t a f) -> p t a f", t=T, a=2)
            for k in range(2):
                gain = rope[:, 256 + 128 * k:384 + 128 * k].rearrange("p (a h f) -> p a h f", a=2, h=2)
                for t in range(T):
                    keep = tabs[:, 2 * k, t, :].rearrange("p (a h f) -> p a h f", a=2, h=2)
                    cross = tabs[:, 2 * k + 1, t, :].rearrange("p (a h f) -> p a h f", a=2, h=2)
                    for h in range(2):
                        V.tensor_tensor(keep[:, :, h, :], gain[:, :, h, :], cos[:, t], ALU.mult)
                        ins = V.scalar_tensor_tensor(cross[:, :, h, :], gain[:, :, 1 - h, :], 1.0 if h else -1.0,
                                                     sin[:, t], ALU.mult, ALU.mult)
                    ins.then_inc(sem("tabs_ready"), 1)
            softplus_of_lambda()
            run("qkv")
            dve.wait_ge(sem("tabs_ready"), 4)
            dve.wait_ge(sem("qkv_out0"), 3)
            dve.wait_ge(sem("qkv_out1"), 3)
            for t in range(T):
                for k, (a, n) in enumerate(((0, QH), (QH, KVH))):
                    src, out_, sw = qkv_h[:, t, a:a + n, :], rot[:, t, a:a + n, :], swapped[:, t, a:a + n, :]
                    V.tensor_tensor(out_, src, tabs[:, 2 * k, t, :].unsqueeze(1).to_broadcast([P, n, HEAD]), ALU.mult)
                    s5 = src.rearrange("p h (a z f) -> p h a z f", a=2, z=2)
                    w5 = sw.rearrange("p h (a z f) -> p h a z f", a=2, z=2)
                    c4 = tabs[:, 2 * k + 1, t, :].rearrange("p (a z f) -> p a z f", a=2, z=2)
                    for z in range(2):
                        ins = V.tensor_tensor(w5[:, :, :, z, :], s5[:, :, :, 1 - z, :],
                                              c4[:, :, z, :].unsqueeze(1).to_broadcast([P, n, 2, FREQS]), ALU.mult)
            link = ordered(dve, "vector")
            link(ins)
            link(V.tensor_tensor(rot, rot, swapped, ALU.add))
            dve.wait_ge(s_sq, 1)
            by_head = lambda ap: ap.rearrange("p (h t) -> p t h", t=T)
            link(V.reduce_sum(by_head(ssq), squares, AX))
            V.tensor_scalar(ssq, ssq, 1.0 / HEAD, EPS, ALU.mult, ALU.add).then_inc(sem("head_mean"), 1)
            dve.wait_ge(s_rq, 1)
            link(V.reciprocal(rq, rq))
            V.tensor_scalar(rqs, rq, HEAD ** -0.5, None, ALU.mult)
            for t in range(T):
                ins = V.tensor_tensor(rot[:, t, QH:, :], rot[:, t, QH:, :],
                                      by_head(rq)[:, t, QH:].unsqueeze(2).to_broadcast([P, KVH, HEAD]), ALU.mult)
            ins.then_inc(s_rot, 1)
            for n, gi in enumerate((1, 3)):
                dve.wait_ge(s_qt, gi + 1)
                V.tensor_copy(qk_t[:, 4 * gi:4 * gi + 4, :], [acc[1].rearrange("p t (h s) -> p (t h) s", s=S), tr[1]][n]).then_inc(s_qe_v, 1)

            def head_max(u):
                dve.wait_ge(s_sc, u + 1)
                b = 2 * (u % 2)
                link(V.tensor_reduce(mx[:, 4 * u:4 * u + 4], psum[:, b:b + 2, :].rearrange("p h (t k) -> p (h t) k", k=S), AX, ALU.max))
                V.scalar_tensor_tensor(nmx[:, 4 * u:4 * u + 4], mx[:, 4 * u:4 * u + 4], -1.0, rqs[:, 4 * u:4 * u + 4],
                                       ALU.mult, ALU.mult).then_inc(s_nm, 1)

            def heads_lo(u):
                dve.wait_ge(s_oh, u + 1)
                V.tensor_tensor(olo[:, 2 * u:2 * u + 2, :], psum[:, 6 + u % 2, :].rearrange("p (h s) -> p h s", s=S),
                                ohi[:, 2 * u:2 * u + 2, :].bitcast(F32), ALU.subtract).then_inc(s_ol, 1)
            head_max(0)
            for u in range(8):
                if u < 7:
                    head_max(u + 1)
                dve.wait_ge(s_exp, u + 1)
                link(V.reciprocal(rinv[:, 4 * u:4 * u + 4], sums[:, 4 * u:4 * u + 4]))
                V.tensor_tensor(probs[:, u % 2, :, :], probs[:, u % 2, :, :],
                                rinv[:, 4 * u:4 * u + 4].unsqueeze(2).to_broadcast([P, 4, S]), ALU.mult).then_inc(s_pn, 1)
                if u:
                    heads_lo(u - 1)
            heads_lo(7)
            residual("w_o", 2)
            if has("ffn0"):
                gated("ffn0")
            if has("down0"):
                residual("down0", 3)
            if has("rnn_in"):
                recurrent_in()
                residual("rnn_out", 4)
            if has("ffn1"):
                gated("ffn1")
            def ada_gains():
                dve.wait_ge(ada_done, ADA_CHUNKS)
                for at, g in ((1, "g_pre_mix"), (2, "g_post_mix"), (4, "g_pre_ffn"), (5, "g_post_ffn")):
                    v = adat_[:, 16 * at:16 * at + 16]
                    ins = V.scalar_tensor_tensor(v, v, 1.0, sm[g], ALU.add, ALU.mult)
                ins.then_inc(ada_ready, 1)
                dve.wait_ge(ada_ready, 1)

            def token_norm(name, n_rstd, sh, gs):
                dve.wait_ge(rstd_ready, n_rstd)
                V.tensor_scalar(normed[:, 1, :], x_[:, D:2 * D], rstd[:, 1:2], None, ALU.mult).then_inc(sem(f"{name}_normed"), 1)
                for q in range(4):
                    b = q % 2
                    dve.wait_ge(sem(f"{name}_hi"), q + 1)
                    for j in range(4):
                        c = 4 * q + j
                        ins = V.tensor_scalar(shifted[b][:, j, :], tr[b][:, j, :], gs[:, c:c + 1], sh[:, c:c + 1], ALU.mult, ALU.add)
                    ins.then_inc(sem(f"{name}_shifted"), 1)
                    dve.wait_ge(sem(f"{name}_shifted"), q + 1)
                    V.tensor_tensor(xlo[:, 4 * q:4 * q + 4, :], shifted[b], xhi[:, 4 * q:4 * q + 4, :].bitcast(F32),
                                    ALU.subtract).then_inc(tr_free[b], 1)

            def state_parameters():
                link = ordered(dve, "vector")
                lr, li = sm["lam_re"], sm["lam_im"]
                dt, ang, lrdt, red, sin_, half_, th, cos_, e, m, f_re, f_im, a1, a2, a3, den = st_tmp[:16]
                w_re, w_im, v_re, v_im = st_tmp[16:20]
                TWO_PI = [6.28125, 0.0019350051879882812, 3.019916050561733e-07]
                MAGIC = 1.5 * 2.0 ** 23

                def angles():
                    dve.wait_ge(sem("setup_steps"), SETUP_STEPS["dt_ready"])
                    link(V.tensor_tensor(lrdt, lr, dt, ALU.mult))
                    link(V.tensor_tensor(ang, li, dt, ALU.mult))
                    link(V.tensor_scalar(a1, ang, 1.0 / (2.0 * np.pi), MAGIC, ALU.mult, ALU.add))
                    link(V.tensor_scalar(a1, a1, MAGIC, None, ALU.subtract))
                    link(V.scalar_tensor_tensor(red, a1, -TWO_PI[0], ang, ALU.mult, ALU.add))
                    link(V.scalar_tensor_tensor(red, a1, -TWO_PI[1], red, ALU.mult, ALU.add))
                    link(V.scalar_tensor_tensor(red, a1, -TWO_PI[2], red, ALU.mult, ALU.add))
                    V.tensor_scalar(red, red, 3.1415925, -3.1415925, ALU.min, ALU.max).then_inc(sem("parameter_steps"), 1)

                def factors():
                    dve.wait_ge(sem("setup_steps"), SETUP_STEPS["sines_ready"])
                    link(V.tensor_scalar(a1, th, -1.0, 1.0, ALU.mult, ALU.add))
                    link(V.reciprocal(a1, a1))
                    link(V.scalar_tensor_tensor(e, th, 2.0, a1, ALU.mult, ALU.mult))
                    link(V.tensor_scalar(m, e, 1.0, None, ALU.add))
                    link(V.tensor_tensor(a2, half_, half_, ALU.mult))
                    link(V.tensor_scalar(cos_, a2, -2.0, 1.0, ALU.mult, ALU.add))
                    link(V.scalar_tensor_tensor(a3, a2, -2.0, m, ALU.mult, ALU.mult))
                    link(V.tensor_tensor(e, e, a3, ALU.add))
                    link(V.tensor_tensor(a1, m, sin_, ALU.mult))
                    link(V.tensor_tensor(a2, lr, lr, ALU.mult))
                    link(V.tensor_tensor(a3, li, li, ALU.mult))
                    link(V.tensor_tensor(den, a2, a3, ALU.add))
                    link(V.reciprocal(den, den))

                def factors2():
                    link(V.tensor_tensor(a2, e, lr, ALU.mult))
                    link(V.tensor_tensor(a3, a1, li, ALU.mult))
                    link(V.tensor_tensor(f_re, a2, a3, ALU.add))
                    link(V.tensor_tensor(f_re, f_re, den, ALU.mult))
                    link(V.tensor_tensor(a2, a1, lr, ALU.mult))
                    link(V.tensor_tensor(a3, e, li, ALU.mult))
                    link(V.tensor_tensor(f_im, a2, a3, ALU.subtract))
                    link(V.tensor_tensor(f_im, f_im, den, ALU.mult))
                    link(V.tensor_copy(mag_keep, m))

                def input_matrix(part):
                    if part == 0:
                        dve.wait_ge(ssm_arrived, 16)
                        link(V.memset(scr(2048, 2048), 0.0))
                    f = [v.unsqueeze(2).to_broadcast([P, ST, GROUP]) for v in (f_re, f_im)]
                    t0, t1 = (by_tile(scr(4096 + 512 * i, 512), GROUP) for i in range(2))
                    link(V.tensor_tensor(t0, b_raw[part], f[0], ALU.mult))
                    link(V.tensor_tensor(t1, b_raw[1 - part], f[1], ALU.mult))
                    for g in range(2):
                        r = slice(64 * g, 64 * g + 64)
                        ins = V.tensor_tensor(bd[part][r, :, GROUP * g:GROUP * g + GROUP], t0[r], t1[r],
                                              ALU.add if part else ALU.subtract)
                    link(ins)
                    if part:
                        V.engine_nop().then_inc(sem("parameter_steps"), 1)

                def turned_matrix(b):
                    dve.wait_ge(tr_ready[0], GROUP_AT["ssm_b"][0] + b + 1)
                    V.tensor_copy(bb_made[:, 1024 * b:1024 * b + 1024], tr[0].rearrange("p c s -> p (c s)")).then_inc(tr_free[0], 1)

                def output_matrix():
                    link(V.memset(scr(2048, 2048), 0.0))
                    for g in range(2):
                        r, c = slice(64 * g, 64 * g + 64), slice(GROUP * g, GROUP * g + GROUP)
                        V.tensor_copy(c_made[0][r, :, c], c_raw[0][r])
                        ins = V.tensor_scalar(c_made[1][r, :, c], c_raw[1][r], -1.0, None, ALU.mult)
                    ins.then_inc(sem("parameter_steps"), 1)
                    dve.wait_ge(sem("parameter_steps"), PARAMETER_STEPS["output_matrix"])

                def cmul(out_, a_, w_, n):
                    t_ = [by_tile(v[:, 0:ST * n], n) for v in cm_tmp]
                    wb = [v.unsqueeze(2).to_broadcast([P, ST, n]) for v in w_]
                    V.tensor_tensor(t_[0], a_[0], wb[0], ALU.mult)
                    V.tensor_tensor(t_[1], a_[1], wb[1], ALU.mult)
                    V.tensor_tensor(t_[2], a_[0], wb[1], ALU.mult)
                    link(V.tensor_tensor(t_[3], a_[1], wb[0], ALU.mult))
                    V.tensor_tensor(out_[0], t_[0], t_[1], ALU.subtract)
                    link(V.tensor_tensor(out_[1], t_[2], t_[3], ALU.add))

                def powers(step):
                    dst = e1 if step < 4 else e16
                    k = 1 << (step % 4)
                    one = lambda v: v.unsqueeze(2)
                    if step == 0:
                        V.tensor_copy(w_re, cos_)
                        link(V.tensor_copy(w_im, sin_))
                    if k == 1:
                        V.memset(dst[0][:, :, 0:1], 1.0)
                        link(V.memset(dst[1][:, :, 0:1], 0.0))
                    cmul([v[:, :, k:2 * k] for v in dst], [v[:, :, 0:k] for v in dst], (w_re, w_im), k)
                    if step < 7:
                        cmul([one(v_re), one(v_im)], [one(w_re), one(w_im)], (w_re, w_im), 1)
                        V.tensor_copy(w_re, v_re)
                        link(V.tensor_copy(w_im, v_im))
                    else:
                        V.engine_nop().then_inc(sem("parameter_steps"), 1)
                steps = {13: angles, 15: factors, 17: factors2, 19: lambda: input_matrix(0), 20: lambda: input_matrix(1),
                         24: lambda: turned_matrix(0), 26: lambda: turned_matrix(1), 28: output_matrix}
                for n in range(8):
                    steps[29 + n + n // 2] = lambda n=n: powers(n)
                return lambda i, pos: steps[pos]() if i == 0 and pos in steps else None

            def project_in():
                def copied(c, half):
                    n = 2 * c + half
                    dve.wait_ge(tr_ready[0], GROUP_AT["w_in"][0] + n + 1)
                    dst = u_t[:, 2 * n:2 * n + 2, :] if c < 2 else q2_t[:, 2 * n - 8:2 * n - 6, :]
                    V.tensor_copy(dst, by_tile(psum[:, 5, :], S)).then_inc(tr_free[0], 1)

                def extra(i, pos):
                    for half in range(2):
                        for b in range(2):
                            if pos == TURN_AT[half] + 8 * (1 - b) and (b == 0 or i):
                                copied(2 * i if not b else 2 * i - 1, half)
                    for part in range(3):
                        at = divmod(16 * i + pos - part, 16)
                        if at in STREAM_UNITS:
                            unit(STREAM_UNITS[at], part)
                    if (i, pos) == (1, 12):
                        skip(0)
                run("w_in", None, None, extra)
                for n in range(4):
                    splits[0] = TILE0["w_in_kv"] + RING + n
                    split(TILE0["w_in_kv"] + RING + n)
                    if n == 0:
                        unit(4, 2)
                    if n >= 2:
                        copied(3, n - 2)
                dve.wait_ge(tr_ready[0], GROUP_AT["w_in_k"][0] + 1)
                V.tensor_copy(k2_t, psum[:, 5, 0:S]).then_inc(tr_free[0], 1)

            def unit(k, part):
                link = ordered(dve, "vector")
                zr, zi, a0, a1, b0, b1 = unit_bufs[k % 2]
                c_, s_ = tables[k % 4][:, 0], tables[k % 4][:, 1]
                re_, im_ = (psum[:, 6:8, b * S:(b + 1) * S] for b in range(2))
                if part == 0:
                    dve.wait_ge(table_arrived[k % 4], 16 * (k // 4 + 1))
                    dve.wait_ge(sem("inputs_ready"), k + 1)
                    after(dve, sem("state_out"), k - 1)
                    V.tensor_tensor(a0, re_, c_, ALU.mult)
                    V.tensor_tensor(a1, im_, s_, ALU.mult)
                    V.tensor_tensor(b0, im_, c_, ALU.mult)
                    V.tensor_tensor(b1, re_, s_, ALU.mult).then_inc(sem("inputs_taken"), 1)
                if part == 1:
                    dve.wait_ge(sem("inputs_taken"), k + 1)
                    V.tensor_tensor(zr, a0, a1, ALU.add)
                    link(V.tensor_tensor(zi, b0, b1, ALU.subtract))
                if part == 2:
                    for j in range(2):
                        decay_ = mag_keep[:, 2 * k + j:2 * k + j + 1].to_broadcast([P, S])
                        for z in (zr, zi):
                            ins = V.tensor_tensor_scan(z[:, j, :], decay_, z[:, j, :], 0.0, ALU.mult, ALU.add)
                    ins.then_inc(sem("scanned"), 1)

            def skip(q):
                dve.wait_ge(sem("state_out"), 2 * q + 2)
                V.scalar_tensor_tensor(z_t[:, q, :], u_t[:, q, :], sm["d_skip"][:, q:q + 1], psum[:, Y_BANK[q], 0:S],
                                       ALU.mult, ALU.add).then_inc(sem("skip_added"), 1)

            pair_of = lambda v, w: v[:, 4 * w:4 * w + 4].rearrange("p (h n) -> p h n", n=2)

            def window_max(w):
                link = ordered(dve, "vector")
                if w == 0:
                    dve.wait_ge(mask_arrived, 16)
                dve.wait_ge(sem("scores2_ready"), w + 1)
                after(dve, sem("probs2_turned"), w - 1)
                mk = masked[w % 2]
                V.scalar_tensor_tensor(mk, psum[:, 0:2, 0:384], HEAD2 ** -0.5, mask.unsqueeze(1).to_broadcast([P, 2, 384]),
                                       ALU.mult, ALU.add).then_inc(sem("scores2_taken"), 1)
                dve.wait_ge(sem("scores2_taken"), w + 1)
                m, nm = pair_of(m2, w), pair_of(nm2, w)
                V.tensor_reduce(m[:, :, 0], mk[:, :, 0:P], AX, ALU.max)
                link(V.tensor_reduce(m[:, :, 1], mk[:, :, P:3 * P], AX, ALU.max))
                sink = sm["sinks"][:, 2 * w:2 * w + 2].unsqueeze(2).to_broadcast([P, 2, 2])
                link(V.tensor_tensor(m, m, sink, ALU.max))
                link(V.tensor_scalar(nm, m, -1.0, None, ALU.mult))
                V.tensor_tensor(m, nm, sink, ALU.add).then_inc(sem("max2_ready"), 1)

            def window_out(w):
                link = ordered(dve, "vector")
                c4 = slice(4 * w, 4 * w + 4)
                dve.wait_ge(sem("exp2_ready"), w + 1)
                link(V.tensor_tensor(sum2[:, c4], sum2[:, c4], m2[:, c4], ALU.add))
                link(V.reciprocal(rinv2[:, c4], sum2[:, c4]))
                dve.wait_ge(sem("heads2_ready"), w + 1)
                V.tensor_tensor(merged[:, :, 128 * w:128 * w + 128].rearrange("p t (h d) -> p h t d", d=HEAD2),
                                psum[:, 3, 256:512].rearrange("p (h t d) -> p h t d", h=2, t=T),
                                pair_of(rinv2, w).unsqueeze(3).to_broadcast([P, 2, 2, HEAD2]), ALU.mult).then_inc(sem("attn2_out"), 1)

            def z_lo(half):
                dve.wait_ge(sem("z_hi_ready"), half + 1)
                c4 = slice(4 * half, 4 * half + 4)
                V.tensor_tensor(xlo[:, c4, :], z_t[:, c4, :], xhi[:, c4, :].bitcast(F32), ALU.subtract).then_inc(sem("z_lo_ready"), 1)

            def mixers():
                for n in range(11):
                    k, w = 5 + n, n
                    for part in range(3):
                        unit(k, part)
                    if k % 2:
                        skip((k - 3) // 2)
                    if w < 8:
                        window_max(w)
                    if 1 <= w <= 8:
                        window_out(w - 1)
                    if k == 10:
                        z_lo(0)
                skip(7)
                z_lo(1)

            if has("w_in"):
                residual("down1", 5, state_parameters())
                ada_gains()
                token_norm("norm_mix", 5, sh_m, gs_m)
                project_in()
                mixers()

                def glu_out(i, b):
                    dve.wait_ge(sem(f"glu_out{b}"), 1)
                    dve.wait_ge(tr_ready[b], GROUP_AT["glu"][b] + 1)
                    V.tensor_tensor(merged[:, :, W2 + NW * b:W2 + NW * (b + 1)], tmp[:, b, :, :],
                                    psum[:, 4 + 2 * b:6 + 2 * b, :], ALU.mult).then_inc(tr_free[b], 1)
                    dve.wait_ge(tr_free[b], GROUP_AT["glu"][b] + 1)
                    V.engine_nop().then_inc(sem("merged_ready"), 1)
                run("glu", glu_out)
                dve.wait_ge(sem("merge_squares"), 1)
                rstd_of("merge", None, 6, 4)
                dve.wait_ge(rstd_ready, 6)
                for half in range(2):
                    m_ = merged[:, 1, half * W2:(half + 1) * W2]
                    V.tensor_scalar(m_, m_, rstd[:, 2 + half:3 + half], None, ALU.mult).then_inc(sem("merge_scaled"), 1)
                for q in range(4):
                    group_lo(q % 2, xlo[:, 4 * q:4 * q + 4, :], xhi[:, 4 * q:4 * q + 4, :],
                             sm["g_merged"][:, 4 * q:4 * q + 4], sem("merge_hi"), q + 1)

                def gain_steps(i, pos, name, gain, diag, dst, at):
                    if (i, pos) == (0, at):
                        if name == "down2":
                            dve.wait_ge(sem("ffn2_lo"), 11)
                        for c in range(FC):
                            ins = V.tensor_scalar(diag[:, c * P:(c + 1) * P], ident, gain[:, c:c + 1], None, ALU.mult)
                        ins.then_inc(sem(f"{name}_diagonal"), 1)
                    if (i, pos) == (0, at + 2):
                        dve.wait_ge(sem(f"{name}_rows"), 1)
                        V.tensor_copy(dst, psum[:, 4:8, :].rearrange("p b e -> p (b e)")).then_inc(sem(f"{name}_gain"), 1)
                run("w_out", None, None, lambda i, pos: gain_steps(i, pos, "w_out", gp_m, diag_mix, gain_mix, 2))

                def post_norm(layer, count, gain, signal):
                    for b in range(2):
                        dve.wait_ge(sem(f"{layer}_out{b}"), 2)
                    rstd_of(layer, V.reduce_sum(mean[:, 0:T], ss, AX), count)
                    dve.wait_ge(rstd_ready, count)
                    dve.wait_ge(sem(f"{layer}_gain"), 1)
                    link = ordered(dve, "vector")
                    rows = GATHERED[layer].rearrange("p t n e -> p t (n e)")
                    for t in range(T):
                        link(V.scalar_tensor_tensor(rows[:, t, :], rows[:, t, :], rstd[:, t:t + 1], gain, ALU.mult, ALU.mult))
                        V.tensor_tensor(x_[:, t * D:(t + 1) * D], x_[:, t * D:(t + 1) * D], rows[:, t, :], ALU.add).then_inc(signal, 1)
                post_norm("w_out", 7, gain_mix, sem("x_mixed"))
                dve.wait_ge(sem("x_squares"), 1)
                rstd_of("norm_ffn", V.tensor_copy(mean[:, 0:T], ss[:, :, 0]), 8)
                token_norm("norm_ffn", 8, sh_f, gs_f)

                w = sm["conv2_w"].rearrange("p (k h n j) -> p k h n j", k=3, h=2, j=4)
                flat = conv_.rearrange("p (h e) -> p h e", h=2)

                def tap(i, b, n):
                    k, by = ((1, 1), (0, 2))[n]
                    dve.wait_ge((sem(f"ffn2_base{b}"), sem(f"ffn2_tap{b}"))[n], i + 1)
                    for j in range(4):
                        dst = conv[:, 4 * b + j, by:S]
                        ins = V.scalar_tensor_tensor(dst, tr[b][:, j, 0:S - by], w[:, k, b, i, j:j + 1], dst, ALU.mult, ALU.add)
                    ins.then_inc((sem(f"ffn2_tap{b}"), tr_free[b])[n], 1)

                def prod(i):
                    dve.wait_ge(sem("ffn2_gelu"), i + 1)
                    V.tensor_tensor(flat[:, 0, :], flat[:, 0, :], flat[:, 1, :], ALU.mult).then_inc(sem("ffn2_prod"), 1)

                def lo(i):
                    dve.wait_ge(sem("ffn2_hi"), i + 1)
                    V.tensor_tensor(mlo_.rearrange("p (n e) -> p n e", e=4 * S)[:, i, :], flat[:, 0, :],
                                    mhi_.rearrange("p (n e) -> p n e", e=4 * S)[:, i, :].bitcast(F32),
                                    ALU.subtract).then_inc(sem("ffn2_lo"), 1)
                run("ffn2", None, None, None, tuple((5 + 2 * b + n, lambda i, b=b, n=n: tap(i, b, n)) for b in range(2)
                                                    for n in range(2)) + ((10, prod), (12, lo)))
                run("down2", None, None, lambda i, pos: gain_steps(i, pos, "down2", gp_f, diag_ff, gain_ff, 14))
                post_norm("down2", 9, gain_ff, sem("x_final"))
            if upto != "down2":
                for b in range(2):
                    dve.wait_ge(sem(f"sum_used{b}"), 2 * RES_AT[upto] + 2)
                V.engine_nop().then_inc(sem("x_final"), 1)

        @block.tensor
        def _(pe):
            M = nc.tensor.matmul
            slots = [0]

            def tile_products(layer, tile, b, k0, first, last, nk=KT, width=NW):
                hi, lo = LHS[layer]
                s = slots[0] % RING
                slots[0] += 1
                pe.wait_ge(lo_ready, tile + 1)
                for k in range(nk):
                    wh = whi[:, s, k * width:(k + 1) * width]
                    wl = wlo[:, s, k * width:(k + 1) * width]
                    for t in range(T):
                        xh, xl = (v[:, k0 + k, t * P:(t + 1) * P] for v in (hi, lo))
                        for n, (a, w) in enumerate(((xh, wh), (xh, wl), (xl, wh))):
                            ins = M(acc[b][:, t, 0:width], a, w, start=first and k == 0 and n == 0,
                                    stop=last and k == nk - 1 and n == 2)
                ins.then_inc(tiles_used, 1)

            def turn(b, before, src, signal=None):
                after(pe, tr_free[b], before)
                for j in range(4):
                    for t in range(T):
                        ins = nc.tensor.transpose(tr[b][:, j, t * P:(t + 1) * P], src(t, j), ident)
                ins.then_inc(tr_ready[b], 1)

            def ada_sum(i, at):
                pe.wait_ge(ada_step, i * 16 + (16 * at + 16))
                after(pe, ada_done, i + at)
                for j in range(4):
                    ins = M(psum[:, 6, j:j + 1], adacc_[:, j * P:(j + 1) * P], ones[:, 0:1], start=True, stop=True)
                ins.then_inc(ada_summed, 1)

            carried = []

            def carried_steps(pos):
                for at, step in [c for c in carried if c[0] == pos]:
                    step()
                    carried.remove((at, step))

            def carry(layer, tail, late):
                n = PAIRS[layer] - 1
                if tail and layer in CARRIED_AT:
                    carried.append((CARRIED_AT[layer], lambda: tail(n, 1)))
                elif tail:
                    tail(n, 1)
                for at, step in late:
                    carried.append((at, lambda step=step: step(n)))

            def run(layer, tail=None, extra=None, needs=None, late=()):
                kt = KTILES[layer]
                ada = ADA_AT.get(layer) if has("down1") else None

                def body(i, first):
                    slots[0] = TILE0[layer]
                    for pos in range(2 * kt):
                        b, k = pos // kt, pos % kt
                        if extra:
                            extra(i, pos)
                        for at, step in late:
                            if at == pos and not first:
                                step(i - 1)
                        if first:
                            carried_steps(pos)
                            if needs and pos in needs:
                                needs[pos]()
                        if pos == HOOK and not first:
                            if tail:
                                tail(i - 1, 1)
                            if ada is not None:
                                ada_sum(i - 1, ada)
                        if tail and pos == kt + HOOK:
                            tail(i, 0)
                        if k == 0:
                            after(pe, sem(released(layer, b)), i + 2 * RES_AT.get(layer, 0))
                        tile_products(layer, i * (2 * kt) + (TILE0[layer] + pos), b, KT * k, k == 0, k == kt - 1)
                each_pair(pe, layer, body)
                carry(layer, tail, late)
                if ada is not None:
                    ada_sum(PAIRS[layer] - 1, ada)
                    pe.wait_ge(ada_done, ada + PAIRS[layer])

            def residual(layer, extra=None, needs=None):
                def tail(i, b):
                    pe.wait_ge(sem(f"sum_ready{b}"), i + (2 * RES_AT[layer] + 1))
                    turn(0, GROUP_AT[layer][0] + 2 * i + b, lambda t, j: tmp[:, b, t, j * P:(j + 1) * P])
                run(layer, tail if RESIDUAL[layer] else None, extra, needs)

            def gated(layer, needs):
                def tail(i, b):
                    if b:
                        pe.wait_ge(sem(f"{layer}_prod"), i + 1)
                        turn(0, i + GROUP_AT[layer][0], lambda t, j: tmp[:, 1, t, j * P:(j + 1) * P])
                run(layer, tail, None, needs)

            def groups_in(name, layer):
                n = sum(GROUP_AT[name][0:1]) + dict((g[0], g[1]) for g in GROUPS)[name]
                return {0: lambda: pe.wait_ge(tr_free[0], n - 1),
                        KTILES[layer] - 2: lambda: pe.wait_ge(tr_free[0], n)}

            def input_ready(name, signal=None):
                for b in range(2):
                    n = GROUP_AT[name][b] + dict((g[0], g[1 + b]) for g in GROUPS)[name]
                    after(pe, tr_free[b], n)

            pe.wait_ge(small_arrived, 16)
            pe.wait_ge(ones_ready, 1)
            pe.wait_ge(x_arrived, 16)
            for q in range(4):
                turn(q % 2, q // 2, lambda t, j: x[:, t, q, j * P:(j + 1) * P])
            input_ready("first")
            run("qkv")
            pe.wait_ge(s_rot, 1)
            banks = [acc[0].rearrange("p t (h s) -> p (t h) s", s=S), acc[1].rearrange("p t (h s) -> p (t h) s", s=S),
                     tr[0], tr[1], acc[0].rearrange("p t (h s) -> p (t h) s", s=S)]
            for gi in range(5):
                if gi == 4:
                    pe.wait_ge(s_qe_a, 1)
                for j in range(4):
                    for t in range(T):
                        ins = nc.tensor.transpose(banks[gi][:, j, t * P:(t + 1) * P], rot[:, t, 4 * gi + j, :], ident)
                ins.then_inc(s_qt, 1)
            pe.wait_ge(s_qe_a, 3)
            pe.wait_ge(s_qe_v, 2)

            def scores(u):
                after(pe, s_exp, u - 1)
                for h in range(2):
                    for t in range(T):
                        ins = M(psum[:, 2 * (u % 2) + h, t * S:(t + 1) * S], qk_t[:, 2 * u + h, t * P:(t + 1) * P],
                                qk_t[:, QH + u // 2, :], start=True, stop=True)
                ins.then_inc(s_sc, 1)
            scores(0)
            for u in range(8):
                if u < 7:
                    scores(u + 1)
                pe.wait_ge(s_pn, u + 1)
                after(pe, s_pte, u)
                for h in range(2):
                    for k in range(T):
                        for t in range(T):
                            ins = nc.tensor.transpose(tr[0][:, 2 * h + k, t * P:(t + 1) * P],
                                                      probs[:, u % 2, 2 * h + t, k * P:(k + 1) * P], ident)
                ins.then_inc(s_pt, 1)
                pe.wait_ge(s_pte, u + 1)
                after(pe, s_ol, u - 1)
                for h in range(2):
                    for k in range(T):
                        ins = M(psum[:, 6 + u % 2, h * S:(h + 1) * S], qkv_h[:, k, QH + KVH + u // 2, :],
                                probs_t[:, u % 2, h, k, :], start=k == 0, stop=k == T - 1)
                ins.then_inc(s_pv, 1)
            pe.wait_ge(s_ol, 8)
            residual("w_o")
            gated("ffn0", groups_in("w_o", "ffn0"))
            residual("down0", None, groups_in("ffn0", "down0"))

            def recurrent_in():
                def tail(i, b):
                    c = 2 * i + b
                    pe.wait_ge(sem(f"rnn_in_out{b}"), i + 1)
                    turn(0, GROUP_AT["rnn_in"][0] + c, lambda t, j: tmp[:, b, t, j * P:(j + 1) * P])

                def unit(i, pos):
                    if i < 2 or pos % 2:
                        return
                    u = 8 * (i - 2) + pos // 2
                    blk, half = u // 2, u % 2
                    pe.wait_ge(gate_arrived[blk % 2], 16 * (blk // 2 + 1))
                    pe.wait_ge(s_conv, 3 * ((2 * blk + 1) // 4 + 1))
                    if u:
                        pe.wait_ge(s_drive, u)
                        pe.wait_ge(s_tanh, 2 * u)
                    for d in range(2):
                        for g in range(2):
                            for k in range(2):
                                ins = M(gates[:, d, g, :], gate_ws[blk % 2][:, k, d, g, half * P:(half + 1) * P],
                                        xc[:, 2 * blk + k, :], start=k == 0, stop=k == 1)
                    ins.then_inc(s_gate, 1)
                run("rnn_in", tail, unit, groups_in("down0", "rnn_in"))
            recurrent_in()
            residual("rnn_out", None, {2 * k: lambda k=k: pe.wait_ge(s_hlo, k + 1) for k in range(4)})
            gated("ffn1", groups_in("rnn_out", "ffn1"))

            def token_norm(name):
                pe.wait_ge(sem(f"{name}_normed"), 2)
                for q in range(4):
                    turn(q % 2, GROUP_AT[name][q % 2] + q // 2, lambda t, j: normed[:, t, (4 * q + j) * P:(4 * q + j + 1) * P])
                input_ready(name)

            def turned_matrices(i, pos):
                if i == 0 and pos in (23, 25):
                    b = (pos - 23) // 2
                    pe.wait_ge(sem("parameter_steps"), PARAMETER_STEPS["input_matrix"])
                    after(pe, tr_free[0], GROUP_AT["ssm_b"][0] + b)
                    for j in range(8):
                        ins = nc.tensor.transpose(tr[0].rearrange("p c s -> p (c s)")[:, j * P:(j + 1) * P],
                                                  bd[b].rearrange("p c e -> p (c e)")[:, j * P:(j + 1) * P], ident)
                    ins.then_inc(tr_ready[0], 1)

            def inputs(k):
                pe.wait_ge(tr_free[0], GROUP_AT["w_in"][0] + (k // 4 + 1))
                if k == 0:
                    pe.wait_ge(sem("matrices_back"), 32)
                after(pe, sem("inputs_taken"), k)
                for b in range(2):
                    for jj in range(2):
                        j = 2 * (k % 2) + jj
                        r = slice(32 * j, 32 * j + 32)
                        ins = M(psum[:, 6 + jj, b * S:(b + 1) * S], bb_t[b][r, k // 2, :], u_t[r, k // 2, :], start=True, stop=True)
                ins.then_inc(sem("inputs_ready"), 1)

            def outputs(k):
                pe.wait_ge(sem("parts_ready"), k + 1)
                if k % 2 == 0:
                    after(pe, sem("skip_added"), {1: 1, 2: 0}.get(k // 2, k // 2 - 1))
                bufs = unit_bufs[k % 2]
                for jj in range(2):
                    j = 2 * (k % 2) + jj
                    for n, (c_, part) in enumerate(((c_re, bufs[2]), (nc_im, bufs[4]))):
                        ins = M(psum[32 * j:32 * j + 32, Y_BANK[k // 2], 0:S], c_[:, 2 * k + jj, :], part[:, jj, :],
                                start=n == 0, stop=n == 1)
                ins.then_inc(sem("state_out"), 1)

            def project_in():
                def turn_two(c, half):
                    n = 2 * c + half
                    pe.wait_ge(sem(f"w_in_out{c % 2}"), c // 2 + 1)
                    pe.wait_ge(tr_free[0], GROUP_AT["w_in"][0] + n)
                    for j in range(2):
                        for t in range(T):
                            ins = nc.tensor.transpose(psum[:, 5, j * S + t * P:j * S + (t + 1) * P],
                                                      tmp[:, c % 2, t, (2 * half + j) * P:(2 * half + j + 1) * P], ident)
                    ins.then_inc(tr_ready[0], 1)

                def extra(i, pos):
                    for half in range(2):
                        for b in range(2):
                            if pos == TURN_AT[half] + 8 * (1 - b) and (b == 0 or i):
                                turn_two(2 * i if not b else 2 * i - 1, half)
                    if (i, pos) in STREAM_UNITS:
                        k = STREAM_UNITS[(i, pos)]
                        if k > 1:
                            outputs(k - 2)
                        inputs(k)
                run("w_in", None, extra)
                pe.wait_ge(sem("w_in_out0"), 2)
                for n in range(4):
                    if n >= 2:
                        turn_two(3, n - 2)
                    slots[0] = n
                    tile_products("w_in_kv", TILE0["w_in_kv"] + n, 0, 4 * n, n == 0, n == 3, nk=4, width=256)
                pe.wait_ge(sem("w_in_kv_out"), 1)
                pe.wait_ge(tr_free[0], GROUP_AT["w_in_k"][0])
                for t in range(T):
                    ins = nc.tensor.transpose(psum[:, 5, t * P:(t + 1) * P], kv[:, t, 0:P], ident)
                ins.then_inc(tr_ready[0], 1)
                outputs(3)
                inputs(5)
                pe.wait_ge(tr_free[0], GROUP_AT["w_in_k"][0] + 1)

            def window_scores(w):
                after(pe, sem("scores2_taken"), w)
                for h in range(2):
                    rows = slice(HEAD2 * h, HEAD2 * h + HEAD2)
                    for t in range(T):
                        k = S if t else P
                        ins = M(psum[:, h, t * P:t * P + k], q2_t[rows, w, t * P:(t + 1) * P], k2_t[rows, 0:k],
                                start=True, stop=True)
                ins.then_inc(sem("scores2_ready"), 1)

            def window_heads(w):
                pe.wait_ge(sem("exp2_ready"), w + 1)
                after(pe, sem("attn2_out"), w)
                flat = psum[:, 2:4, :].rearrange("p b (n q) -> p (b n) q", q=P)
                for h in range(2):
                    for n in range(3):
                        ins = nc.tensor.transpose(flat[:, 3 * h + n, :], masked[w % 2][:, h, n * P:(n + 1) * P], ident)
                ins.then_inc(sem("probs2_turned"), 1)
                pe.wait_ge(sem("turned2_ready"), w + 1)
                for h in range(2):
                    o = lambda t: psum[:, 3, 256 + (2 * h + t) * HEAD2:256 + (2 * h + t + 1) * HEAD2]
                    v = lambda t: kv[:, t, P + HEAD2 * h:P + HEAD2 * (h + 1)]
                    M(o(0), turned[w % 2][:, h, 0, :], v(0), start=True, stop=True)
                    M(o(1), turned[w % 2][:, h, 1, :], v(0), start=True, stop=False)
                    ins = M(o(1), turned[w % 2][:, h, 2, :], v(1), start=False, stop=True)
                ins.then_inc(sem("heads2_ready"), 1)

            def mixers():
                for n in range(11):
                    k, w = 5 + n, n
                    if n:
                        outputs(k - 2)
                        inputs(k)
                    if w < 8:
                        window_scores(w)
                    if 1 <= w <= 8:
                        window_heads(w - 1)
                outputs(14)
                outputs(15)
                pe.wait_ge(sem("z_lo_ready"), 2)
                pe.wait_ge(sem("skip_added"), 8)

            def gain_rows(name, diag):
                pe.wait_ge(sem(f"{name}_diagonal"), 1)
                for c in range(FC):
                    ins = M(psum[:, 4 + c // 4, (c % 4) * P:(c % 4 + 1) * P], ones, diag[:, c * P:(c + 1) * P], start=True, stop=True)
                ins.then_inc(sem(f"{name}_rows"), 1)

            if has("w_in"):
                residual("down1", turned_matrices, groups_in("ffn1", "down1"))
                token_norm("norm_mix")
                project_in()
                mixers()
                run("glu")
                for b in range(2):
                    after(pe, tr_free[b], GROUP_AT["glu"][b])
                    for j in range(4):
                        for t in range(T):
                            ins = nc.tensor.transpose(psum[:, 4 + 2 * b + t, j * P:(j + 1) * P], z_t[:, 4 * b + j, t * P:(t + 1) * P], ident)
                    ins.then_inc(tr_ready[b], 1)
                pe.wait_ge(sem("merge_scaled"), 4)
                for q in range(4):
                    turn(q % 2, GROUP_AT["merge"][q % 2] + q // 2, lambda t, j: merged[:, t, (4 * q + j) * P:(4 * q + j + 1) * P])
                input_ready("merge")
                run("w_out", None, lambda i, pos: (i, pos) == (0, 4) and gain_rows("w_out", diag_mix))
                pe.wait_ge(sem("w_out_gain"), 1)
                token_norm("norm_ffn")

                def up_turned(i, v):
                    pe.wait_ge(sem(f"ffn2_copied{v}"), i + 1)
                    turn(v, i + GROUP_AT["ffn2"][v], lambda t, j: tmp[:, v, t, j * P:(j + 1) * P])
                run("ffn2", late=((3, lambda i: up_turned(i, 0)), (4, lambda i: up_turned(i, 1))))

                def rows_of_down2(i, pos):
                    if (i, pos) == (0, 16):
                        gain_rows("down2", diag_ff)
                run("down2", None, rows_of_down2, {0: lambda: pe.wait_ge(sem("ffn2_lo"), 10),
                                                   20: lambda: pe.wait_ge(sem("ffn2_lo"), 11)})
def _tiles(w):
    k, n = w.shape
    return w.reshape(k // (KT * P), KT, P, n // NW, NW).transpose(3, 0, 2, 1, 4).reshape(n // NW, k // (KT * P), P, TW)

def _cols(v):
    return v.reshape(-1, P).T

def _head_order(n, per):
    return np.arange(n * per).reshape(2, n // 2, per).transpose(1, 0, 2).reshape(-1)

def pack(**a):
    a = {k: np.asarray(v) for k, v in a.items()}
    flat = lambda w: w.reshape(-1, P, TW)
    both = lambda g, u: np.stack([_tiles(g), _tiles(u)], axis=1)
    order2 = _head_order(QH2, HEAD2)
    w_in = a["w_in_2"][0]
    w_in_uq = np.concatenate([w_in[:, W2 + 256:], w_in[:, :W2][:, order2]], axis=1)
    w_in_kv = w_in[:, W2:W2 + 256].reshape(4, 4, P, 256).transpose(0, 2, 1, 3)
    w_up = a["w_up_2"][0]
    stream = [_tiles(a["attn_w_qkv"][0]), _tiles(a["attn_w_o"][0]),
              both(a["ffn_w_gate"][0], a["ffn_w_up"][0]), _tiles(a["ffn_w_down"][0]),
              _tiles(a["rnn_w_in"][0]), _tiles(a["rnn_w_out"][0]),
              both(a["ffn_w_gate"][1], a["ffn_w_up"][1]), _tiles(a["ffn_w_down"][1]),
              _tiles(w_in_uq), w_in_kv, _tiles(a["w_glu_2"][0]),
              _tiles(np.concatenate([a["w_out_2"][0][:W2][order2], a["w_out_2"][0][W2:]])),
              both(w_up[:, :D_FF], w_up[:, D_FF:]), _tiles(a["w_down_2"][0])]
    weights = np.concatenate([flat(w) for w in stream])
    gates = np.stack([a["rnn_w_a"][0], a["rnn_w_i"][0]], axis=1)
    gates = gates.reshape(2, 2, RNN_BLOCKS, 2, P, RNN_W).transpose(2, 4, 3, 0, 1, 5).reshape(RNN_BLOCKS, P, 2048)
    by_state = lambda v: v.reshape(ST, P).T
    small = {"g_mix0": _cols(a["norm_mix"][0]), "g_mix1": _cols(a["norm_mix"][1]),
             "g_ffn0": _cols(a["norm_ffn"][0]), "g_ffn1": _cols(a["norm_ffn"][1]),
             "conv_w": _cols(a["rnn_conv_w"][0]), "conv_b": _cols(a["rnn_conv_b"][0]),
             "b_a": _cols(a["rnn_b_a"][0]), "b_i": _cols(a["rnn_b_i"][0]), "lam": _cols(a["rnn_lambda"][0]),
             "c": _cols(a["c_2"]), "b_ada": _cols(a["b_ada_2"][0]), "g_pre_mix": _cols(a["g_pre_mix_2"][0]),
             "g_post_mix": _cols(a["g_post_mix_2"][0]), "g_pre_ffn": _cols(a["g_pre_ffn_2"][0]),
             "g_post_ffn": _cols(a["g_post_ffn_2"][0]),
             "g_merged": _cols(np.concatenate([a["g_attn_out_2"][0][order2], a["g_ssm_out_2"][0]])),
             "d_skip": _cols(a["ssm_d_2"][0].reshape(-1)), "conv2_w": _cols(a["conv_w_2"][0]),
             "conv2_b": _cols(a["conv_b_2"][0]), "lam_re": by_state(a["lam_re_2"][0]),
             "lam_im": by_state(a["lam_im_2"][0]), "log_step": by_state(np.repeat(a["log_step_2"][0], STATE)),
             "sinks": np.broadcast_to(a["attn_sinks_2"][0][_head_order(QH2, 1)], (P, QH2)),
             "ident": np.eye(P, dtype=np.float32)}
    small = np.concatenate([small[k] for k, _ in SMALL], axis=1)
    pos = np.arange(S)
    freqs = np.float32(10000.0) ** (-np.arange(FREQS, dtype=np.float32) / np.float32(FREQS))
    ang = np.stack([(pos // 64).astype(np.float32)[:, None] * freqs, (pos % 64).astype(np.float32)[:, None] * freqs], axis=1)
    table = lambda f: f(ang).astype(np.float32).reshape(T, P, 64).transpose(1, 0, 2).reshape(P, 128)
    rope = np.concatenate([table(np.cos), table(np.sin), np.broadcast_to(a["attn_q_gain"][0], (P, HEAD)),
                           np.broadcast_to(a["attn_k_gain"][0], (P, HEAD))], axis=1)
    b = lambda v: v[0].reshape(ST, P, GROUP).transpose(1, 0, 2).reshape(P, -1)
    c = lambda v: v[0].transpose(0, 2, 1).reshape(ST, P, GROUP).transpose(1, 0, 2).reshape(P, -1)
    ssm = np.concatenate([b(a["ssm_b_re_2"]), b(a["ssm_b_im_2"]), c(a["ssm_c_re_2"]), c(a["ssm_c_im_2"])], axis=1)
    q, k = np.arange(P)[:, None], np.arange(S)[None, :]
    own = np.where(q >= k[:, :P], 0.0, NEG)
    band = np.where((k > q) & (k <= q + WINDOW), 0.0, NEG)
    mask = np.concatenate([own, band], axis=1).astype(np.float32)
    return {"x": a["x"][0], "weights": weights, "ada_w": flat(_tiles(a["w_ada_2"][0])), "gate_w": gates,
            "small": small, "rope": rope, "ssm": ssm, "mask": mask}


_INS = ("x", "weights", "ada_w", "gate_w", "small", "rope", "ssm", "mask")


def kernel(**inputs):
    import concourse.bacc as bacc
    from concourse.bass_utils import run_bass_kernel_spmd

    arrays = {k: np.ascontiguousarray(v) for k, v in pack(**inputs).items()}
    nc = bacc.Bacc("TRN2", target_bir_lowering=False, num_devices=1)
    args = [nc.dram_tensor(k, arrays[k].shape, mybir.dt.from_np(arrays[k].dtype), kind="ExternalInput").ap() for k in _INS]
    out = nc.dram_tensor("out_0", (S, D), F32, kind="ExternalOutput").ap()
    build(nc, *args, out)
    r = run_bass_kernel_spmd(nc, [arrays], core_ids=[0])
    return r.results[0]["out_0"].reshape(1, S, D)
```

```python
from contextlib import ExitStack

import numpy as np
import concourse.bass as bass
from concourse import mybir

F32 = mybir.dt.float32
F32R = mybir.dt.float32r
ACT = mybir.ActivationFunctionType
ALU = mybir.AluOpType
AX = mybir.AxisListType.X

P = 128
D = 2048
S = 256
T = S // P
FC = D // P
NW = 512
KT = 2
TW = KT * NW
RING = 4
D_FF = 5632
FFC = D_FF // P
EPS = 1e-6
HEAD = 128
QH, KVH = 16, 4
FREQS = 32
RNN_BLOCKS, RNN_W = 8, 256
HALF = 2
LRU_C = 8.0
HEAD2 = 64
QH2, KVH2 = 16, 2
W2 = 1024
WINDOW = 128
GROUP, STATE = 16, 64
ST = 32
ADA_CHUNKS = 6 * D // NW
NEG = -1e30

LAYERS = [("qkv", 3, 8), ("w_o", 2, 8), ("ffn0", 11, 8), ("down0", 2, 22), ("rnn_in", 4, 8),
          ("rnn_out", 2, 8), ("ffn1", 11, 8), ("down1", 2, 22), ("w_in", 2, 8), ("w_in_kv", 0, 4),
          ("glu", 1, 4), ("w_out", 2, 8), ("ffn2", 11, 8), ("down2", 2, 22)]
TILE0, CHUNK0, CHUNK1 = {}, {}, {}
_n = _e = _o = 0
for _name, _pairs, _kt in LAYERS:
    TILE0[_name], CHUNK0[_name], CHUNK1[_name] = _n, _e, _o
    _n += max(1, 2 * _pairs) * _kt
    _e += max(1, _pairs)
    _o += _pairs
TILES = _n
PAIRS = {a: b for a, b, _ in LAYERS}
KTILES = {a: c for a, _, c in LAYERS}
GROUPS = [("first", 2, 2), ("w_o", 4, 0), ("ffn0", 11, 0), ("down0", 4, 0), ("rnn_in", 8, 0),
          ("rnn_out", 4, 0), ("ffn1", 11, 0), ("ssm_b", 2, 0), ("norm_mix", 2, 2), ("w_in", 8, 0),
          ("w_in_k", 1, 0), ("glu", 1, 1), ("merge", 2, 2), ("norm_ffn", 2, 2), ("ffn2", 11, 11)]
GROUP_AT = {}
_a = _b = 0
for _name, _x, _y in GROUPS:
    GROUP_AT[_name] = (_a, _b)
    _a, _b = _a + _x, _b + _y

NORM_AT = {name: n + 1 for n, name in enumerate(
    ("first", "w_o", "down0", "rnn_out", "down1", "merge", "w_out", "norm_ffn", "down2"))}
PARAMETER_STEPS = {"angle_ready": 1, "input_matrix": 2, "output_matrix": 3, "e_ready": 4}
SETUP_STEPS = {"lam_abs": 1, "lam_exp": 2, "c_ready": 3, "dt_ready": 4, "sines_ready": 5}
RES_AT = {name: n for n, name in enumerate(("w_o", "down0", "rnn_out", "down1"))}

SMALL = [("g_mix0", 16), ("g_mix1", 16), ("g_ffn0", 16), ("g_ffn1", 16), ("conv_w", 64),
         ("conv_b", 16), ("b_a", 32), ("b_i", 32), ("lam", 32), ("c", 16), ("b_ada", 96),
         ("g_pre_mix", 16), ("g_post_mix", 16), ("g_pre_ffn", 16), ("g_post_ffn", 16),
         ("g_merged", 16), ("d_skip", 8), ("conv2_w", 264), ("conv2_b", 88), ("lam_re", 32),
         ("lam_im", 32), ("log_step", 32), ("sinks", 16), ("ident", 128)]
SMALL_AT = {}
_n = 0
for _name, _w in SMALL:
    SMALL_AT[_name] = (_n, _w)
    _n += _w
NSMALL = _n
HOOK = 3
CARRIED_AT = {"w_o": HOOK, "ffn0": HOOK, "down0": HOOK, "rnn_in": 1, "rnn_out": HOOK, "ffn1": HOOK}


def build(nc, x_in, weights, ada_w, gate_w, small_in, rope_in, ssm_in, mask_in, out):
    ctx = ExitStack()
    with ctx:
        sems = {}

        def sem(name):
            if name not in sems:
                sems[name] = ctx.enter_context(nc.semaphore(name))
            return sems[name]

        cursor = [16512]

        def place(name, cols, dt=F32, at=None):
            if at is None:
                at = cursor[0]
                cursor[0] += 4 * cols
            return nc.alloc_sbuf_tensor_at(name, [P, cols], dt, offset=at)[:, :], at

        def shaped(ap, pattern, **kw):
            return ap.rearrange(pattern, **kw)

        raw_, _ = place("raw", RING * TW)
        whi_, _ = place("w_hi", RING * TW, F32R)
        wlo_, _ = place("w_lo", RING * TW, F32R)
        x_, _ = place("x_tok", T * D)
        _, xt_at = place("xt_region", 2 * FC * S)
        xhi_, _ = place("xt_hi", FC * S, F32R, at=xt_at)
        xlo_, _ = place("xt_lo", FC * S, F32R, at=xt_at + 4 * FC * S)
        sc_, _ = place("scratch", 2 * FC * S, at=xt_at)
        _, mid_at = place("mid_region", 2 * FFC * S)
        mhi_, _ = place("mid_hi", FFC * S, F32R, at=mid_at)
        mlo_, _ = place("mid_lo", FFC * S, F32R, at=mid_at + 4 * FFC * S)
        mid_, _ = place("mid", 2 * FFC * S, at=mid_at)
        tmp_, _ = place("tmp", 2 * T * NW)
        small_, _ = place("small", NSMALL)
        ones_, _ = place("ones", P)
        adacc_, ada_at = place("ada_acc", NW)
        araw_, _ = place("ada_raw", 2 * TW)
        conv_, _ = place("conv_buf", 4 * 2 * S, at=ada_at)
        adat_, _ = place("ada_t", 96)
        stat_, _ = place("stat", 48)
        assert cursor[0] <= 229344, cursor

        raw = shaped(raw_, "p (r e) -> p r e", r=RING)
        whi = shaped(whi_, "p (r e) -> p r e", r=RING)
        wlo = shaped(wlo_, "p (r e) -> p r e", r=RING)
        x = shaped(x_, "p (t n e) -> p t n e", t=T, e=NW)
        xhi = shaped(xhi_, "p (c s) -> p c s", s=S)
        xlo = shaped(xlo_, "p (c s) -> p c s", s=S)
        mhi = shaped(mhi_, "p (c s) -> p c s", s=S)
        mlo = shaped(mlo_, "p (c s) -> p c s", s=S)
        tmp = shaped(tmp_, "p (b t e) -> p b t e", b=2, t=T)
        araw = shaped(araw_, "p (r k e) -> p r k e", r=2, k=KT)
        conv = shaped(conv_, "p (c s) -> p c s", s=S)
        sm = {k: small_[:, a:a + w] for k, (a, w) in SMALL_AT.items()}
        ident = sm["ident"]
        ones = ones_
        ss = stat_[:, 0:8].rearrange("p (t n) -> p t n", t=T)
        mean = stat_[:, 8:12]
        root = stat_[:, 12:16]
        rstd = stat_[:, 16:20]
        c_act = stat_[:, 20:36]
        mid = lambda a, n: mid_[:, a:a + n]
        scr = lambda a, n: sc_[:, a:a + n]

        psum = nc.alloc_psum_tensor("psum", [P, 8, NW], F32)
        acc = [psum[:, 2 * b:2 * b + 2, :] for b in range(2)]
        tr = [psum[:, 4 + 2 * b:6 + 2 * b, :].rearrange("p b (c s) -> p (b c) s", s=S) for b in range(2)]

        raw_arrived = [sem(f"raw_arrived{s}") for s in range(RING)]
        hi_ready, lo_ready, tiles_used = sem("hi_ready"), sem("lo_ready"), sem("tiles_used")
        tr_ready = [sem("tr_ready0"), sem("tr_ready1")]
        tr_free = [sem("tr_free0"), sem("tr_free1")]
        small_arrived, stored = sem("small_arrived"), sem("stored")
        x_arrived = [sem("x_arrived0"), sem("x_arrived1")]
        ones_ready = sem("ones_ready")
        ada_arrived = [sem("ada_arrived0"), sem("ada_arrived1")]
        ada_step, ada_summed, ada_done = sem("ada_step"), sem("ada_summed"), sem("ada_done")
        rstd_ready = sem("rstd_ready")

        def after(eng, what, value):
            if not isinstance(value, int) or value > 0:
                eng.wait_ge(what, value)

        steps_taken = {"vector": 0, "gpsimd": 0}

        def ordered(eng, name):
            what = sem(f"{name}_steps")

            def link(instruction):
                steps_taken[name] += 1
                instruction.then_inc(what, 1)
                eng.wait_ge(what, steps_taken[name])
            return link

        def each_pair(eng, layer, body):
            n = PAIRS[layer]
            if layer in ("qkv", "rnn_in"):
                for i in range(n):
                    body(i, i == 0)
                return
            body(0, True)
            if n == 2:
                body(1, False)
            elif n > 2:
                with eng.Fori(1, n) as i:
                    body(i, False)

        ADA_AT = {"ffn0": 0, "rnn_out": 11, "ffn1": 13}
        ADA_POS = range(4, 12)

        qkv = mid(0, 6144).rearrange("p (t n e) -> p t n e", t=T, e=NW)
        qkv_h = mid(0, 6144).rearrange("p (t h d) -> p t h d", t=T, d=HEAD)
        rope = mid(6144, 512)
        tabs = mid(6656, 1024).rearrange("p (k t d) -> p k t d", k=4, t=T)
        rot = mid(7680, 5120).rearrange("p (t h d) -> p t h d", t=T, d=HEAD)
        swapped = [mid(17920 + 1024 * i, 1024).rearrange("p (t h d) -> p t h d", t=T, d=HEAD) for i in range(2)]
        squares = [mid(19968 + 1024 * i, 1024).rearrange("p (t h d) -> p t h d", t=T, d=HEAD) for i in range(2)]
        qk_t = mid(12800, 5120).rearrange("p (h s) -> p h s", s=S)
        ohi_, _ = place("o_hi", FC * S, F32R, at=mid_at + 4 * 7680)
        olo_, _ = place("o_lo", FC * S, F32R, at=mid_at + 4 * 17920)
        ohi = shaped(ohi_, "p (c s) -> p c s", s=S)
        olo = shaped(olo_, "p (c s) -> p c s", s=S)
        probs = scr(6144, 2048).rearrange("p (b i k) -> p b i k", b=2, k=S)
        probs_t = scr(0, 2048).rearrange("p (b h k q) -> p b h k q", b=2, h=2, k=T)
        ssq = mid(22016, 40)
        rq = mid(22016 + 40, 40)
        rqs = mid(22016 + 80, 40)
        mx = mid(22016 + 120, 32)
        nmx = mid(22016 + 152, 32)
        sums = mid(22016 + 184, 32)
        rinv = mid(22016 + 216, 32)
        s_rot, s_sq, s_rq = sem("rotated"), sem("squares_ready"), sem("head_root")
        s_qt, s_qe = sem("qk_transposed"), sem("qk_out")
        HEADS_AT = {"rotate": 8, "add": 10, "sum": 11, "turn": 13}
        K_CHUNK = 4
        s_sc, s_nm, s_exp, s_pn = sem("scores_ready"), sem("max_ready"), sem("exp_ready"), sem("probs_ready")
        s_pt, s_pte, s_pv, s_oh, s_ol = (sem("probs_turned"), sem("probs_t_ready"), sem("heads_ready"),
                                         sem("o_hi_ready"), sem("o_lo_ready"))
        s_rope = sem("rope_arrived")

        xb = mid(0, 4096).rearrange("p (c s) -> p c s", s=S)
        y_gelu = mid(4096, 4096).rearrange("p (c s) -> p c s", s=S)
        xc = mid(8192, 4096).rearrange("p (c s) -> p c s", s=S)
        hhi_, _ = place("h_hi", FC * S, F32R, at=mid_at + 4 * 8192)
        hlo_, _ = place("h_lo", FC * S, F32R, at=mid_at + 4 * 4096)
        hhi = shaped(hhi_, "p (c s) -> p c s", s=S)
        hlo = shaped(hlo_, "p (c s) -> p c s", s=S)
        of_batch = lambda at: mid(at, 2048).rearrange("p (c d s) -> p c d s", d=2, s=S)
        half_tanh = [of_batch(12288), of_batch(0)]
        decay = [of_batch(14336), of_batch(18432)]
        drive = [of_batch(16384), of_batch(2048)]
        gw_shape = lambda ap: ap.rearrange("p (k d g j) -> p k d g j", k=2, d=2, g=2)
        gate_ws = [gw_shape(mid(20480, 2048)), gw_shape(araw_)]
        gates = psum[:, 6:8, :].rearrange("p d (g s) -> p d g s", g=2)
        lam_tmp = [mid(22016 + 32 * i, 32) for i in range(4)]
        neg4sp = sm["lam"]
        gate_arrived = [sem("gate_w_arrived0"), sem("gate_w_arrived1")]
        s_xb, s_base, s_conv = sem("xb_ready"), sem("conv_base"), sem("conv_ready")
        s_gate, s_sig, s_tanh, s_ig, s_drive = (sem("gates_summed"), sem("r_ready"), sem("tanh_ready"),
                                                sem("i_ready"), sem("drive_started"))
        s_unit, s_sqrt, s_mixed, s_hhi, s_hlo = (sem("unit_ready"), sem("sqrt_ready"), sem("mixed_ready"),
                                                 sem("h_hi_ready"), sem("h_lo_ready"))
        s_decay, s_below, s_scaled, s_scan = (sem("decay_ready"), sem("below_one"), sem("drive_scaled"),
                                              sem("batch_scanned"))
        s_lam = sem("lambda_ready")
        BATCH_AT = {"root": 8, "scan": 12, "hi": 14, "lo": 15}
        LAST_BATCH_AT = {"mix": 1, "hi": 2, "lo": 3}
        UNITS = 16

        UNITS2 = ST // 2
        by_tile = lambda ap, e: ap.rearrange("p (c e) -> p c e", e=e)
        q2_t, k2_t, u_t = by_tile(mid(0, 2048), S), mid(2048, S), by_tile(mid(2816, 2048), S)
        kv = mid(2304, 512).rearrange("p (t e) -> p t e", t=T)
        z_t = u_t
        merged = mid(4864, 4096).rearrange("p (t e) -> p t e", t=T)
        bb_t = [by_tile(mid(8960 + 1024 * i, 1024), P) for i in range(2)]
        c_re, nc_im = (by_tile(mid(11008 + 1024 * i, 1024), 2 * GROUP) for i in range(2))
        tables = [mid(13056 + 1024 * i, 1024).rearrange("p (f c s) -> p f c s", f=2, s=S) for i in range(4)]
        unit_bufs = [[by_tile(mid(17152 + 2048 * i + 512 * n, 512), S) for n in range(4)]
                     + [by_tile(merged[:, i, W2 + 512 * n:W2 + 512 * n + 512], S) for n in range(2)] for i in range(2)]
        normed = mid(17152, 4096).rearrange("p (t e) -> p t e", t=T)
        shifted = [by_tile(mid(4864 + 1024 * i, 1024), S) for i in range(2)]
        m2, nm2, sum2, rinv2 = (mid(21248 + 32 * i, 32) for i in range(4))
        squares_out = mid(8960, 4096)
        ssm_raw = scr(0, 2048)
        b_raw = [by_tile(scr(512 * i, 512), GROUP) for i in range(2)]
        c_raw = [by_tile(scr(1024 + 512 * i, 512), GROUP) for i in range(2)]
        bd = [by_tile(scr(2048 + 1024 * i, 1024), 2 * GROUP) for i in range(2)]
        c_made = bd
        bb_made = scr(5120, 2048)
        e1 = [by_tile(scr(512 * i, 512), 16) for i in range(2)]
        e16 = [by_tile(scr(1024 + 512 * i, 512), 16) for i in range(2)]
        cm_tmp = [scr(4096 + 256 * i, 256) for i in range(4)]
        table_out = [scr(2048 + 1024 * i, 1024) for i in range(2)]
        table_tmp = scr(4096, 512)
        st_tmp = [scr(7168 + 32 * i, 32) for i in range(32)]
        mag_keep = sm["lam_re"]
        mask = conv_[:, 0:384]
        masked = [conv_[:, 384 + 768 * i:1152 + 768 * i].rearrange("p (h k) -> p h k", k=384) for i in range(2)]
        turned = [tmp_[:, 768 * i:768 * i + 768].rearrange("p (h n q) -> p h n q", h=2, n=3) for i in range(2)]
        mixed = mid(0, 4096).rearrange("p (t n e) -> p t n e", t=T, e=NW)
        mixed_ff = scr(0, 4096).rearrange("p (t n e) -> p t n e", t=T, e=NW)
        gain_mix, gain_ff = mid(13056, D), scr(4096, D)
        diag_mix, diag_ff = mid(15104, D), conv_
        sh_m, gs_m, gp_m, sh_f, gs_f, gp_f = (adat_[:, 16 * i:16 * i + 16] for i in range(6))
        ssm_arrived, mask_arrived, ada_ready = sem("ssm_arrived"), sem("mask_arrived"), sem("ada_gains")
        table_store = nc.dram_tensor("table_store", [UNITS2, P, 1024], F32, kind="Internal").ap()
        matrix_store = nc.dram_tensor("matrix_store", [2, P, 2048], F32, kind="Internal").ap()
        table_arrived = [sem(f"table_arrived{i}") for i in range(4)]
        STREAM_UNITS = {(0, 14): 0, (1, 2): 1, (1, 6): 2, (1, 10): 3, (1, 14): 4}
        TURN_AT = (HOOK, HOOK + 3)
        Y_BANK = [4, 4] + [4 + (q + 1) % 2 for q in range(2, 8)]

        LHS = {"qkv": (xhi, xlo), "w_o": (ohi, olo), "ffn0": (xhi, xlo), "down0": (mhi, mlo),
               "rnn_in": (xhi, xlo), "rnn_out": (hhi, hlo), "ffn1": (xhi, xlo), "down1": (mhi, mlo), "w_in": (xhi, xlo),
               "w_in_kv": (xhi, xlo), "glu": (xhi, xlo), "w_out": (xhi, xlo), "ffn2": (xhi, xlo),
               "down2": (mhi, mlo)}
        RESIDUAL = {"w_o": "g_ffn0", "down0": "g_mix1", "rnn_out": "g_ffn1", "down1": None}
        GATHERED = {"w_out": mixed, "down2": mixed_ff}
        GATED = ("ffn0", "ffn1")

        def released(layer, b):
            if layer in RESIDUAL:
                return f"sum_ready{b}"
            if layer == "ffn2":
                return f"ffn2_copied{b}"
            return f"{layer}_{('gate', 'prod')[b]}" if layer in GATED else f"{layer}_out{b}"

        block = ctx.enter_context(nc.Block())

        @block.sync
        def _(sp):
            for h in range(2):
                half = slice(h * D // 2, (h + 1) * D // 2)
                sp.dma_start(x_.rearrange("p (t e) -> p t e", t=T)[:, :, half],
                             x_in.rearrange("(t p) e -> p t e", p=P)[:, :, half]).then_inc(x_arrived[h], 16)
                if h == 0:
                    sp.dma_start(small_, small_in).then_inc(small_arrived, 16)
            for s in range(RING):
                sp.dma_start(raw[:, s, :], weights[s]).then_inc(raw_arrived[s], 16)
            sp.dma_start(rope, rope_in).then_inc(s_rope, 16)
            with sp.Fori(1, TILES // RING) as i:
                for s in range(RING):
                    sp.wait_ge(lo_ready, i * RING + (s - 3))
                    sp.dma_start(raw[:, s, :], weights[i * RING + s]).then_inc(raw_arrived[s], 16)

        def finish(pool):
            for t in range(T):
                pool.wait_ge(sem("x_final"), 2 * t + 2)
                pool.dma_start(out[t * P:(t + 1) * P, :], x_[:, t * D:(t + 1) * D]).then_inc(stored, 16)
            pool.wait_ge(stored, 16 * T)

        @block.gpsimd
        def _(pool):
            nc.gpsimd.memset(ones, 1.0).then_inc(ones_ready, 1)
            for s in range(2):
                pool.dma_start(araw_[:, s * TW:(s + 1) * TW], ada_w[s]).then_inc(ada_arrived[s], 16)

            def ada_tiles(i):
                for s in range(2):
                    pool.wait_ge(ada_step, i * 4 + (2 * s - 2))
                    pool.dma_start(araw_[:, s * TW:(s + 1) * TW], ada_w[i * 2 + s]).then_inc(ada_arrived[s], 16)
            with pool.Fori(1, ADA_AT["rnn_out"] * 4) as i:
                ada_tiles(i)

            def batch_before_scan(k):
                pool.wait_ge(s_sqrt, k + 1)
                nc.gpsimd.tensor_tensor(drive[k % 2], drive[k % 2], half_tanh[k % 2], ALU.mult).then_inc(s_scaled, 1)

            def batch_after_scan(k):
                w, th = drive[k % 2], half_tanh[k % 2]
                out_ = th.rearrange("p c d s -> p (c d) s")[:, 0:4, :]
                pool.wait_ge(s_scan, k + 1)
                ordered(pool, "gpsimd")(nc.gpsimd.tensor_tensor(out_, w[:, :, 0, :], w[:, :, 1, :], ALU.add))
                pool.wait_ge(tr_free[0], GROUP_AT["rnn_in"][0] + 5 + k)
                nc.gpsimd.tensor_tensor(out_, out_, y_gelu[:, 4 * k:4 * k + 4, :], ALU.mult).then_inc(s_mixed, 1)

            for b in range(RNN_BLOCKS):
                if b in (4, 6):
                    batch_before_scan(b // 2 - 2)
                if b == 0:
                    pool.wait_ge(tiles_used, TILE0["rnn_in"])
                elif b == 1:
                    pool.wait_ge(ada_step, ADA_AT["rnn_out"] * 16)
                else:
                    pool.wait_ge(s_gate, 2 * (b - 1))
                dst = mid(20480, 2048) if b % 2 == 0 else araw_
                pool.dma_start(dst, gate_w[b]).then_inc(gate_arrived[b % 2], 16)
                if b in (4, 6):
                    batch_after_scan(b // 2 - 2)
            batch_before_scan(2)
            batch_after_scan(2)
            pool.wait_ge(s_gate, UNITS)
            with pool.Fori(ADA_AT["rnn_out"] * 4, ADA_CHUNKS * 4) as i:
                ada_tiles(i)
            pool.wait_ge(ada_step, ADA_CHUNKS * 16)
            pool.wait_ge(ada_summed, ADA_CHUNKS)
            pool.dma_start(mask, mask_in).then_inc(mask_arrived, 16)
            pool.wait_ge(sem("parameter_steps"), PARAMETER_STEPS["output_matrix"])
            pool.dma_start(matrix_store[0], bb_made).then_inc(sem("matrices_stored"), 16)
            pool.dma_start(matrix_store[1], scr(2048, 2048)).then_inc(sem("matrices_stored"), 16)
            pool.wait_ge(sem("matrices_stored"), 32)
            pool.wait_ge(sem("parameter_steps"), PARAMETER_STEPS["e_ready"])
            link = ordered(pool, "gpsimd")
            G = nc.gpsimd
            stored_tables = [sem("tables_stored0"), sem("tables_stored1")]
            grid = [P, 2, 16, 16]
            four = lambda ap: ap.rearrange("p (c a b) -> p c a b", a=16, b=16)
            for k in range(UNITS2):
                two = slice(2 * k, 2 * k + 2)
                coarse = [e16[i][:, two, :].unsqueeze(3).to_broadcast(grid) for i in range(2)]
                fine = [e1[i][:, two, :].unsqueeze(2).to_broadcast(grid) for i in range(2)]
                out_ = table_out[k % 2]
                if k >= 2:
                    pool.wait_ge(stored_tables[k % 2], 16 * (k // 2))
                G.tensor_tensor(four(out_[:, 0:512]), coarse[0], fine[0], ALU.mult)
                link(G.tensor_tensor(four(table_tmp), coarse[1], fine[1], ALU.mult))
                link(G.tensor_tensor(out_[:, 0:512], out_[:, 0:512], table_tmp, ALU.subtract))
                G.tensor_tensor(four(out_[:, 512:]), coarse[0], fine[1], ALU.mult)
                link(G.tensor_tensor(four(table_tmp), coarse[1], fine[0], ALU.mult))
                link(G.tensor_tensor(out_[:, 512:], out_[:, 512:], table_tmp, ALU.add))
                pool.dma_start(table_store[k], out_).then_inc(stored_tables[k % 2], 16)
            for b in range(2):
                pool.wait_ge(stored_tables[b], 16 * UNITS2 // 2)
            pool.wait_ge(tiles_used, TILE0["w_in"])
            pool.dma_start(mid(8960, 2048), matrix_store[0]).then_inc(sem("matrices_back"), 16)
            pool.dma_start(mid(11008, 2048), matrix_store[1]).then_inc(sem("matrices_back"), 16)

            def load_tables(k):
                pool.dma_start(mid(13056 + 1024 * (k % 4), 1024), table_store[k]).then_inc(table_arrived[k % 4], 16)
            for k in range(4):
                load_tables(k)
            for k in range(UNITS2 - 1):
                zr, zi, a0, a1, b0, b1 = unit_bufs[k % 2]
                c_, s_ = tables[k % 4][:, 0], tables[k % 4][:, 1]
                pool.wait_ge(sem("scanned"), k + 1)
                G.tensor_tensor(a0, zr, c_, ALU.mult)
                G.tensor_tensor(a1, zi, s_, ALU.mult)
                G.tensor_tensor(b0, zr, s_, ALU.mult)
                link(G.tensor_tensor(b1, zi, c_, ALU.mult))
                G.tensor_tensor(a0, a0, a1, ALU.subtract)
                G.tensor_tensor(b0, b0, b1, ALU.add).then_inc(sem("parts_ready"), 1)
                if k + 4 < UNITS2:
                    load_tables(k + 4)
            finish(pool)

        @block.scalar
        def _(act):
            A = nc.scalar.activation
            splits = [0]

            def split(tile):
                s = splits[0] % RING
                splits[0] += 1
                act.wait_ge(raw_arrived[s], (tile + (RING - s)) * (16 // RING))
                after(act, tiles_used, tile - (RING - 1) if isinstance(tile, int) else tile + (1 - RING))
                A(whi[:, s, :], raw[:, s, :], ACT.Copy).then_inc(hi_ready, 1)

            def group_hi(b, before, dst, g, signal):
                act.wait_ge(tr_ready[b], before + 1)
                for j in range(4):
                    ins = A(dst[:, j, :], tr[b][:, j, :], ACT.Copy, scale=g[:, j:j + 1])
                ins.then_inc(signal, 1)

            def root_of(name, n):
                act.wait_ge(sem("mean_ready"), NORM_AT[name])
                A(root[:, 0:n], mean[:, 0:n], ACT.Sqrt).then_inc(sem("root_ready"), 1)

            carried = []

            def carried_steps(pos):
                for at, step in [c for c in carried if c[0] == pos]:
                    step()
                    carried.remove((at, step))

            def carry(layer, tail, late):
                n = PAIRS[layer] - 1
                if tail and layer in CARRIED_AT:
                    carried.append((CARRIED_AT[layer], lambda: tail(n, 1)))
                elif tail:
                    tail(n, 1)
                for at, step in late:
                    carried.append((at, lambda step=step: step(n)))

            def run(layer, evac, tail=None, extra=None, late=(), early=None):
                kt = KTILES[layer]

                def body(i, first):
                    splits[0] = TILE0[layer] + RING
                    for pos in range(2 * kt):
                        if early:
                            early(i, pos)
                        if not (layer == "down2" and not first and pos >= 2 * kt - RING):
                            split(i * (2 * kt) + (TILE0[layer] + pos + RING))
                        if extra:
                            extra(i, pos)
                        for at, step in late:
                            if at == pos and not first:
                                step(i - 1)
                        if first:
                            carried_steps(pos)
                        if tail and pos == HOOK and not first:
                            tail(i - 1, 1)
                        if pos == kt - 1:
                            evac(i, 0)
                        if tail and pos == kt + HOOK:
                            tail(i, 0)
                        if pos == 2 * kt - 1:
                            evac(i, 1)

                each_pair(act, layer, body)
                carry(layer, tail, late)

            def chunk_done(layer, i, b):
                act.wait_ge(tiles_used, i * (2 * KTILES[layer]) + (TILE0[layer] + (b + 1) * KTILES[layer]))

            def scaled_to(layer, dst, ready=None):
                def evac(i, b):
                    if ready:
                        ready(i, b)
                    chunk_done(layer, i, b)
                    for t in range(T):
                        ins = A(dst(i, b, t), acc[b][:, t, :], ACT.Copy, scale=rstd[:, t:t + 1])
                    ins.then_inc(sem(f"{layer}_out{b}"), 1)
                return evac

            def residual(layer, extra=None):
                g = RESIDUAL[layer]

                def evac(i, b):
                    act.wait_ge(sem(f"sum_ready{b}"), i + (2 * RES_AT[layer] + 1))
                    A(x[:, :, 2 * i + b, :], tmp[:, b, :, :], ACT.Copy).then_inc(sem(f"x_new{b}"), 1)

                def turned(i, b):
                    if g:
                        c = 4 * (2 * i + b)
                        group_hi(0, GROUP_AT[layer][0] + 2 * i + b, xhi[:, c:c + 4, :], sm[g][:, c:c + 4],
                                 sem("residual_hi"))

                def tail(i, b):
                    last = (i, b) == (PAIRS[layer] - 1, 1)
                    if last and g:
                        carried.append((CARRIED_AT[layer], lambda: turned(i, b)))
                    else:
                        turned(i, b)
                    act.wait_ge(sem(f"x_new{b}"), i + (2 * RES_AT[layer] + 1))
                    for t in range(T):
                        ins = A(mid(t * NW, NW) if last and g else tmp[:, b, t, :], tmp[:, b, t, :], ACT.Square,
                                accum_out=ss[:, t, 2 * i + b:2 * i + b + 1])
                    ins.then_inc(sem(f"sum_used{b}"), 1)
                run(layer, evac, tail, extra)
                if g:
                    _, last_tail = carried.pop()
                    last_tail()
                root_of(layer, 2)

            def gated(layer):
                def evac(i, b):
                    if b:
                        return
                    if not isinstance(i, int):
                        act.wait_ge(sem(f"{layer}_prod"), i)
                    chunk_done(layer, i, 0)
                    for t in range(T):
                        ins = A(tmp[:, 0, t, :], acc[0][:, t, :], ACT.Silu, scale=rstd[:, t:t + 1])
                    ins.then_inc(sem(f"{layer}_gate"), 1)

                def tail(i, b):
                    if b:
                        act.wait_ge(tr_ready[0], i + (GROUP_AT[layer][0] + 1))
                        A(mhi_.rearrange("p (n e) -> p n e", e=4 * S)[:, i, :],
                          tr[0].rearrange("p c s -> p (c s)"), ACT.Copy).then_inc(sem(f"{layer}_hi"), 1)
                act.wait_ge(rstd_ready, {"ffn0": 2, "ffn1": 4}[layer])
                run(layer, evac, tail)

            def recurrent_in():
                def evac(i, b):
                    chunk_done("rnn_in", i, b)
                    c = 2 * i + b
                    if c >= 2:
                        act.wait_ge(tr_ready[0], GROUP_AT["rnn_in"][0] + c - 1)
                    for t in range(T):
                        ins = A(tmp[:, b, t, :], acc[b][:, t, :], ACT.Copy, scale=rstd[:, t:t + 1])
                    ins.then_inc(sem(f"rnn_in_out{b}"), 1)

                def tail(i, b):
                    c = 2 * i + b
                    if c < 4:
                        act.wait_ge(s_xb, c + 1)
                        for j in range(4 * c, 4 * c + 4):
                            ins = A(xc[:, j, :], xb[:, j, :], ACT.Identity, scale=sm["conv_w"][:, 32 + j:33 + j],
                                    bias=sm["conv_b"][:, j:j + 1])
                        ins.then_inc(s_base, 1)
                    else:
                        act.wait_ge(tr_ready[0], GROUP_AT["rnn_in"][0] + c + 1)
                        A(y_gelu[:, 4 * c - 16:4 * c - 12, :], tr[0], ACT.Gelu_apprx_tanh).then_inc(tr_free[0], 1)

                def decay_of(u):
                    act.wait_ge(s_unit, u + 1)
                    a = decay[u // 4 % 2][:, u % 4]
                    A(a, a, ACT.Copy, scale=2.0, bias=-1.0).then_inc(s_decay, 1)

                def root_of_drive(k):
                    act.wait_ge(s_unit, 4 * k + 4)
                    th = half_tanh[k % 2]
                    A(th, th, ACT.Sqrt, scale=-1.0).then_inc(s_sqrt, 1)

                def state_hi(k):
                    act.wait_ge(s_mixed, k + 1)
                    A(hhi[:, 4 * k:4 * k + 4, :], half_tanh[k % 2].rearrange("p c d s -> p (c d) s")[:, 0:4, :],
                      ACT.Copy).then_inc(s_hhi, 1)

                def unit(i, pos):
                    if i < 2:
                        return
                    f = 16 * (i - 2) + pos
                    if pos % 2 == 0:
                        gate_functions(f // 2)
                        if f:
                            decay_of(f // 2 - 1)
                    for k in range(3):
                        if f == 8 * k + BATCH_AT["root"]:
                            root_of_drive(k)
                        if f == 8 * k + BATCH_AT["hi"]:
                            state_hi(k)

                def gate_functions(u):
                    th = half_tanh[u // 4 % 2][:, u % 4]
                    act.wait_ge(s_gate, u + 1)
                    for d in range(2):
                        A(gates[:, d, 0, :], gates[:, d, 0, :], ACT.Sigmoid,
                          bias=sm["b_a"][:, 16 * d + u:16 * d + u + 1]).then_inc(s_sig, 1)
                        A(gates[:, d, 1, :], gates[:, d, 1, :], ACT.Sigmoid,
                          bias=sm["b_i"][:, 16 * d + u:16 * d + u + 1]).then_inc(s_ig, 1)
                    act.wait_ge(s_sig, 2 * u + 2)
                    if u >= 8:
                        act.wait_ge(s_hlo, u // 4 - 1)
                    for d in range(2):
                        A(th[:, d, :], gates[:, d, 0, :], ACT.Tanh,
                          scale=neg4sp[:, 16 * d + u:16 * d + u + 1]).then_inc(s_tanh, 1)
                    act.wait_ge(s_tanh, 2 * u + 2)
                    A(decay[u // 4 % 2][:, u % 4], th, ACT.Copy, scale=-1.0, bias=1.0).then_inc(s_below, 1)
                act.wait_ge(s_lam, 1)
                act.wait_ge(rstd_ready, 3)
                run("rnn_in", evac, tail, early=unit)
                decay_of(15)
                root_of_drive(3)
                carried.append((LAST_BATCH_AT["hi"], lambda: state_hi(3)))

            act.wait_ge(small_arrived, 16)
            A(lam_tmp[0], sm["lam"], ACT.Abs).then_inc(sem("setup_steps"), 1)
            act.wait_ge(sem("setup_steps"), SETUP_STEPS["lam_abs"])
            A(lam_tmp[0], lam_tmp[0], ACT.Exp, scale=-1.0).then_inc(sem("setup_steps"), 1)
            A(c_act, sm["c"], ACT.Silu).then_inc(sem("setup_steps"), 1)
            for q in range(4):
                if q == 2:
                    for s in range(RING):
                        splits[0] = s
                        split(s)
                group_hi(q % 2, q // 2, xhi[:, 4 * q:4 * q + 4, :], sm["g_mix0"][:, 4 * q:4 * q + 4], sem("first_hi"))

            def heads(i, pos):
                if (i, pos) == (0, 3):
                    for h in range(2):
                        act.wait_ge(x_arrived[h], 16)
                    for t in range(T):
                        ins = A(mid(t * D, D), x_[:, t * D:(t + 1) * D], ACT.Square, accum_out=ss[:, t, 0:1])
                    ins.then_inc(sem("first_squares"), 1)
                if (i, pos) == (0, 4):
                    root_of("first", 2)
                    act.wait_ge(rstd_ready, 1)
                for c in range(K_CHUNK + 1):
                    at = 16 * i + pos - 8 * c
                    if at == HEADS_AT["rotate"]:
                        act.wait_ge(sem(f"qkv_out{c % 2}"), c // 2 + 1)
                        after(act, s_rot, c)
                        A(squares[c % 2], qkv_h[:, :, 4 * c:4 * c + 4, :], ACT.Square).then_inc(s_sq, 1)
                    if at == HEADS_AT["sum"] and c == K_CHUNK:
                        act.wait_ge(sem("head_mean"), 1)
                        A(rq, ssq, ACT.Sqrt).then_inc(s_rq, 1)
                    if at == HEADS_AT["turn"] + (c == K_CHUNK):
                        act.wait_ge(s_qt, c + 1)
                        A(qk_t[:, 4 * c:4 * c + 4, :], tr[0], ACT.Copy).then_inc(s_qe, 1)
            run("qkv", scaled_to("qkv", lambda i, b, t: qkv[:, t, 2 * i + b, :]), None, heads)

            def exps(u):
                act.wait_ge(s_nm, u + 1)
                after(act, s_pt, u - 1)
                for i in range(4):
                    n = 4 * u + i
                    ins = A(probs[:, u % 2, i, :], psum[:, 2 * (u % 2) + i // 2, (i % 2) * S:(i % 2 + 1) * S], ACT.Exp,
                            scale=rqs[:, n:n + 1], bias=nmx[:, n:n + 1], accum_out=sums[:, n:n + 1])
                ins.then_inc(s_exp, 1)

            def heads_hi(u):
                act.wait_ge(s_pv, u + 1)
                A(ohi[:, 2 * u:2 * u + 2, :], psum[:, 6 + u % 2, :].rearrange("p (h s) -> p h s", s=S),
                  ACT.Copy).then_inc(s_oh, 1)
            exps(0)
            exps(1)
            for u in range(8):
                act.wait_ge(s_pt, u + 1)
                after(act, s_pv, u - 1)
                A(probs_t[:, u % 2, :, :, :].rearrange("p h k q -> p (h k q)"),
                  tr[0].rearrange("p c s -> p (c s)"), ACT.Copy).then_inc(s_pte, 1)
                if u < 6:
                    exps(u + 2)
                heads_hi(u)
            residual("w_o")
            gated("ffn0")
            residual("down0")
            recurrent_in()
            residual("rnn_out")
            gated("ffn1")

            def token_norm(name, n_rstd, sh, gs):
                act.wait_ge(rstd_ready, n_rstd)
                for n in range(4):
                    A(normed[:, 0, n * NW:(n + 1) * NW], x_[:, n * NW:(n + 1) * NW], ACT.Copy,
                      scale=rstd[:, 0:1]).then_inc(sem("normed0"), 1)
                for q in range(4):
                    b = q % 2
                    act.wait_ge(tr_ready[b], GROUP_AT[name][b] + q // 2 + 1)
                    for j in range(4):
                        c = 4 * q + j
                        ins = A(xhi[:, c, :], tr[b][:, j, :], ACT.Identity, scale=gs[:, c:c + 1], bias=sh[:, c:c + 1])
                    ins.then_inc(sem(f"{name}_hi"), 1)

            def parameters(i, pos):
                if (i, pos) == (0, 0):
                    act.wait_ge(tiles_used, TILE0["down1"])
                    act.dma_start(ssm_raw, ssm_in).then_inc(ssm_arrived, 16)
                    A(st_tmp[0], sm["log_step"], ACT.Exp).then_inc(sem("setup_steps"), 1)
                if (i, pos) == (0, 5):
                    act.wait_ge(sem("parameter_steps"), PARAMETER_STEPS["angle_ready"])
                    A(st_tmp[4], st_tmp[3], ACT.Sin)
                    A(st_tmp[5], st_tmp[3], ACT.Sin, scale=0.5)
                    A(st_tmp[6], st_tmp[2], ACT.Tanh, scale=0.5).then_inc(sem("setup_steps"), 1)

            def project_in():
                def evac(i, b):
                    chunk_done("w_in", i, b)
                    after(act, tr_ready[0], 0 if not i else GROUP_AT["w_in"][0] + 2 * b + 2)
                    A(tmp[:, b, :, :], acc[b], ACT.Copy).then_inc(sem(f"w_in_out{b}"), 1)

                def extra(i, pos):
                    if (i, pos) == (1, 13):
                        gelu(0)
                run("w_in", evac, None, extra)
                for n in range(4):
                    splits[0] = TILE0["w_in_kv"] + RING + n
                    split(TILE0["w_in_kv"] + RING + n)
                act.wait_ge(tiles_used, TILE0["glu"])
                A(kv, acc[0][:, :, 0:256], ACT.Copy).then_inc(sem("w_in_kv_out"), 1)

            def gelu(q):
                act.wait_ge(sem("skip_added"), q + 1)
                A(z_t[:, q, :], z_t[:, q, :], ACT.Gelu_apprx_tanh).then_inc(sem("z_ready"), 1)

            def window_exps(w):
                act.wait_ge(sem("max2_ready"), w + 1)
                for h in range(2):
                    for n, k in enumerate((slice(0, P), slice(P, 3 * P))):
                        c = 4 * w + 2 * h + n
                        A(masked[w % 2][:, h, k], masked[w % 2][:, h, k], ACT.Exp, bias=nm2[:, c:c + 1],
                          accum_out=sum2[:, c:c + 1])
                A(m2[:, 4 * w:4 * w + 4], m2[:, 4 * w:4 * w + 4], ACT.Exp).then_inc(sem("exp2_ready"), 1)

            def window_turned(w):
                act.wait_ge(sem("probs2_turned"), w + 1)
                after(act, sem("heads2_ready"), w - 1)
                A(turned[w % 2].rearrange("p h n q -> p (h n q)"), psum[:, 2:4, :].rearrange("p b e -> p (b e)")[:, 0:768],
                  ACT.Copy).then_inc(sem("turned2_ready"), 1)

            def z_hi(half):
                act.wait_ge(sem("z_ready"), 4 * half + 4)
                A(xhi[:, 4 * half:4 * half + 4, :], z_t[:, 4 * half:4 * half + 4, :], ACT.Copy).then_inc(sem("z_hi_ready"), 1)

            def mixers():
                for n in range(11):
                    k, w = 5 + n, n
                    if 1 <= w <= 8:
                        window_turned(w - 1)
                    if k % 2:
                        gelu((k - 3) // 2)
                    if w < 8:
                        window_exps(w)
                    if k == 9:
                        z_hi(0)
                gelu(7)
                z_hi(1)

            def glu_and_merge():
                def evac(i, b):
                    chunk_done("glu", i, b)
                    A(tmp[:, b, :, :], acc[b], ACT.Sigmoid).then_inc(sem(f"glu_out{b}"), 1)

                def squares_of(n, a, w):
                    for t in range(T):
                        ins = A(squares_out[:, (2 * t + a // W2) * W2:][:, a % W2:a % W2 + w], merged[:, t, a:a + w], ACT.Square,
                                accum_out=ss[:, t, n:n + 1])
                    ins.then_inc(sem("merge_squares"), 1)

                def beside(i, pos):
                    if pos == 1:
                        act.wait_ge(sem("attn2_out"), 8)
                        squares_of(0, 0, W2)
                    if pos == 6:
                        act.wait_ge(sem("merged_ready"), 1)
                        squares_of(1, W2, NW)
                run("glu", evac, None, beside)
                act.wait_ge(sem("merged_ready"), 2)
                squares_of(2, W2 + NW, NW)
                root_of("merge", 4)
                act.wait_ge(rstd_ready, 6)
                for n in range(4):
                    m = merged[:, 0, n * NW:(n + 1) * NW]
                    A(m, m, ACT.Copy, scale=rstd[:, n // 2:n // 2 + 1]).then_inc(sem("normed0"), 1)
                for q in range(4):
                    group_hi(q % 2, GROUP_AT["merge"][q % 2] + q // 2, xhi[:, 4 * q:4 * q + 4, :],
                             sm["g_merged"][:, 4 * q:4 * q + 4], sem("merge_hi"))

            def gathered(layer):
                dst = GATHERED[layer]

                def evac(i, b):
                    chunk_done(layer, i, b)
                    n = 2 * i + b
                    after(act, sem(f"{layer}_out{b}"), i)
                    A(dst[:, :, n, :], acc[b], ACT.Copy)
                    for t in range(T):
                        ins = A(tmp[:, b, t, :], acc[b][:, t, :], ACT.Square, accum_out=ss[:, t, n:n + 1])
                    ins.then_inc(sem(f"{layer}_out{b}"), 1)
                run(layer, evac)
                root_of(layer, 2)

            def up_convolved():
                w = sm["conv2_w"].rearrange("p (k h n j) -> p k h n j", k=3, h=2, j=4)
                bias = sm["conv2_b"].rearrange("p (h n j) -> p h n j", h=2, j=4)
                flat = conv_.rearrange("p (h e) -> p h e", h=2)

                def evac(i, b):
                    chunk_done("ffn2", i, b)
                    after(act, tr_ready[b], i + GROUP_AT["ffn2"][b])
                    A(tmp[:, b, :, :], acc[b], ACT.Copy).then_inc(sem(f"ffn2_copied{b}"), 1)

                def base(i, b):
                    after(act, sem("ffn2_lo"), i)
                    act.wait_ge(tr_ready[b], i + (GROUP_AT["ffn2"][b] + 1))
                    for j in range(4):
                        ins = A(conv[:, 4 * b + j, :], tr[b][:, j, :], ACT.Identity, scale=w[:, 2, b, i, j:j + 1],
                                bias=bias[:, b, i, j:j + 1])
                    ins.then_inc(sem(f"ffn2_base{b}"), 1)

                def gelu(i):
                    act.wait_ge(tr_free[1], i + (GROUP_AT["ffn2"][1] + 1))
                    A(flat[:, 1, :], flat[:, 1, :], ACT.Gelu_apprx_tanh).then_inc(sem("ffn2_gelu"), 1)

                def hi(i):
                    act.wait_ge(sem("ffn2_prod"), i + 1)
                    A(mhi_.rearrange("p (n e) -> p n e", e=4 * S)[:, i, :], flat[:, 0, :], ACT.Copy).then_inc(sem("ffn2_hi"), 1)
                run("ffn2", evac, None, None, ((4, lambda i: base(i, 0)), (5, lambda i: base(i, 1)), (9, gelu), (11, hi)))

            residual("down1", parameters)
            act.wait_ge(ada_ready, 1)
            for b in range(2):
                act.wait_ge(sem(f"tables_stored{b}"), 16 * UNITS2 // 2)
            token_norm("norm_mix", 5, sh_m, gs_m)
            project_in()
            mixers()
            glu_and_merge()
            gathered("w_out")
            for n in range(2 * T):
                act.wait_ge(sem("x_mixed"), n + 1)
                ins = A(mid(6912 + n * D // 2, D // 2), x_[:, n * D // 2:(n + 1) * D // 2], ACT.Square,
                        accum_out=ss[:, n // 2, n % 2:n % 2 + 1])
            ins.then_inc(sem("x_squares"), 1)
            root_of("norm_ffn", 2)
            token_norm("norm_ffn", 8, sh_f, gs_f)
            up_convolved()
            gathered("down2")

        @block.vector
        def _(dve):
            V = nc.vector
            splits = [0]

            def split(tile):
                s = splits[0] % RING
                splits[0] += 1
                dve.wait_ge(hi_ready, tile + 1)
                V.tensor_tensor(wlo[:, s, :], raw[:, s, :], whi[:, s, :].bitcast(F32), ALU.subtract).then_inc(lo_ready, 1)

            def group_lo(b, dst_lo, dst_hi, g, signal, count):
                dve.wait_ge(signal, count)
                for j in range(4):
                    ins = V.scalar_tensor_tensor(dst_lo[:, j, :], tr[b][:, j, :], g[:, j:j + 1],
                                                 dst_hi[:, j, :].bitcast(F32), ALU.mult, ALU.subtract)
                ins.then_inc(tr_free[b], 1)

            def rstd_of(name, total, count, n=2):
                if total is not None:
                    ordered(dve, "vector")(total)
                V.tensor_scalar(mean[:, 0:n], mean[:, 0:n], 1.0 / (D if n == 2 else W2), EPS, ALU.mult,
                                ALU.add).then_inc(sem("mean_ready"), 1)
                dve.wait_ge(sem("root_ready"), NORM_AT[name])
                V.reciprocal(rstd[:, 0:n], root[:, 0:n]).then_inc(rstd_ready, 1)

            def ada_product(a, i, at):
                s = a % 2
                dve.wait_ge(ada_arrived[s], (i * 4 + (at * 4 + a // 2 + 1)) * 16)
                for k in range(KT):
                    w, c = araw[:, s, k, :], c_act[:, 2 * a + k:2 * a + k + 1]
                    if a == 0 and k == 0:
                        after(dve, ada_summed, i + at)
                        ins = V.tensor_scalar(adacc_, w, c, None, ALU.mult)
                    else:
                        dve.wait_ge(ada_step, i * 16 + (at * 16 + 2 * a + k))
                        ins = V.scalar_tensor_tensor(adacc_, w, c, adacc_, ALU.mult, ALU.add)
                    ins.then_inc(ada_step, 1)

            def ada_out(i, at):
                dve.wait_ge(ada_summed, i + (at + 1))
                cols = adat_.rearrange("p (n j) -> p n j", j=4)
                bias = sm["b_ada"].rearrange("p (n j) -> p n j", j=4)
                V.tensor_tensor(cols[:, i + at, :], psum[:, 6, 0:4], bias[:, i + at, :], ALU.add).then_inc(ada_done, 1)

            carried = []

            def carried_steps(pos):
                for at, step in [c for c in carried if c[0] == pos]:
                    step()
                    carried.remove((at, step))

            def carry(layer, tail, late):
                n = PAIRS[layer] - 1
                if tail and layer in CARRIED_AT:
                    carried.append((CARRIED_AT[layer], lambda: tail(n, 1)))
                elif tail:
                    tail(n, 1)
                for at, step in late:
                    carried.append((at, lambda step=step: step(n)))

            def run(layer, evac=None, tail=None, extra=None, late=(), early=None):
                kt = KTILES[layer]
                ada = ADA_AT.get(layer)

                def body(i, first):
                    splits[0] = TILE0[layer] + RING
                    for pos in range(2 * kt):
                        if early:
                            early(i, pos)
                        if not (layer == "down2" and not first and pos >= 2 * kt - RING):
                            split(i * (2 * kt) + (TILE0[layer] + pos + RING))
                        if extra:
                            extra(i, pos)
                        for at, step in late:
                            if at == pos and not first:
                                step(i - 1)
                        if first:
                            carried_steps(pos)
                        if ada is not None and pos in ADA_POS:
                            ada_product(pos - ADA_POS[0], i, ada)
                        if pos == HOOK and not first:
                            if tail:
                                tail(i - 1, 1)
                            if ada is not None:
                                ada_out(i - 1, ada)
                        if evac and pos == kt - 1:
                            evac(i, 0)
                        if tail and pos == kt + HOOK:
                            tail(i, 0)
                        if evac and pos == 2 * kt - 1:
                            evac(i, 1)
                each_pair(dve, layer, body)
                carry(layer, tail, late)
                if ada is not None:
                    ada_out(PAIRS[layer] - 1, ada)

            def chunk_done(layer, i, b):
                dve.wait_ge(tiles_used, i * (2 * KTILES[layer]) + (TILE0[layer] + (b + 1) * KTILES[layer]))

            def residual(layer, count, extra=None):
                g = RESIDUAL[layer]

                def evac(i, b):
                    chunk_done(layer, i, b)
                    after(dve, sem(f"sum_used{b}"), i + 2 * RES_AT[layer])
                    V.tensor_tensor(tmp[:, b, :, :], acc[b], x[:, :, 2 * i + b, :], ALU.add).then_inc(
                        sem(f"sum_ready{b}"), 1)

                def tail(i, b):
                    if g:
                        c = 4 * (2 * i + b)
                        group_lo(0, xlo[:, c:c + 4, :], xhi[:, c:c + 4, :], sm[g][:, c:c + 4],
                                 sem("residual_hi"), 4 * RES_AT[layer] + 2 * i + b + 1)
                run(layer, evac, tail, extra)
                for b in range(2):
                    dve.wait_ge(sem(f"sum_used{b}"), 2 * RES_AT[layer] + 2)
                rstd_of(layer, V.reduce_sum(mean[:, 0:T], ss, AX), count)

            def gated(layer):
                dve.wait_ge(rstd_ready, {"ffn0": 2, "ffn1": 4}[layer])

                def evac(i, b):
                    if not b:
                        return
                    chunk_done(layer, i, 1)
                    after(dve, tr_ready[0], i + GROUP_AT[layer][0])
                    dve.wait_ge(sem(f"{layer}_gate"), i + 1)
                    for t in range(T):
                        ins = V.scalar_tensor_tensor(tmp[:, 1, t, :], acc[1][:, t, :], rstd[:, t:t + 1],
                                                     tmp[:, 0, t, :], ALU.mult, ALU.mult)
                    ins.then_inc(sem(f"{layer}_prod"), 1)

                def tail(i, b):
                    if b:
                        dve.wait_ge(sem(f"{layer}_hi"), i + 1)
                        hi = mhi_.rearrange("p (n e) -> p n e", e=4 * S)[:, i, :]
                        lo = mlo_.rearrange("p (n e) -> p n e", e=4 * S)[:, i, :]
                        V.tensor_tensor(lo, tr[0].rearrange("p c s -> p (c s)"), hi.bitcast(F32),
                                        ALU.subtract).then_inc(tr_free[0], 1)
                run(layer, evac, tail)

            def softplus_of_lambda():
                link = ordered(dve, "vector")
                y, z, z2, poly = lam_tmp
                dve.wait_ge(sem("setup_steps"), SETUP_STEPS["lam_exp"])
                link(V.tensor_scalar(z, y, 2.0, None, ALU.add))
                link(V.reciprocal(z, z))
                link(V.tensor_tensor(z, z, y, ALU.mult))
                link(V.tensor_tensor(z2, z, z, ALU.mult))
                link(V.tensor_scalar(poly, z2, 1.0 / 17, 1.0 / 15, ALU.mult, ALU.add))
                for n in (13, 11, 9, 7, 5, 3, 1):
                    link(V.tensor_tensor(poly, poly, z2, ALU.mult))
                    link(V.tensor_scalar(poly, poly, 1.0 / n, None, ALU.add))
                link(V.tensor_tensor(poly, poly, z, ALU.mult))
                link(V.tensor_scalar(z, sm["lam"], -1.0, 0.0, ALU.mult, ALU.max))
                link(V.scalar_tensor_tensor(z, poly, 2.0, z, ALU.mult, ALU.add))
                V.tensor_scalar(neg4sp, z, -LRU_C / 2, None, ALU.mult).then_inc(s_lam, 1)

            def recurrent_in():
                def tail(i, b):
                    c = 2 * i + b
                    if c >= 4:
                        return
                    dve.wait_ge(tr_ready[0], GROUP_AT["rnn_in"][0] + c + 1)
                    V.tensor_copy(xb[:, 4 * c:4 * c + 4, :], tr[0]).then_inc(tr_free[0], 1)
                    dve.wait_ge(tr_free[0], GROUP_AT["rnn_in"][0] + c + 1)
                    V.engine_nop().then_inc(s_xb, 1)
                    dve.wait_ge(s_base, c + 1)
                    for n, (tap, dst, src) in enumerate(((0, slice(2, S), slice(0, S - 2)), (1, slice(1, S), slice(0, S - 1)),
                                                         (3, slice(0, S - 1), slice(1, S)))):
                        for j in range(4 * c, 4 * c + 4):
                            ins = V.scalar_tensor_tensor(xc[:, j, dst], xb[:, j, src], sm["conv_w"][:, 16 * tap + j:16 * tap + j + 1],
                                                         xc[:, j, dst], ALU.mult, ALU.add)
                        ins.then_inc(s_conv, 1)
                        dve.wait_ge(s_conv, 3 * c + n + 1)

                link = ordered(dve, "vector")

                def gated_input(u):
                    w = drive[u // 4 % 2][:, u % 4]
                    dve.wait_ge(s_ig, 2 * u + 2)
                    dve.wait_ge(s_tanh, 2 * u + 2)
                    V.tensor_tensor(w, gates[:, :, 1, :], xc[:, u, :].unsqueeze(1).to_broadcast([P, 2, S]), ALU.mult).then_inc(s_drive, 1)

                def one_plus_decay(u):
                    a, w = (v[u // 4 % 2][:, u % 4] for v in (decay, drive))
                    dve.wait_ge(s_below, u + 1)
                    link(V.reciprocal(a, a))
                    V.scalar_tensor_tensor(w, w, 2.0, a, ALU.mult, ALU.mult).then_inc(s_unit, 1)

                def scans(k):
                    a, w = (v[k % 2] for v in (decay, drive))
                    dve.wait_ge(s_decay, 4 * k + 4)
                    if k < 3:
                        dve.wait_ge(s_scaled, k + 1)
                    for c in range(4):
                        V.tensor_tensor_scan(w[:, c, 0, :], a[:, c, 0, :], w[:, c, 0, :], 0.0, ALU.mult, ALU.add)
                        ins = V.tensor_tensor_scan(w[:, c, 1, ::-1], a[:, c, 1, ::-1], w[:, c, 1, ::-1], 0.0, ALU.mult, ALU.add)
                    ins.then_inc(s_scan, 1)

                def state_lo(k):
                    dve.wait_ge(s_hhi, k + 1)
                    V.tensor_tensor(hlo[:, 4 * k:4 * k + 4, :], half_tanh[k % 2].rearrange("p c d s -> p (c d) s")[:, 0:4, :],
                                    hhi[:, 4 * k:4 * k + 4, :].bitcast(F32), ALU.subtract).then_inc(s_hlo, 1)

                def unit(i, pos):
                    if i < 2:
                        return
                    f = 16 * (i - 2) + pos
                    (one_plus_decay if f % 2 else gated_input)(f // 2)
                    for k in range(3):
                        if f == 8 * k + BATCH_AT["scan"]:
                            scans(k)
                        if f == 8 * k + BATCH_AT["lo"]:
                            state_lo(k)
                run("rnn_in", None, tail, early=unit)
                w, th = drive[1], half_tanh[1]
                out_ = th.rearrange("p c d s -> p (c d) s")[:, 0:4, :]
                dve.wait_ge(s_sqrt, 4)
                link(V.tensor_tensor(w, w, th, ALU.mult))
                scans(3)

                def mix():
                    dve.wait_ge(s_scan, 4)
                    link(V.tensor_tensor(out_, w[:, :, 0, :], w[:, :, 1, :], ALU.add))
                    dve.wait_ge(tr_free[0], GROUP_AT["rnn_in"][0] + 8)
                    V.tensor_tensor(out_, out_, y_gelu[:, 12:16, :], ALU.mult).then_inc(s_mixed, 1)
                carried.append((LAST_BATCH_AT["mix"], mix))
                carried.append((LAST_BATCH_AT["lo"], lambda: state_lo(3)))

            for q in range(4):
                if q == 2:
                    for s in range(RING):
                        splits[0] = s
                        split(s)
                group_lo(q % 2, xlo[:, 4 * q:4 * q + 4, :], xhi[:, 4 * q:4 * q + 4, :],
                         sm["g_mix0"][:, 4 * q:4 * q + 4], sem("first_hi"), q + 1)
            dve.wait_ge(sem("setup_steps"), SETUP_STEPS["c_ready"])
            def rotation_factors():
                dve.wait_ge(s_rope, 16)
                cos = rope[:, 0:128].rearrange("p (t a f) -> p t a f", t=T, a=2)
                sin = rope[:, 128:256].rearrange("p (t a f) -> p t a f", t=T, a=2)
                for k in range(2):
                    gain = rope[:, 256 + 128 * k:384 + 128 * k].rearrange("p (a h f) -> p a h f", a=2, h=2)
                    for t in range(T):
                        keep = tabs[:, 2 * k, t, :].rearrange("p (a h f) -> p a h f", a=2, h=2)
                        cross = tabs[:, 2 * k + 1, t, :].rearrange("p (a h f) -> p a h f", a=2, h=2)
                        for h in range(2):
                            V.tensor_tensor(keep[:, :, h, :], gain[:, :, h, :], cos[:, t], ALU.mult)
                            ins = V.scalar_tensor_tensor(cross[:, :, h, :], gain[:, :, 1 - h, :], 1.0 if h else -1.0,
                                                         sin[:, t], ALU.mult, ALU.mult)
                        ins.then_inc(sem("tabs_ready"), 1)
                dve.wait_ge(sem("tabs_ready"), 4)

            link = ordered(dve, "vector")
            by_head = lambda ap: ap.rearrange("p (h t) -> p t h", t=T)

            def rotate(c, t):
                k = c // K_CHUNK
                if t == 0:
                    dve.wait_ge(sem(f"qkv_out{c % 2}"), c // 2 + 1)
                    after(dve, s_rot, c - 1)
                src, sw = qkv_h[:, t, 4 * c:4 * c + 4, :], swapped[c % 2][:, t]
                V.tensor_tensor(rot[:, t, 4 * c:4 * c + 4, :], src, tabs[:, 2 * k, t, :].unsqueeze(1).to_broadcast([P, 4, HEAD]), ALU.mult)
                s5 = src.rearrange("p h (a z f) -> p h a z f", a=2, z=2)
                w5 = sw.rearrange("p h (a z f) -> p h a z f", a=2, z=2)
                c4 = tabs[:, 2 * k + 1, t, :].rearrange("p (a z f) -> p a z f", a=2, z=2)
                for z in range(2):
                    ins = V.tensor_tensor(w5[:, :, :, z, :], s5[:, :, :, 1 - z, :],
                                          c4[:, :, z, :].unsqueeze(1).to_broadcast([P, 4, 2, FREQS]), ALU.mult)
                if t == T - 1:
                    link(ins)

            def heads(i, pos):
                if (i, pos) == (0, 2):
                    rotation_factors()
                if (i, pos) == (0, 4):
                    dve.wait_ge(sem("first_squares"), 1)
                    rstd_of("first", V.tensor_copy(mean[:, 0:T], ss[:, :, 0]), 1)
                if (i, pos) == (0, 5):
                    softplus_of_lambda()
                for c in range(K_CHUNK + 1):
                    at = 16 * i + pos - 8 * c
                    four = slice(4 * c, 4 * c + 4)
                    for t in range(T):
                        if at == HEADS_AT["rotate"] + t:
                            rotate(c, t)
                    if at == HEADS_AT["add"]:
                        ins = V.tensor_tensor(rot[:, :, four, :], rot[:, :, four, :], swapped[c % 2], ALU.add)
                        if c < K_CHUNK:
                            ins.then_inc(s_rot, 1)
                        else:
                            link(ins)
                    if at == HEADS_AT["sum"]:
                        dve.wait_ge(s_sq, c + 1)
                        link(V.reduce_sum(by_head(ssq)[:, :, four], squares[c % 2], AX))
                        if c == K_CHUNK:
                            V.tensor_scalar(ssq, ssq, 1.0 / HEAD, EPS, ALU.mult, ALU.add).then_inc(sem("head_mean"), 1)
                    if at == HEADS_AT["sum"] + 1 and c == K_CHUNK:
                        dve.wait_ge(s_rq, 1)
                        link(V.reciprocal(rq, rq))
                        V.tensor_scalar(rqs, rq, HEAD ** -0.5, None, ALU.mult)
                        for t in range(T):
                            ins = V.tensor_tensor(rot[:, t, four, :], rot[:, t, four, :],
                                                  by_head(rq)[:, t, four].unsqueeze(2).to_broadcast([P, KVH, HEAD]), ALU.mult)
                        ins.then_inc(s_rot, 1)
            run("qkv", None, None, heads)

            def head_max(u):
                dve.wait_ge(s_sc, u + 1)
                b = 2 * (u % 2)
                link(V.tensor_reduce(mx[:, 4 * u:4 * u + 4], psum[:, b:b + 2, :].rearrange("p h (t k) -> p (h t) k", k=S), AX, ALU.max))
                V.scalar_tensor_tensor(nmx[:, 4 * u:4 * u + 4], mx[:, 4 * u:4 * u + 4], -1.0, rqs[:, 4 * u:4 * u + 4],
                                       ALU.mult, ALU.mult).then_inc(s_nm, 1)

            def heads_lo(u):
                dve.wait_ge(s_oh, u + 1)
                V.tensor_tensor(olo[:, 2 * u:2 * u + 2, :], psum[:, 6 + u % 2, :].rearrange("p (h s) -> p h s", s=S),
                                ohi[:, 2 * u:2 * u + 2, :].bitcast(F32), ALU.subtract).then_inc(s_ol, 1)
            def normalized(u):
                dve.wait_ge(s_exp, u + 1)
                link(V.reciprocal(rinv[:, 4 * u:4 * u + 4], sums[:, 4 * u:4 * u + 4]))
                V.tensor_tensor(probs[:, u % 2, :, :], probs[:, u % 2, :, :],
                                rinv[:, 4 * u:4 * u + 4].unsqueeze(2).to_broadcast([P, 4, S]), ALU.mult).then_inc(s_pn, 1)
            head_max(0)
            head_max(1)
            normalized(0)
            for u in range(8):
                if u < 7:
                    normalized(u + 1)
                if u < 6:
                    head_max(u + 2)
                if u:
                    heads_lo(u - 1)
            heads_lo(7)
            residual("w_o", 2)
            gated("ffn0")
            residual("down0", 3)
            recurrent_in()
            residual("rnn_out", 4)
            gated("ffn1")

            def ada_gains():
                dve.wait_ge(ada_done, ADA_CHUNKS)
                for at, g in ((1, "g_pre_mix"), (2, "g_post_mix"), (4, "g_pre_ffn"), (5, "g_post_ffn")):
                    v = adat_[:, 16 * at:16 * at + 16]
                    ins = V.scalar_tensor_tensor(v, v, 1.0, sm[g], ALU.add, ALU.mult)
                ins.then_inc(ada_ready, 1)
                dve.wait_ge(ada_ready, 1)

            def token_norm(name, n_rstd, sh, gs):
                dve.wait_ge(rstd_ready, n_rstd)
                for n in range(4):
                    V.tensor_scalar(normed[:, 1, n * NW:(n + 1) * NW], x_[:, D + n * NW:D + (n + 1) * NW], rstd[:, 1:2],
                                    None, ALU.mult).then_inc(sem("normed1"), 1)
                for q in range(4):
                    b = q % 2
                    dve.wait_ge(sem(f"{name}_hi"), q + 1)
                    for j in range(4):
                        c = 4 * q + j
                        ins = V.tensor_scalar(shifted[b][:, j, :], tr[b][:, j, :], gs[:, c:c + 1], sh[:, c:c + 1], ALU.mult, ALU.add)
                    ins.then_inc(sem(f"{name}_shifted"), 1)
                    dve.wait_ge(sem(f"{name}_shifted"), q + 1)
                    V.tensor_tensor(xlo[:, 4 * q:4 * q + 4, :], shifted[b], xhi[:, 4 * q:4 * q + 4, :].bitcast(F32),
                                    ALU.subtract).then_inc(tr_free[b], 1)

            def state_parameters():
                link = ordered(dve, "vector")
                lr, li = sm["lam_re"], sm["lam_im"]
                dt, ang, lrdt, red, sin_, half_, th, cos_, e, m, f_re, f_im, a1, a2, a3, den = st_tmp[:16]
                w_re, w_im, v_re, v_im = st_tmp[16:20]
                TWO_PI = [6.28125, 0.0019350051879882812, 3.019916050561733e-07]
                MAGIC = 1.5 * 2.0 ** 23

                def angles():
                    dve.wait_ge(sem("setup_steps"), SETUP_STEPS["dt_ready"])
                    link(V.tensor_tensor(lrdt, lr, dt, ALU.mult))
                    link(V.tensor_tensor(ang, li, dt, ALU.mult))
                    link(V.tensor_scalar(a1, ang, 1.0 / (2.0 * np.pi), MAGIC, ALU.mult, ALU.add))
                    link(V.tensor_scalar(a1, a1, MAGIC, None, ALU.subtract))
                    link(V.scalar_tensor_tensor(red, a1, -TWO_PI[0], ang, ALU.mult, ALU.add))
                    link(V.scalar_tensor_tensor(red, a1, -TWO_PI[1], red, ALU.mult, ALU.add))
                    link(V.scalar_tensor_tensor(red, a1, -TWO_PI[2], red, ALU.mult, ALU.add))
                    V.tensor_scalar(red, red, 3.1415925, -3.1415925, ALU.min, ALU.max).then_inc(sem("parameter_steps"), 1)

                def factors():
                    dve.wait_ge(sem("setup_steps"), SETUP_STEPS["sines_ready"])
                    link(V.tensor_scalar(a1, th, -1.0, 1.0, ALU.mult, ALU.add))
                    link(V.reciprocal(a1, a1))
                    link(V.scalar_tensor_tensor(e, th, 2.0, a1, ALU.mult, ALU.mult))
                    link(V.tensor_scalar(m, e, 1.0, None, ALU.add))
                    link(V.tensor_tensor(a2, half_, half_, ALU.mult))
                    link(V.tensor_scalar(cos_, a2, -2.0, 1.0, ALU.mult, ALU.add))
                    link(V.scalar_tensor_tensor(a3, a2, -2.0, m, ALU.mult, ALU.mult))
                    link(V.tensor_tensor(e, e, a3, ALU.add))
                    link(V.tensor_tensor(a1, m, sin_, ALU.mult))
                    link(V.tensor_tensor(a2, lr, lr, ALU.mult))
                    link(V.tensor_tensor(a3, li, li, ALU.mult))
                    link(V.tensor_tensor(den, a2, a3, ALU.add))
                    link(V.reciprocal(den, den))

                def factors2():
                    link(V.tensor_tensor(a2, e, lr, ALU.mult))
                    link(V.tensor_tensor(a3, a1, li, ALU.mult))
                    link(V.tensor_tensor(f_re, a2, a3, ALU.add))
                    link(V.tensor_tensor(f_re, f_re, den, ALU.mult))
                    link(V.tensor_tensor(a2, a1, lr, ALU.mult))
                    link(V.tensor_tensor(a3, e, li, ALU.mult))
                    link(V.tensor_tensor(f_im, a2, a3, ALU.subtract))
                    link(V.tensor_tensor(f_im, f_im, den, ALU.mult))
                    link(V.tensor_copy(mag_keep, m))

                def input_matrix(part):
                    if part == 0:
                        dve.wait_ge(ssm_arrived, 16)
                        link(V.memset(scr(2048, 2048), 0.0))
                    f = [v.unsqueeze(2).to_broadcast([P, ST, GROUP]) for v in (f_re, f_im)]
                    t0, t1 = (by_tile(scr(4096 + 512 * i, 512), GROUP) for i in range(2))
                    link(V.tensor_tensor(t0, b_raw[part], f[0], ALU.mult))
                    link(V.tensor_tensor(t1, b_raw[1 - part], f[1], ALU.mult))
                    for g in range(2):
                        r = slice(64 * g, 64 * g + 64)
                        ins = V.tensor_tensor(bd[part][r, :, GROUP * g:GROUP * g + GROUP], t0[r], t1[r],
                                              ALU.add if part else ALU.subtract)
                    link(ins)
                    if part:
                        V.engine_nop().then_inc(sem("parameter_steps"), 1)

                def turned_matrix(b):
                    dve.wait_ge(tr_ready[0], GROUP_AT["ssm_b"][0] + b + 1)
                    V.tensor_copy(bb_made[:, 1024 * b:1024 * b + 1024], tr[0].rearrange("p c s -> p (c s)")).then_inc(tr_free[0], 1)

                def output_matrix():
                    link(V.memset(scr(2048, 2048), 0.0))
                    for g in range(2):
                        r, c = slice(64 * g, 64 * g + 64), slice(GROUP * g, GROUP * g + GROUP)
                        V.tensor_copy(c_made[0][r, :, c], c_raw[0][r])
                        ins = V.tensor_scalar(c_made[1][r, :, c], c_raw[1][r], -1.0, None, ALU.mult)
                    ins.then_inc(sem("parameter_steps"), 1)
                    dve.wait_ge(sem("parameter_steps"), PARAMETER_STEPS["output_matrix"])

                def cmul(out_, a_, w_, n):
                    t_ = [by_tile(v[:, 0:ST * n], n) for v in cm_tmp]
                    wb = [v.unsqueeze(2).to_broadcast([P, ST, n]) for v in w_]
                    V.tensor_tensor(t_[0], a_[0], wb[0], ALU.mult)
                    V.tensor_tensor(t_[1], a_[1], wb[1], ALU.mult)
                    V.tensor_tensor(t_[2], a_[0], wb[1], ALU.mult)
                    link(V.tensor_tensor(t_[3], a_[1], wb[0], ALU.mult))
                    V.tensor_tensor(out_[0], t_[0], t_[1], ALU.subtract)
                    link(V.tensor_tensor(out_[1], t_[2], t_[3], ALU.add))

                def powers(step):
                    dst = e1 if step < 4 else e16
                    k = 1 << (step % 4)
                    one = lambda v: v.unsqueeze(2)
                    if step == 0:
                        V.tensor_copy(w_re, cos_)
                        link(V.tensor_copy(w_im, sin_))
                    if k == 1:
                        V.memset(dst[0][:, :, 0:1], 1.0)
                        link(V.memset(dst[1][:, :, 0:1], 0.0))
                    cmul([v[:, :, k:2 * k] for v in dst], [v[:, :, 0:k] for v in dst], (w_re, w_im), k)
                    if step < 7:
                        cmul([one(v_re), one(v_im)], [one(w_re), one(w_im)], (w_re, w_im), 1)
                        V.tensor_copy(w_re, v_re)
                        link(V.tensor_copy(w_im, v_im))
                    else:
                        V.engine_nop().then_inc(sem("parameter_steps"), 1)
                steps = {4: angles, 6: factors, 8: factors2, 10: lambda: input_matrix(0), 12: lambda: input_matrix(1),
                         16: lambda: turned_matrix(0), 19: lambda: turned_matrix(1), 21: output_matrix}
                for n in range(8):
                    steps[22 + n + n // 2] = lambda n=n: powers(n)
                return lambda i, pos: steps[pos]() if i == 0 and pos in steps else None

            def project_in():
                def copied(c, half):
                    n = 2 * c + half
                    dve.wait_ge(tr_ready[0], GROUP_AT["w_in"][0] + n + 1)
                    dst = u_t[:, 2 * n:2 * n + 2, :] if c < 2 else q2_t[:, 2 * n - 8:2 * n - 6, :]
                    V.tensor_copy(dst, by_tile(psum[:, 5, :], S)).then_inc(tr_free[0], 1)

                def extra(i, pos):
                    for half in range(2):
                        for b in range(2):
                            if pos == TURN_AT[half] + 8 * (1 - b) and (b == 0 or i):
                                copied(2 * i if not b else 2 * i - 1, half)
                    for part in range(3):
                        at = divmod(16 * i + pos - part, 16)
                        if at in STREAM_UNITS:
                            unit(STREAM_UNITS[at], part)
                    if (i, pos) == (1, 12):
                        skip(0)
                run("w_in", None, None, extra)
                for n in range(4):
                    splits[0] = TILE0["w_in_kv"] + RING + n
                    split(TILE0["w_in_kv"] + RING + n)
                    if n == 0:
                        unit(4, 2)
                    if n >= 2:
                        copied(3, n - 2)
                dve.wait_ge(tr_ready[0], GROUP_AT["w_in_k"][0] + 1)
                V.tensor_copy(k2_t, psum[:, 5, 0:S]).then_inc(tr_free[0], 1)

            def unit(k, part):
                link = ordered(dve, "vector")
                zr, zi, a0, a1, b0, b1 = unit_bufs[k % 2]
                c_, s_ = tables[k % 4][:, 0], tables[k % 4][:, 1]
                re_, im_ = (psum[:, 6:8, b * S:(b + 1) * S] for b in range(2))
                if part == 0:
                    dve.wait_ge(table_arrived[k % 4], 16 * (k // 4 + 1))
                    dve.wait_ge(sem("inputs_ready"), k + 1)
                    after(dve, sem("state_out"), k - 1)
                    V.tensor_tensor(a0, re_, c_, ALU.mult)
                    V.tensor_tensor(a1, im_, s_, ALU.mult)
                    V.tensor_tensor(b0, im_, c_, ALU.mult)
                    V.tensor_tensor(b1, re_, s_, ALU.mult).then_inc(sem("inputs_taken"), 1)
                if part == 1:
                    dve.wait_ge(sem("inputs_taken"), k + 1)
                    V.tensor_tensor(zr, a0, a1, ALU.add)
                    link(V.tensor_tensor(zi, b0, b1, ALU.subtract))
                if part == 2:
                    for j in range(2):
                        decay_ = mag_keep[:, 2 * k + j:2 * k + j + 1].to_broadcast([P, S])
                        for z in (zr, zi):
                            ins = V.tensor_tensor_scan(z[:, j, :], decay_, z[:, j, :], 0.0, ALU.mult, ALU.add)
                    ins.then_inc(sem("scanned"), 1)
                if part == 2 and k == UNITS2 - 1:
                    dve.wait_ge(sem("scanned"), UNITS2)
                    V.tensor_tensor(a0, zr, c_, ALU.mult)
                    V.tensor_tensor(a1, zi, s_, ALU.mult)
                    V.tensor_tensor(b0, zr, s_, ALU.mult)
                    link(V.tensor_tensor(b1, zi, c_, ALU.mult))
                    V.tensor_tensor(a0, a0, a1, ALU.subtract)
                    V.tensor_tensor(b0, b0, b1, ALU.add).then_inc(sem("scanned"), 1)

            def skip(q):
                dve.wait_ge(sem("state_out"), 2 * q + 2)
                V.scalar_tensor_tensor(z_t[:, q, :], u_t[:, q, :], sm["d_skip"][:, q:q + 1], psum[:, Y_BANK[q], 0:S],
                                       ALU.mult, ALU.add).then_inc(sem("skip_added"), 1)

            pair_of = lambda v, w: v[:, 4 * w:4 * w + 4].rearrange("p (h n) -> p h n", n=2)

            def window_max(w):
                link = ordered(dve, "vector")
                if w == 0:
                    dve.wait_ge(mask_arrived, 16)
                dve.wait_ge(sem("scores2_ready"), w + 1)
                after(dve, sem("probs2_turned"), w - 1)
                mk = masked[w % 2]
                V.scalar_tensor_tensor(mk, psum[:, 0:2, 0:384], HEAD2 ** -0.5, mask.unsqueeze(1).to_broadcast([P, 2, 384]),
                                       ALU.mult, ALU.add).then_inc(sem("scores2_taken"), 1)
                dve.wait_ge(sem("scores2_taken"), w + 1)
                m, nm = pair_of(m2, w), pair_of(nm2, w)
                V.tensor_reduce(m[:, :, 0], mk[:, :, 0:P], AX, ALU.max)
                link(V.tensor_reduce(m[:, :, 1], mk[:, :, P:3 * P], AX, ALU.max))
                sink = sm["sinks"][:, 2 * w:2 * w + 2].unsqueeze(2).to_broadcast([P, 2, 2])
                link(V.tensor_tensor(m, m, sink, ALU.max))
                link(V.tensor_scalar(nm, m, -1.0, None, ALU.mult))
                V.tensor_tensor(m, nm, sink, ALU.add).then_inc(sem("max2_ready"), 1)

            def window_out(w):
                link = ordered(dve, "vector")
                c4 = slice(4 * w, 4 * w + 4)
                dve.wait_ge(sem("exp2_ready"), w + 1)
                link(V.tensor_tensor(sum2[:, c4], sum2[:, c4], m2[:, c4], ALU.add))
                link(V.reciprocal(rinv2[:, c4], sum2[:, c4]))
                dve.wait_ge(sem("heads2_ready"), w + 1)
                V.tensor_tensor(merged[:, :, 128 * w:128 * w + 128].rearrange("p t (h d) -> p h t d", d=HEAD2),
                                psum[:, 3, 256:512].rearrange("p (h t d) -> p h t d", h=2, t=T),
                                pair_of(rinv2, w).unsqueeze(3).to_broadcast([P, 2, 2, HEAD2]), ALU.mult).then_inc(sem("attn2_out"), 1)

            def z_lo(half):
                dve.wait_ge(sem("z_hi_ready"), half + 1)
                c4 = slice(4 * half, 4 * half + 4)
                V.tensor_tensor(xlo[:, c4, :], z_t[:, c4, :], xhi[:, c4, :].bitcast(F32), ALU.subtract).then_inc(sem("z_lo_ready"), 1)

            def mixers():
                for n in range(11):
                    k, w = 5 + n, n
                    for part in range(3):
                        unit(k, part)
                    if k % 2:
                        skip((k - 3) // 2)
                    if w < 8:
                        window_max(w)
                    if 1 <= w <= 8:
                        window_out(w - 1)
                    if k == 10:
                        z_lo(0)
                skip(7)
                z_lo(1)

            residual("down1", 5, state_parameters())
            ada_gains()
            token_norm("norm_mix", 5, sh_m, gs_m)
            project_in()
            mixers()

            def glu_out(i, b):
                dve.wait_ge(sem(f"glu_out{b}"), 1)
                dve.wait_ge(tr_ready[b], GROUP_AT["glu"][b] + 1)
                V.tensor_tensor(merged[:, :, W2 + NW * b:W2 + NW * (b + 1)], tmp[:, b, :, :],
                                psum[:, 4 + 2 * b:6 + 2 * b, :], ALU.mult).then_inc(tr_free[b], 1)
                dve.wait_ge(tr_free[b], GROUP_AT["glu"][b] + 1)
                V.engine_nop().then_inc(sem("merged_ready"), 1)
            run("glu", None, None, lambda i, pos: pos == 5 and glu_out(0, 0))
            glu_out(0, 1)
            dve.wait_ge(sem("merge_squares"), 3)
            halves = mean[:, 0:4].rearrange("p (t h) -> p t h", h=2)
            V.tensor_copy(halves[:, :, 0], ss[:, :, 0])
            rstd_of("merge", V.tensor_tensor(halves[:, :, 1], ss[:, :, 1], ss[:, :, 2], ALU.add), 6, 4)
            dve.wait_ge(rstd_ready, 6)
            for n in range(4):
                m = merged[:, 1, n * NW:(n + 1) * NW]
                V.tensor_scalar(m, m, rstd[:, 2 + n // 2:3 + n // 2], None, ALU.mult).then_inc(sem("normed1"), 1)
            for q in range(4):
                group_lo(q % 2, xlo[:, 4 * q:4 * q + 4, :], xhi[:, 4 * q:4 * q + 4, :],
                         sm["g_merged"][:, 4 * q:4 * q + 4], sem("merge_hi"), q + 1)

            def gain_steps(i, pos, name, gain, diag, dst, at):
                if (i, pos) == (0, at):
                    if name == "down2":
                        dve.wait_ge(sem("ffn2_lo"), 11)
                    for c in range(FC):
                        ins = V.tensor_scalar(diag[:, c * P:(c + 1) * P], ident, gain[:, c:c + 1], None, ALU.mult)
                    ins.then_inc(sem(f"{name}_diagonal"), 1)
                if (i, pos) == (0, at + 2):
                    dve.wait_ge(sem(f"{name}_rows"), 1)
                    V.tensor_copy(dst, psum[:, 4:8, :].rearrange("p b e -> p (b e)")).then_inc(sem(f"{name}_gain"), 1)
                kt = KTILES[name]
                if (i, pos) in ((0, kt + 2), (1, 2), (1, kt + 2)):
                    times_gain(name, dst, (2 * i + pos // kt) - 1)

            def times_gain(name, gain, n):
                dve.wait_ge(sem(f"{name}_gain"), 1)
                dve.wait_ge(sem(f"{name}_out{n % 2}"), n // 2 + 1)
                part = GATHERED[name][:, :, n, :]
                V.tensor_tensor(part, part, gain[:, n * NW:(n + 1) * NW].unsqueeze(1).to_broadcast([P, T, NW]),
                                ALU.mult).then_inc(sem("gain_taken"), 1)
            run("w_out", None, None, lambda i, pos: gain_steps(i, pos, "w_out", gp_m, diag_mix, gain_mix, 5))

            def post_norm(layer, count, gain, signal):
                for b in range(2):
                    dve.wait_ge(sem(f"{layer}_out{b}"), 2)
                rstd_of(layer, V.reduce_sum(mean[:, 0:T], ss, AX), count)
                times_gain(layer, gain, 3)
                dve.wait_ge(rstd_ready, count)
                dve.wait_ge(sem("gain_taken"), {"w_out": 4, "down2": 8}[layer])
                rows = GATHERED[layer].rearrange("p t n e -> p t (n e)")
                for t in range(T):
                    for half in range(2):
                        a = half * D // 2
                        x_half = x_[:, t * D + a:t * D + a + D // 2]
                        V.scalar_tensor_tensor(x_half, rows[:, t, a:a + D // 2], rstd[:, t:t + 1], x_half,
                                               ALU.mult, ALU.add).then_inc(signal, 1)
            post_norm("w_out", 7, gain_mix, sem("x_mixed"))
            dve.wait_ge(sem("x_squares"), 1)
            rstd_of("norm_ffn", V.tensor_tensor(mean[:, 0:T], ss[:, :, 0], ss[:, :, 1], ALU.add), 8)
            token_norm("norm_ffn", 8, sh_f, gs_f)

            w = sm["conv2_w"].rearrange("p (k h n j) -> p k h n j", k=3, h=2, j=4)
            flat = conv_.rearrange("p (h e) -> p h e", h=2)

            def tap(i, b, n):
                k, by = ((1, 1), (0, 2))[n]
                dve.wait_ge((sem(f"ffn2_base{b}"), sem(f"ffn2_tap{b}"))[n], i + 1)
                for j in range(4):
                    dst = conv[:, 4 * b + j, by:S]
                    ins = V.scalar_tensor_tensor(dst, tr[b][:, j, 0:S - by], w[:, k, b, i, j:j + 1], dst, ALU.mult, ALU.add)
                ins.then_inc((sem(f"ffn2_tap{b}"), tr_free[b])[n], 1)

            def prod(i):
                dve.wait_ge(sem("ffn2_gelu"), i + 1)
                V.tensor_tensor(flat[:, 0, :], flat[:, 0, :], flat[:, 1, :], ALU.mult).then_inc(sem("ffn2_prod"), 1)

            def lo(i):
                dve.wait_ge(sem("ffn2_hi"), i + 1)
                V.tensor_tensor(mlo_.rearrange("p (n e) -> p n e", e=4 * S)[:, i, :], flat[:, 0, :],
                                mhi_.rearrange("p (n e) -> p n e", e=4 * S)[:, i, :].bitcast(F32),
                                ALU.subtract).then_inc(sem("ffn2_lo"), 1)
            run("ffn2", None, None, None, tuple((5 + 2 * b + n, lambda i, b=b, n=n: tap(i, b, n)) for b in range(2)
                                                for n in range(2)) + ((10, prod), (12, lo)))
            run("down2", None, None, lambda i, pos: gain_steps(i, pos, "down2", gp_f, diag_ff, gain_ff, 14))
            post_norm("down2", 9, gain_ff, sem("x_final"))

        @block.tensor
        def _(pe):
            M = nc.tensor.matmul
            slots = [0]

            def tile_products(layer, tile, b, k0, first, last, nk=KT, width=NW):
                hi, lo = LHS[layer]
                s = slots[0] % RING
                slots[0] += 1
                pe.wait_ge(lo_ready, tile + 1)
                for k in range(nk):
                    wh = whi[:, s, k * width:(k + 1) * width]
                    wl = wlo[:, s, k * width:(k + 1) * width]
                    for t in range(T):
                        xh, xl = (v[:, k0 + k, t * P:(t + 1) * P] for v in (hi, lo))
                        for n, (a, w) in enumerate(((xh, wh), (xh, wl), (xl, wh))):
                            ins = M(acc[b][:, t, 0:width], a, w, start=first and k == 0 and n == 0,
                                    stop=last and k == nk - 1 and n == 2)
                ins.then_inc(tiles_used, 1)

            def turn(b, before, src, signal=None):
                after(pe, tr_free[b], before)
                for j in range(4):
                    for t in range(T):
                        ins = nc.tensor.transpose(tr[b][:, j, t * P:(t + 1) * P], src(t, j), ident)
                ins.then_inc(tr_ready[b], 1)

            def ada_sum(i, at):
                pe.wait_ge(ada_step, i * 16 + (16 * at + 16))
                after(pe, ada_done, i + at)
                for j in range(4):
                    ins = M(psum[:, 6, j:j + 1], adacc_[:, j * P:(j + 1) * P], ones[:, 0:1], start=True, stop=True)
                ins.then_inc(ada_summed, 1)

            carried = []

            def carried_steps(pos):
                for at, step in [c for c in carried if c[0] == pos]:
                    step()
                    carried.remove((at, step))

            def carry(layer, tail, late):
                n = PAIRS[layer] - 1
                if tail and layer in CARRIED_AT:
                    carried.append((CARRIED_AT[layer], lambda: tail(n, 1)))
                elif tail:
                    tail(n, 1)
                for at, step in late:
                    carried.append((at, lambda step=step: step(n)))

            def run(layer, tail=None, extra=None, needs=None, late=()):
                kt = KTILES[layer]
                ada = ADA_AT.get(layer)

                def body(i, first):
                    slots[0] = TILE0[layer]
                    for pos in range(2 * kt):
                        b, k = pos // kt, pos % kt
                        if extra:
                            extra(i, pos)
                        for at, step in late:
                            if at == pos and not first:
                                step(i - 1)
                        if first:
                            carried_steps(pos)
                            if needs and pos in needs:
                                needs[pos]()
                        if pos == HOOK and not first:
                            if tail:
                                tail(i - 1, 1)
                            if ada is not None:
                                ada_sum(i - 1, ada)
                        if tail and pos == kt + HOOK:
                            tail(i, 0)
                        if k == 0:
                            after(pe, sem(released(layer, b)), i + 2 * RES_AT.get(layer, 0))
                        tile_products(layer, i * (2 * kt) + (TILE0[layer] + pos), b, KT * k, k == 0, k == kt - 1)
                each_pair(pe, layer, body)
                carry(layer, tail, late)
                if ada is not None:
                    ada_sum(PAIRS[layer] - 1, ada)
                    pe.wait_ge(ada_done, ada + PAIRS[layer])

            def residual(layer, extra=None, needs=None):
                def tail(i, b):
                    pe.wait_ge(sem(f"sum_ready{b}"), i + (2 * RES_AT[layer] + 1))
                    turn(0, GROUP_AT[layer][0] + 2 * i + b, lambda t, j: tmp[:, b, t, j * P:(j + 1) * P])
                run(layer, tail if RESIDUAL[layer] else None, extra, needs)

            def gated(layer, needs):
                def tail(i, b):
                    if b:
                        pe.wait_ge(sem(f"{layer}_prod"), i + 1)
                        turn(0, i + GROUP_AT[layer][0], lambda t, j: tmp[:, 1, t, j * P:(j + 1) * P])
                run(layer, tail, None, needs)

            def groups_in(name, layer):
                n = GROUP_AT[name][0] + dict((g[0], g[1]) for g in GROUPS)[name]
                return {0: lambda: pe.wait_ge(tr_free[0], n - 1),
                        KTILES[layer] - 2: lambda: pe.wait_ge(tr_free[0], n)}

            def quarters(name, source, ready):
                def turned(q):
                    for t in range(T):
                        pe.wait_ge(*ready(t, q))
                    turn(q % 2, GROUP_AT[name][q % 2] + q // 2, lambda t, j: source[:, t, (4 * q + j) * P:(4 * q + j + 1) * P])

                def split_off(q):
                    pe.wait_ge(tr_free[q % 2], GROUP_AT[name][q % 2] + q // 2 + 1)

                turned(0)
                turned(1)
                return {0: lambda: split_off(0), 1: lambda: turned(2), 2: lambda: (split_off(1), turned(3)),
                        4: lambda: split_off(2), 6: lambda: split_off(3)}

            pe.wait_ge(small_arrived, 16)
            pe.wait_ge(ones_ready, 1)
            first_needs = quarters("first", x_.rearrange("p (t e) -> p t e", t=T), lambda t, q: (x_arrived[q // 2], 16))

            def heads(i, pos):
                for c in range(K_CHUNK + 1):
                    if 16 * i + pos - 8 * c == HEADS_AT["turn"] + (c == K_CHUNK):
                        pe.wait_ge(s_rot, c + 1)
                        after(pe, s_qe, c)
                        if c == 0:
                            pe.wait_ge(tr_free[0], GROUP_AT["first"][0] + 2)
                        for j in range(4):
                            for t in range(T):
                                ins = nc.tensor.transpose(tr[0][:, j, t * P:(t + 1) * P], rot[:, t, 4 * c + j, :], ident)
                        ins.then_inc(s_qt, 1)
            run("qkv", None, heads, first_needs)
            pe.wait_ge(s_qe, K_CHUNK + 1)
            for b in range(2):
                pe.wait_ge(sem(f"qkv_out{b}"), 3)

            def scores(u):
                after(pe, s_exp, u - 1)
                for h in range(2):
                    for t in range(T):
                        ins = M(psum[:, 2 * (u % 2) + h, t * S:(t + 1) * S], qk_t[:, 2 * u + h, t * P:(t + 1) * P],
                                qk_t[:, QH + u // 2, :], start=True, stop=True)
                ins.then_inc(s_sc, 1)
            scores(0)
            scores(1)
            for u in range(8):
                pe.wait_ge(s_pn, u + 1)
                after(pe, s_pte, u)
                for h in range(2):
                    for k in range(T):
                        for t in range(T):
                            ins = nc.tensor.transpose(tr[0][:, 2 * h + k, t * P:(t + 1) * P],
                                                      probs[:, u % 2, 2 * h + t, k * P:(k + 1) * P], ident)
                ins.then_inc(s_pt, 1)
                if u < 6:
                    scores(u + 2)
                pe.wait_ge(s_pte, u + 1)
                after(pe, s_ol, u - 1)
                for h in range(2):
                    for k in range(T):
                        ins = M(psum[:, 6 + u % 2, h * S:(h + 1) * S], qkv_h[:, k, QH + KVH + u // 2, :],
                                probs_t[:, u % 2, h, k, :], start=k == 0, stop=k == T - 1)
                ins.then_inc(s_pv, 1)
            residual("w_o", None, {k: lambda k=k: pe.wait_ge(s_ol, k + 1) for k in range(8)})
            gated("ffn0", groups_in("w_o", "ffn0"))
            residual("down0", None, groups_in("ffn0", "down0"))

            def recurrent_in():
                def tail(i, b):
                    c = 2 * i + b
                    pe.wait_ge(sem(f"rnn_in_out{b}"), i + 1)
                    turn(0, GROUP_AT["rnn_in"][0] + c, lambda t, j: tmp[:, b, t, j * P:(j + 1) * P])

                def unit(i, pos):
                    if i < 2 or pos % 2:
                        return
                    u = 8 * (i - 2) + pos // 2
                    blk, half = u // 2, u % 2
                    pe.wait_ge(gate_arrived[blk % 2], 16 * (blk // 2 + 1))
                    pe.wait_ge(s_conv, 3 * ((2 * blk + 1) // 4 + 1))
                    if u:
                        pe.wait_ge(s_drive, u)
                        pe.wait_ge(s_tanh, 2 * u)
                    for d in range(2):
                        for g in range(2):
                            for k in range(2):
                                ins = M(gates[:, d, g, :], gate_ws[blk % 2][:, k, d, g, half * P:(half + 1) * P],
                                        xc[:, 2 * blk + k, :], start=k == 0, stop=k == 1)
                    ins.then_inc(s_gate, 1)
                run("rnn_in", tail, unit, groups_in("down0", "rnn_in"))
            recurrent_in()
            residual("rnn_out", None, {2 * k: lambda k=k: pe.wait_ge(s_hlo, k + 1) for k in range(4)})
            gated("ffn1", groups_in("rnn_out", "ffn1"))

            def token_norm(name):
                before = {"norm_mix": 0, "norm_ffn": 8}[name]
                return quarters(name, normed, lambda t, q: (sem(f"normed{t}"), before + q + 1))

            def turned_matrices(i, pos):
                if i == 0 and pos in (15, 18):
                    b = (pos - 15) // 3
                    pe.wait_ge(sem("parameter_steps"), PARAMETER_STEPS["input_matrix"])
                    after(pe, tr_free[0], GROUP_AT["ssm_b"][0] + b)
                    for j in range(8):
                        ins = nc.tensor.transpose(tr[0].rearrange("p c s -> p (c s)")[:, j * P:(j + 1) * P],
                                                  bd[b].rearrange("p c e -> p (c e)")[:, j * P:(j + 1) * P], ident)
                    ins.then_inc(tr_ready[0], 1)

            def inputs(k):
                pe.wait_ge(tr_free[0], GROUP_AT["w_in"][0] + (k // 4 + 1))
                if k == 0:
                    pe.wait_ge(sem("matrices_back"), 32)
                after(pe, sem("inputs_taken"), k)
                for b in range(2):
                    for jj in range(2):
                        j = 2 * (k % 2) + jj
                        r = slice(32 * j, 32 * j + 32)
                        ins = M(psum[:, 6 + jj, b * S:(b + 1) * S], bb_t[b][r, k // 2, :], u_t[r, k // 2, :], start=True, stop=True)
                ins.then_inc(sem("inputs_ready"), 1)

            def outputs(k):
                pe.wait_ge(*((sem("parts_ready"), k + 1) if k < UNITS2 - 1 else (sem("scanned"), UNITS2 + 1)))
                if k % 2 == 0:
                    after(pe, sem("skip_added"), {1: 1, 2: 0}.get(k // 2, k // 2 - 1))
                bufs = unit_bufs[k % 2]
                for jj in range(2):
                    j = 2 * (k % 2) + jj
                    for n, (c_, part) in enumerate(((c_re, bufs[2]), (nc_im, bufs[4]))):
                        ins = M(psum[32 * j:32 * j + 32, Y_BANK[k // 2], 0:S], c_[:, 2 * k + jj, :], part[:, jj, :],
                                start=n == 0, stop=n == 1)
                ins.then_inc(sem("state_out"), 1)

            def project_in(needs):
                def turn_two(c, half):
                    n = 2 * c + half
                    pe.wait_ge(sem(f"w_in_out{c % 2}"), c // 2 + 1)
                    pe.wait_ge(tr_free[0], GROUP_AT["w_in"][0] + n)
                    for j in range(2):
                        for t in range(T):
                            ins = nc.tensor.transpose(psum[:, 5, j * S + t * P:j * S + (t + 1) * P],
                                                      tmp[:, c % 2, t, (2 * half + j) * P:(2 * half + j + 1) * P], ident)
                    ins.then_inc(tr_ready[0], 1)

                def extra(i, pos):
                    for half in range(2):
                        for b in range(2):
                            if pos == TURN_AT[half] + 8 * (1 - b) and (b == 0 or i):
                                turn_two(2 * i if not b else 2 * i - 1, half)
                    if (i, pos) in STREAM_UNITS:
                        k = STREAM_UNITS[(i, pos)]
                        if k > 1:
                            outputs(k - 2)
                        inputs(k)
                run("w_in", None, extra, needs)
                pe.wait_ge(sem("w_in_out0"), 2)
                for n in range(4):
                    if n >= 2:
                        turn_two(3, n - 2)
                    slots[0] = n
                    tile_products("w_in_kv", TILE0["w_in_kv"] + n, 0, 4 * n, n == 0, n == 3, nk=4, width=256)
                pe.wait_ge(sem("w_in_kv_out"), 1)
                pe.wait_ge(tr_free[0], GROUP_AT["w_in_k"][0])
                for t in range(T):
                    ins = nc.tensor.transpose(psum[:, 5, t * P:(t + 1) * P], kv[:, t, 0:P], ident)
                ins.then_inc(tr_ready[0], 1)
                outputs(3)
                inputs(5)
                pe.wait_ge(tr_free[0], GROUP_AT["w_in_k"][0] + 1)

            def window_scores(w):
                after(pe, sem("scores2_taken"), w)
                for h in range(2):
                    rows = slice(HEAD2 * h, HEAD2 * h + HEAD2)
                    for t in range(T):
                        k = S if t else P
                        ins = M(psum[:, h, t * P:t * P + k], q2_t[rows, w, t * P:(t + 1) * P], k2_t[rows, 0:k],
                                start=True, stop=True)
                ins.then_inc(sem("scores2_ready"), 1)

            def window_heads(w):
                pe.wait_ge(sem("exp2_ready"), w + 1)
                after(pe, sem("attn2_out"), w)
                flat = psum[:, 2:4, :].rearrange("p b (n q) -> p (b n) q", q=P)
                for h in range(2):
                    for n in range(3):
                        ins = nc.tensor.transpose(flat[:, 3 * h + n, :], masked[w % 2][:, h, n * P:(n + 1) * P], ident)
                ins.then_inc(sem("probs2_turned"), 1)
                pe.wait_ge(sem("turned2_ready"), w + 1)
                for h in range(2):
                    o = lambda t: psum[:, 3, 256 + (2 * h + t) * HEAD2:256 + (2 * h + t + 1) * HEAD2]
                    v = lambda t: kv[:, t, P + HEAD2 * h:P + HEAD2 * (h + 1)]
                    M(o(0), turned[w % 2][:, h, 0, :], v(0), start=True, stop=True)
                    M(o(1), turned[w % 2][:, h, 1, :], v(0), start=True, stop=False)
                    ins = M(o(1), turned[w % 2][:, h, 2, :], v(1), start=False, stop=True)
                ins.then_inc(sem("heads2_ready"), 1)

            def mixers():
                for n in range(11):
                    k, w = 5 + n, n
                    if n:
                        outputs(k - 2)
                        inputs(k)
                    if w < 8:
                        window_scores(w)
                    if 1 <= w <= 8:
                        window_heads(w - 1)
                outputs(14)
                outputs(15)
                pe.wait_ge(sem("z_lo_ready"), 2)
                pe.wait_ge(sem("skip_added"), 8)

            def gain_rows(name, diag):
                pe.wait_ge(sem(f"{name}_diagonal"), 1)
                for c in range(FC):
                    ins = M(psum[:, 4 + c // 4, (c % 4) * P:(c % 4 + 1) * P], ones, diag[:, c * P:(c + 1) * P], start=True, stop=True)
                ins.then_inc(sem(f"{name}_rows"), 1)

            residual("down1", turned_matrices, groups_in("ffn1", "down1"))
            project_in(token_norm("norm_mix"))
            mixers()

            def turn_z(i, pos):
                if pos == 1:
                    for b in range(2):
                        after(pe, tr_free[b], GROUP_AT["glu"][b])
                        for j in range(4):
                            for t in range(T):
                                ins = nc.tensor.transpose(psum[:, 4 + 2 * b + t, j * P:(j + 1) * P], z_t[:, 4 * b + j, t * P:(t + 1) * P], ident)
                        ins.then_inc(tr_ready[b], 1)
            run("glu", None, turn_z)
            needs = quarters("merge", merged, lambda t, q: (sem(f"normed{t}"), 4 + q + 1))
            run("w_out", None, lambda i, pos: (i, pos) == (0, 7) and gain_rows("w_out", diag_mix), needs)
            pe.wait_ge(sem("w_out_gain"), 1)
            needs = token_norm("norm_ffn")

            def up_turned(i, v):
                pe.wait_ge(sem(f"ffn2_copied{v}"), i + 1)
                turn(v, i + GROUP_AT["ffn2"][v], lambda t, j: tmp[:, v, t, j * P:(j + 1) * P])
            run("ffn2", needs=needs, late=((3, lambda i: up_turned(i, 0)), (4, lambda i: up_turned(i, 1))))

            def rows_of_down2(i, pos):
                if (i, pos) == (0, 16):
                    gain_rows("down2", diag_ff)
            run("down2", None, rows_of_down2, {0: lambda: pe.wait_ge(sem("ffn2_lo"), 10),
                                               20: lambda: pe.wait_ge(sem("ffn2_lo"), 11)})
def _tiles(w):
    k, n = w.shape
    return w.reshape(k // (KT * P), KT, P, n // NW, NW).transpose(3, 0, 2, 1, 4).reshape(n // NW, k // (KT * P), P, TW)

def _cols(v):
    return v.reshape(-1, P).T

def _head_order(n, per):
    return np.arange(n * per).reshape(2, n // 2, per).transpose(1, 0, 2).reshape(-1)

def pack(**a):
    a = {k: np.asarray(v) for k, v in a.items()}
    flat = lambda w: w.reshape(-1, P, TW)
    both = lambda g, u: np.stack([_tiles(g), _tiles(u)], axis=1)
    order2 = _head_order(QH2, HEAD2)
    w_in = a["w_in_2"][0]
    w_in_uq = np.concatenate([w_in[:, W2 + 256:], w_in[:, :W2][:, order2]], axis=1)
    w_in_kv = w_in[:, W2:W2 + 256].reshape(4, 4, P, 256).transpose(0, 2, 1, 3)
    w_up = a["w_up_2"][0]
    stream = [_tiles(a["attn_w_qkv"][0]), _tiles(a["attn_w_o"][0]),
              both(a["ffn_w_gate"][0], a["ffn_w_up"][0]), _tiles(a["ffn_w_down"][0]),
              _tiles(a["rnn_w_in"][0]), _tiles(a["rnn_w_out"][0]),
              both(a["ffn_w_gate"][1], a["ffn_w_up"][1]), _tiles(a["ffn_w_down"][1]),
              _tiles(w_in_uq), w_in_kv, _tiles(a["w_glu_2"][0]),
              _tiles(np.concatenate([a["w_out_2"][0][:W2][order2], a["w_out_2"][0][W2:]])),
              both(w_up[:, :D_FF], w_up[:, D_FF:]), _tiles(a["w_down_2"][0])]
    weights = np.concatenate([flat(w) for w in stream])
    gates = np.stack([a["rnn_w_a"][0], a["rnn_w_i"][0]], axis=1)
    gates = gates.reshape(2, 2, RNN_BLOCKS, 2, P, RNN_W).transpose(2, 4, 3, 0, 1, 5).reshape(RNN_BLOCKS, P, 2048)
    by_state = lambda v: v.reshape(ST, P).T
    small = {"g_mix0": _cols(a["norm_mix"][0]), "g_mix1": _cols(a["norm_mix"][1]),
             "g_ffn0": _cols(a["norm_ffn"][0]), "g_ffn1": _cols(a["norm_ffn"][1]),
             "conv_w": _cols(a["rnn_conv_w"][0]), "conv_b": _cols(a["rnn_conv_b"][0]),
             "b_a": _cols(a["rnn_b_a"][0]), "b_i": _cols(a["rnn_b_i"][0]), "lam": _cols(a["rnn_lambda"][0]),
             "c": _cols(a["c_2"]), "b_ada": _cols(a["b_ada_2"][0]), "g_pre_mix": _cols(a["g_pre_mix_2"][0]),
             "g_post_mix": _cols(a["g_post_mix_2"][0]), "g_pre_ffn": _cols(a["g_pre_ffn_2"][0]),
             "g_post_ffn": _cols(a["g_post_ffn_2"][0]),
             "g_merged": _cols(np.concatenate([a["g_attn_out_2"][0][order2], a["g_ssm_out_2"][0]])),
             "d_skip": _cols(a["ssm_d_2"][0].reshape(-1)), "conv2_w": _cols(a["conv_w_2"][0]),
             "conv2_b": _cols(a["conv_b_2"][0]), "lam_re": by_state(a["lam_re_2"][0]),
             "lam_im": by_state(a["lam_im_2"][0]), "log_step": by_state(np.repeat(a["log_step_2"][0], STATE)),
             "sinks": np.broadcast_to(a["attn_sinks_2"][0][_head_order(QH2, 1)], (P, QH2)),
             "ident": np.eye(P, dtype=np.float32)}
    small = np.concatenate([small[k] for k, _ in SMALL], axis=1)
    pos = np.arange(S)
    freqs = np.float32(10000.0) ** (-np.arange(FREQS, dtype=np.float32) / np.float32(FREQS))
    ang = np.stack([(pos // 64).astype(np.float32)[:, None] * freqs, (pos % 64).astype(np.float32)[:, None] * freqs], axis=1)
    table = lambda f: f(ang).astype(np.float32).reshape(T, P, 64).transpose(1, 0, 2).reshape(P, 128)
    rope = np.concatenate([table(np.cos), table(np.sin), np.broadcast_to(a["attn_q_gain"][0], (P, HEAD)),
                           np.broadcast_to(a["attn_k_gain"][0], (P, HEAD))], axis=1)
    b = lambda v: v[0].reshape(ST, P, GROUP).transpose(1, 0, 2).reshape(P, -1)
    c = lambda v: v[0].transpose(0, 2, 1).reshape(ST, P, GROUP).transpose(1, 0, 2).reshape(P, -1)
    ssm = np.concatenate([b(a["ssm_b_re_2"]), b(a["ssm_b_im_2"]), c(a["ssm_c_re_2"]), c(a["ssm_c_im_2"])], axis=1)
    q, k = np.arange(P)[:, None], np.arange(S)[None, :]
    own = np.where(q >= k[:, :P], 0.0, NEG)
    band = np.where((k > q) & (k <= q + WINDOW), 0.0, NEG)
    mask = np.concatenate([own, band], axis=1).astype(np.float32)
    return {"x": a["x"][0], "weights": weights, "ada_w": flat(_tiles(a["w_ada_2"][0])), "gate_w": gates,
            "small": small, "rope": rope, "ssm": ssm, "mask": mask}


_INS = ("x", "weights", "ada_w", "gate_w", "small", "rope", "ssm", "mask")


def kernel(**inputs):
    import concourse.bacc as bacc
    from concourse.bass_utils import run_bass_kernel_spmd

    arrays = {k: np.ascontiguousarray(v) for k, v in pack(**inputs).items()}
    nc = bacc.Bacc("TRN2", target_bir_lowering=False, num_devices=1)
    args = [nc.dram_tensor(k, arrays[k].shape, mybir.dt.from_np(arrays[k].dtype), kind="ExternalInput").ap() for k in _INS]
    out = nc.dram_tensor("out_0", (S, D), F32, kind="ExternalOutput").ap()
    build(nc, *args, out)
    r = run_bass_kernel_spmd(nc, [arrays], core_ids=[0])
    return r.results[0]["out_0"].reshape(1, S, D)
```
